# Optimizing a Trainium2 kernel written in Bass

```python
import math
import jax, jax.numpy as jnp
from jax import lax
import numpy as np
import jax
import jax.numpy as jnp

D_MODEL = 1024
BATCH = 1
SEQ = 1024
DEPTH = 1

D_MIX = D_MODEL
HEAD_DIM = 64
N_Q_HEADS = 8
N_KV_HEADS = 2
Q_PER_KV = N_Q_HEADS // N_KV_HEADS
D_ATTN = N_Q_HEADS * HEAD_DIM
D_CONV = D_MIX - D_ATTN
CONV_WIDTH = 31
WINDOW = 128
BLOCK = 128
N_BUCKETS = 32
MAX_EXACT = N_BUCKETS // 2
MAX_DISTANCE = 128
D_FF = int(math.ceil(8 * D_MODEL / 3 / 256) * 256)
EPS = 1e-6
D_Q = N_Q_HEADS * HEAD_DIM
D_KV = N_KV_HEADS * HEAD_DIM
D_IN = D_Q + 2 * D_KV + 2 * D_CONV


def rms_norm(x, g):
    xf = x.astype(jnp.float32)
    y = xf * lax.rsqrt(jnp.mean(xf * xf, axis=-1, keepdims=True) + EPS)
    return (y * g.astype(jnp.float32)).astype(x.dtype)

def layer_norm(x, g, b):
    xf = x.astype(jnp.float32)
    mu = jnp.mean(xf, axis=-1, keepdims=True)
    var = jnp.mean(jnp.square(xf - mu), axis=-1, keepdims=True)
    y = (xf - mu) * lax.rsqrt(var + EPS)
    return (y * g.astype(jnp.float32) + b.astype(jnp.float32)).astype(x.dtype)

def t5_causal_bucket(dist):
    is_small = dist < MAX_EXACT
    d = jnp.maximum(dist, 1).astype(jnp.float32)
    large = MAX_EXACT + (jnp.log(d / MAX_EXACT) / math.log(MAX_DISTANCE / MAX_EXACT)
                         * (N_BUCKETS - MAX_EXACT)).astype(jnp.int32)
    large = jnp.minimum(large, N_BUCKETS - 1)
    return jnp.where(is_small, dist, large)

def conformer_conv(u, conv_dw, conv_dw_b, conv_ln_g, conv_ln_b, w_conv_pw):
    a, gate = jnp.split(u, 2, axis=-1)
    h = a * jax.nn.sigmoid(gate)
    h = lax.conv_general_dilated(
        h, conv_dw[:, None, :].astype(h.dtype), window_strides=(1,),
        padding=[(CONV_WIDTH - 1, 0)],
        dimension_numbers=("NWC", "WIO", "NWC"),
        feature_group_count=D_CONV) + conv_dw_b
    h = jax.nn.silu(layer_norm(h, conv_ln_g, conv_ln_b))
    return h @ w_conv_pw

def sliding_window_attention(q, k, v, attn_sinks, rel_bias):
    B, S = q.shape[0], q.shape[1]
    nb = S // BLOCK
    qb = q.reshape(B, nb, BLOCK, N_KV_HEADS, Q_PER_KV, HEAD_DIM)
    pad = ((0, 0), (BLOCK, 0), (0, 0), (0, 0))
    kp, vp = jnp.pad(k, pad), jnp.pad(v, pad)

    def band(t):
        prev = t[:, :S].reshape(B, nb, BLOCK, N_KV_HEADS, HEAD_DIM)
        cur = t[:, BLOCK:].reshape(B, nb, BLOCK, N_KV_HEADS, HEAD_DIM)
        return jnp.concatenate([prev, cur], axis=2)

    kb, vb = band(kp), band(vp)
    scale = 1.0 / math.sqrt(HEAD_DIM)
    s = jnp.einsum("bnqhgd,bnkhd->bnhgqk", qb, kb).astype(jnp.float32) * scale

    qi = jnp.arange(BLOCK)[:, None]
    kj = jnp.arange(2 * BLOCK)[None, :]
    dist = qi + BLOCK - kj
    in_band = (dist >= 0) & (dist < WINDOW)
    bucket = t5_causal_bucket(jnp.maximum(dist, 0))
    bias = rel_bias.astype(jnp.float32)[bucket]
    bias = jnp.transpose(bias, (2, 0, 1)).reshape(N_KV_HEADS, Q_PER_KV, BLOCK, 2 * BLOCK)
    blk = jnp.arange(nb)[:, None, None]
    valid = in_band[None] & ((blk > 0) | (kj[None] >= BLOCK))
    s = jnp.where(valid[None, :, None, None], s + bias, -jnp.inf)

    sink = attn_sinks.astype(jnp.float32).reshape(N_KV_HEADS, Q_PER_KV, 1, 1)
    m = jnp.maximum(jnp.max(s, axis=-1, keepdims=True), sink)
    p = jnp.exp(s - m)
    denom = jnp.sum(p, axis=-1, keepdims=True) + jnp.exp(sink - m)
    p = (p / denom).astype(v.dtype)
    o = jnp.einsum("bnhgqk,bnkhd->bnqhgd", p, vb)
    return o.reshape(B, S, N_Q_HEADS * HEAD_DIM)

def first_inputs(seed: int = 0) -> dict:
    key = jax.random.key(seed)
    ks = jax.random.split(key, 20)
    f = jnp.float32
    nrm = lambda k, shp, sc: jax.random.normal(k, shp, f) * sc
    gain = lambda k, n: 1.0 + 0.05 * jax.random.normal(k, (n,), f)
    return {
        "x": jax.random.normal(ks[0], (BATCH, SEQ, D_MODEL), f),
        "mix_pre_g": gain(ks[1], D_MODEL),
        "mix_post_g": gain(ks[2], D_MODEL),
        "ffn_pre_g": gain(ks[3], D_MODEL),
        "ffn_post_g": gain(ks[4], D_MODEL),
        "w_in": nrm(ks[5], (D_MODEL, D_IN), D_MODEL ** -0.5),
        "conv_dw": nrm(ks[6], (CONV_WIDTH, D_CONV), CONV_WIDTH ** -0.5),
        "conv_dw_b": nrm(ks[7], (D_CONV,), 0.02),
        "conv_ln_g": gain(ks[8], D_CONV),
        "conv_ln_b": nrm(ks[9], (D_CONV,), 0.02),
        "w_conv_pw": nrm(ks[10], (D_CONV, D_CONV), D_CONV ** -0.5),
        "attn_sinks": nrm(ks[11], (N_Q_HEADS,), 0.5),
        "rel_bias": nrm(ks[12], (N_BUCKETS, N_Q_HEADS), 0.5),
        "w_out": nrm(ks[13], (D_MIX, D_MODEL), D_MIX ** -0.5),
        "w_gate": nrm(ks[14], (D_MODEL, D_FF), D_MODEL ** -0.5),
        "w_up": nrm(ks[15], (D_MODEL, D_FF), D_MODEL ** -0.5),
        "w_down": nrm(ks[16], (D_FF, D_MODEL), D_FF ** -0.5),
    }

def first_block(x, mix_pre_g, mix_post_g, ffn_pre_g, ffn_post_g, w_in, conv_dw, conv_dw_b,
              conv_ln_g, conv_ln_b, w_conv_pw, attn_sinks, rel_bias, w_out,
              w_gate, w_up, w_down):
    B, S, _ = x.shape
    h = x
    for _layer in range(DEPTH):
        hn = rms_norm(h, mix_pre_g)
        proj = hn @ w_in
        q = proj[..., :D_Q].reshape(B, S, N_Q_HEADS, HEAD_DIM)
        k = proj[..., D_Q:D_Q + D_KV].reshape(B, S, N_KV_HEADS, HEAD_DIM)
        v = proj[..., D_Q + D_KV:D_Q + 2 * D_KV].reshape(B, S, N_KV_HEADS, HEAD_DIM)
        u = proj[..., D_Q + 2 * D_KV:]
        attn_out = sliding_window_attention(q, k, v, attn_sinks, rel_bias)
        conv_out = conformer_conv(u, conv_dw, conv_dw_b, conv_ln_g, conv_ln_b, w_conv_pw)
        mixed = jnp.concatenate([attn_out, conv_out], axis=-1) @ w_out
        h = h + rms_norm(mixed, mix_post_g)
        hn = rms_norm(h, ffn_pre_g)
        ff = (jax.nn.silu(hn @ w_gate) * (hn @ w_up)) @ w_down
        h = h + rms_norm(ff, ffn_post_g)
    return h


CHUNK = 64
Q_BLOCK = 128
MEM_LEN = 256

MLA_HEADS = 4
MLA_Q_RANK = 256
MLA_KV_RANK = 128
MLA_NOPE = 64
MLA_ROPE = 32
MLA_V = 128
ROPE_THETA = 10000.0
FOX_HEADS = 4
FOX_DIM = 64
CHK_HEADS = 4
CHK_DIM = 64
CHK_LEFT = 8
BAND = (CHK_LEFT + 1) * CHUNK
REL_MAX = 128
REL_SIZE = (CHUNK - 1) + REL_MAX + 1

A_WIDTH = MLA_HEADS * MLA_V
B_WIDTH = FOX_HEADS * FOX_DIM
C_WIDTH = CHK_HEADS * CHK_DIM
MIX_WIDTH = A_WIDTH + B_WIDTH + C_WIDTH

IN_SIZES = (MLA_Q_RANK, MLA_KV_RANK, MLA_ROPE,
            B_WIDTH, B_WIDTH, B_WIDTH, FOX_HEADS,
            C_WIDTH, C_WIDTH, C_WIDTH)
IN_WIDTH = sum(IN_SIZES)
IN_SPLIT_POINTS = tuple(int(v) for v in np.cumsum(IN_SIZES)[:-1])

CROSS_HEADS = 4
CROSS_DIM = 128
CROSS_WIDTH = CROSS_HEADS * CROSS_DIM

FFN_HIDDEN = ((-(-(8 * D_MODEL) // 3) + 255) // 256) * 256


def _rmsnorm(x, g):
    xf = x.astype(jnp.float32)
    y = xf * lax.rsqrt(jnp.mean(xf * xf, axis=-1, keepdims=True) + EPS)
    return (y * g.astype(jnp.float32)).astype(x.dtype)

def _rope_tables(seq):
    pos = jnp.arange(seq, dtype=jnp.float32)
    inv = ROPE_THETA ** (-jnp.arange(0, MLA_ROPE, 2, dtype=jnp.float32) / MLA_ROPE)
    ang = pos[:, None] * inv[None, :]
    return jnp.cos(ang), jnp.sin(ang)

def _rope(x, cos, sin):
    xf = x.astype(jnp.float32)
    x1, x2 = jnp.split(xf, 2, axis=-1)
    return jnp.concatenate([x1 * cos - x2 * sin, x1 * sin + x2 * cos], axis=-1).astype(x.dtype)

def _split_blocks(a, block):
    b, s = a.shape[:2]
    return jnp.moveaxis(a.reshape((b, s // block, block) + a.shape[2:]), 1, 0)

def _merge_blocks(a):
    nb, b, blk = a.shape[:3]
    return jnp.moveaxis(a, 0, 1).reshape(b, nb * blk, -1)

def _mla(c_q, c_kv, k_rope, q_norm, w_uq, kv_norm, w_ukv, cos, sin):
    b, s, _ = c_q.shape
    q = (_rmsnorm(c_q, q_norm) @ w_uq).reshape(b, s, MLA_HEADS, MLA_NOPE + MLA_ROPE)
    q_nope, q_pe = jnp.split(q, [MLA_NOPE], axis=-1)
    q = jnp.concatenate([q_nope, _rope(q_pe, cos[:, None], sin[:, None])], axis=-1)
    kv = (_rmsnorm(c_kv, kv_norm) @ w_ukv).reshape(b, s, MLA_HEADS, MLA_NOPE + MLA_V)
    k_nope, v = jnp.split(kv, [MLA_NOPE], axis=-1)
    k_pe = _rope(k_rope, cos, sin)
    k = jnp.concatenate(
        [k_nope, jnp.broadcast_to(k_pe[:, :, None, :], (b, s, MLA_HEADS, MLA_ROPE))], axis=-1)
    scale = (MLA_NOPE + MLA_ROPE) ** -0.5
    k_chunk = jnp.arange(s) // CHUNK

    def attend(args):
        qb, idx = args
        q_chunk = (idx * Q_BLOCK + jnp.arange(Q_BLOCK)) // CHUNK
        sc = jnp.einsum('bqhd,bkhd->bhqk', qb, k, preferred_element_type=jnp.float32) * scale
        sc = jnp.where(k_chunk[None, :] <= q_chunk[:, None], sc, -jnp.inf)
        p = jax.nn.softmax(sc, axis=-1).astype(v.dtype)
        return jnp.einsum('bhqk,bkhd->bqhd', p, v)

    out = lax.map(attend, (_split_blocks(q, Q_BLOCK), jnp.arange(s // Q_BLOCK)))
    return _merge_blocks(out)

def _fox(q, k, v, f_logit, f_bias):
    b, s, _ = q.shape
    q = q.reshape(b, s, FOX_HEADS, FOX_DIM)
    k = k.reshape(b, s, FOX_HEADS, FOX_DIM)
    v = v.reshape(b, s, FOX_HEADS, FOX_DIM)
    log_f = jax.nn.log_sigmoid(f_logit.astype(jnp.float32) + f_bias.astype(jnp.float32))
    cum = jnp.cumsum(log_f, axis=1)
    cum_k = jnp.transpose(cum, (0, 2, 1))
    scale = FOX_DIM ** -0.5
    k_pos = jnp.arange(s)

    def attend(args):
        qb, cq, idx = args
        q_pos = idx * Q_BLOCK + jnp.arange(Q_BLOCK)
        sc = jnp.einsum('bqhd,bkhd->bhqk', qb, k, preferred_element_type=jnp.float32) * scale
        sc = sc + jnp.transpose(cq, (0, 2, 1))[..., None] - cum_k[:, :, None, :]
        sc = jnp.where(k_pos[None, :] <= q_pos[:, None], sc, -jnp.inf)
        p = jax.nn.softmax(sc, axis=-1).astype(v.dtype)
        return jnp.einsum('bhqk,bkhd->bqhd', p, v)

    out = lax.map(attend, (_split_blocks(q, Q_BLOCK), _split_blocks(cum, Q_BLOCK),
                           jnp.arange(s // Q_BLOCK)))
    return _merge_blocks(out)

def _chunk_rel(q, k, v, rel_table):
    b, s, _ = q.shape
    q = q.reshape(b, s, CHK_HEADS, CHK_DIM)
    k = k.reshape(b, s, CHK_HEADS, CHK_DIM)
    v = v.reshape(b, s, CHK_HEADS, CHK_DIM)
    pad = CHK_LEFT * CHUNK
    kp = jnp.pad(k, ((0, 0), (pad, 0), (0, 0), (0, 0)))
    vp = jnp.pad(v, ((0, 0), (pad, 0), (0, 0), (0, 0)))
    qi = jnp.arange(CHUNK)
    ki = jnp.arange(BAND)
    rel = qi[:, None] + pad - ki[None, :]
    rel_idx = jnp.clip(rel, -(CHUNK - 1), REL_MAX) + (CHUNK - 1)
    bias = rel_table[:, rel_idx].astype(jnp.float32)
    scale = CHK_DIM ** -0.5

    def attend(args):
        qc, idx = args
        start = idx * CHUNK
        kb = lax.dynamic_slice_in_dim(kp, start, BAND, axis=1)
        vb = lax.dynamic_slice_in_dim(vp, start, BAND, axis=1)
        valid = (start - pad + ki) >= 0
        sc = jnp.einsum('bqhd,bkhd->bhqk', qc, kb, preferred_element_type=jnp.float32) * scale
        sc = jnp.where(valid, sc + bias[None], -jnp.inf)
        p = jax.nn.softmax(sc, axis=-1).astype(vb.dtype)
        return jnp.einsum('bhqk,bkhd->bqhd', p, vb)

    out = lax.map(attend, (_split_blocks(q, CHUNK), jnp.arange(s // CHUNK)))
    return _merge_blocks(out)

def _cross(h, m, w_cq, w_ckv, w_co):
    b, s, _ = h.shape
    n = m.shape[1]
    q = (h @ w_cq).reshape(b, s, CROSS_HEADS, CROSS_DIM)
    k, v = jnp.split(m @ w_ckv, 2, axis=-1)
    k = k.reshape(b, n, CROSS_HEADS, CROSS_DIM)
    v = v.reshape(b, n, CROSS_HEADS, CROSS_DIM)
    sc = jnp.einsum('bshd,bmhd->bhsm', q, k, preferred_element_type=jnp.float32) * (CROSS_DIM ** -0.5)
    p = jax.nn.softmax(sc, axis=-1).astype(v.dtype)
    o = jnp.einsum('bhsm,bmhd->bshd', p, v).reshape(b, s, CROSS_WIDTH)
    return o @ w_co

def second_inputs(seed: int = 0) -> dict:
    key = jax.random.key(seed)
    ks = jax.random.split(key, 24)

    def nrm(k, shape, fan_in):
        return jax.random.normal(k, shape, jnp.float32) * (fan_in ** -0.5)

    def gain(k, shape):
        return 1.0 + 0.05 * jax.random.normal(k, shape, jnp.float32)

    L = DEPTH
    return {
        'x': jax.random.normal(ks[0], (BATCH, SEQ, D_MODEL), jnp.float32),
        'mem': jax.random.normal(ks[1], (BATCH, MEM_LEN, D_MODEL), jnp.float32),
        'norm_mix': gain(ks[2], (L, D_MODEL)),
        'w_in': nrm(ks[3], (L, D_MODEL, IN_WIDTH), D_MODEL),
        'q_norm': gain(ks[4], (L, MLA_Q_RANK)),
        'w_uq': nrm(ks[5], (L, MLA_Q_RANK, MLA_HEADS * (MLA_NOPE + MLA_ROPE)), MLA_Q_RANK),
        'kv_norm': gain(ks[6], (L, MLA_KV_RANK)),
        'w_ukv': nrm(ks[7], (L, MLA_KV_RANK, MLA_HEADS * (MLA_NOPE + MLA_V)), MLA_KV_RANK),
        'f_bias': jax.random.uniform(ks[8], (L, FOX_HEADS), jnp.float32, minval=1.0, maxval=4.0),
        'rel_bias': 0.3 * jax.random.normal(ks[9], (L, CHK_HEADS, REL_SIZE), jnp.float32),
        'out_norm': gain(ks[10], (L, MIX_WIDTH)),
        'w_o': nrm(ks[11], (L, MIX_WIDTH, D_MODEL), MIX_WIDTH),
        'norm_cross': gain(ks[12], (L, D_MODEL)),
        'norm_mem': gain(ks[13], (L, D_MODEL)),
        'w_cq': nrm(ks[14], (L, D_MODEL, CROSS_WIDTH), D_MODEL),
        'w_ckv': nrm(ks[15], (L, D_MODEL, 2 * CROSS_WIDTH), D_MODEL),
        'w_co': nrm(ks[16], (L, CROSS_WIDTH, D_MODEL), CROSS_WIDTH),
        'norm_ffn': gain(ks[17], (L, D_MODEL)),
        'w_gu': nrm(ks[18], (L, D_MODEL, 2 * FFN_HIDDEN), D_MODEL),
        'w_down': nrm(ks[19], (L, FFN_HIDDEN, D_MODEL), FFN_HIDDEN),
        'final_norm': gain(ks[20], (D_MODEL,)),
    }

def second_block(x, mem, norm_mix, w_in, q_norm, w_uq, kv_norm, w_ukv, f_bias, rel_bias,
              out_norm, w_o, norm_cross, norm_mem, w_cq, w_ckv, w_co, norm_ffn, w_gu,
              w_down, final_norm):
    s = x.shape[1]
    cos, sin = _rope_tables(s)
    for l in range(DEPTH):
        h = _rmsnorm(x, norm_mix[l])
        proj = h @ w_in[l]
        (c_q, c_kv, k_rope, fq, fk, fv, f_logit, cq, ck, cv) = jnp.split(
            proj, IN_SPLIT_POINTS, axis=-1)
        ya = _mla(c_q, c_kv, k_rope, q_norm[l], w_uq[l], kv_norm[l], w_ukv[l], cos, sin)
        yb = _fox(fq, fk, fv, f_logit, f_bias[l])
        yc = _chunk_rel(cq, ck, cv, rel_bias[l])
        ga, gb, gc = jnp.split(out_norm[l], [A_WIDTH, A_WIDTH + B_WIDTH])
        y = jnp.concatenate([_rmsnorm(ya, ga), _rmsnorm(yb, gb), _rmsnorm(yc, gc)], axis=-1)
        x = x + y @ w_o[l]
        x = x + _cross(_rmsnorm(x, norm_cross[l]), _rmsnorm(mem, norm_mem[l]),
                       w_cq[l], w_ckv[l], w_co[l])
        h = _rmsnorm(x, norm_ffn[l])
        gate, up = jnp.split(h @ w_gu[l], 2, axis=-1)
        x = x + (jax.nn.silu(gate) * up) @ w_down[l]
    return _rmsnorm(x, final_norm)


def setup_inputs(seed=0):
    out = dict(first_inputs(seed))
    for name, value in second_inputs(seed + 1).items():
        if name != "x":
            out[name + "_2"] = value
    return out


def reference(
    x, mix_pre_g, mix_post_g, ffn_pre_g, ffn_post_g, w_in, conv_dw, conv_dw_b, conv_ln_g,
    conv_ln_b, w_conv_pw, attn_sinks, rel_bias, w_out, w_gate, w_up, w_down, mem_2, norm_mix_2,
    w_in_2, q_norm_2, w_uq_2, kv_norm_2, w_ukv_2, f_bias_2, rel_bias_2, out_norm_2, w_o_2,
    norm_cross_2, norm_mem_2, w_cq_2, w_ckv_2, w_co_2, norm_ffn_2, w_gu_2, w_down_2,
    final_norm_2,
):
    x = first_block(
        x, mix_pre_g, mix_post_g, ffn_pre_g, ffn_post_g, w_in, conv_dw, conv_dw_b, conv_ln_g,
        conv_ln_b, w_conv_pw, attn_sinks, rel_bias, w_out, w_gate, w_up, w_down,
    )
    return second_block(
        x, mem_2, norm_mix_2, w_in_2, q_norm_2, w_uq_2, kv_norm_2, w_ukv_2, f_bias_2,
        rel_bias_2, out_norm_2, w_o_2, norm_cross_2, norm_mem_2, w_cq_2, w_ckv_2, w_co_2,
        norm_ffn_2, w_gu_2, w_down_2, final_norm_2,
    )


_drawn_inputs = setup_inputs


def setup_inputs(seed=0):
    import zlib

    import numpy as np

    out = dict(_drawn_inputs(seed))
    spreads = {}
    factors = {'attn_sinks': 8.0,
     'q_norm_2': 6.653,
     'norm_cross_2': 8.0,
     'norm_mem_2': 8.0,
     'norm_ffn_2': 2.757}
    for name, (base, spread) in spreads.items():
        noise = np.random.default_rng([zlib.crc32(name.encode()), seed]).standard_normal(out[name].shape)
        drawn = base * np.exp(spread * noise) if base else spread * noise
        out[name] = jnp.asarray(drawn.astype(out[name].dtype))
    for name, factor in factors.items():
        out[name] = (out[name] * factor).astype(out[name].dtype)
    return out
```

```python
import math
from contextlib import ExitStack

import numpy as np

import concourse.bass as bass
from concourse import mybir

F32 = mybir.dt.float32
F32R = mybir.dt.float32r
ACT = mybir.ActivationFunctionType
ALU = mybir.AluOpType
AX = mybir.AxisListType

S = 1024
D = 1024
NT = 8
FF = 2816
NF = FF // 128
EPS = 1e-6
NEG = -1e30
TAPS = 31
KB = 1024


class Queue:

    def __init__(self, sem):
        self.sem, self.items, self.count, self.met = sem, [], 0, {}

    def put(self, fn, *waits, inc=True):
        need = {}
        for sem, value in flat(waits):
            if self.met.get(sem.name, 0) < value:
                self.met[sem.name] = value
                need[sem.name] = (sem, value)
        if inc:
            self.count += 1
        self.items.append((list(need.values()), fn, inc))
        return (self.sem, self.count) if inc else None

    def last(self):
        return [(self.sem, self.count)] if self.count else []

    def run(self, eng):
        for need, fn, inc in self.items:
            for sem, value in need:
                eng.wait_ge(sem, value)
            ins = fn(eng)
            if inc:
                ins.then_inc(self.sem, 1)


class Landing:

    def __init__(self, sem):
        self.sem, self.count = sem, 0

    def start(self, queue, out, in_, *waits, **how):
        self.count += 16
        sem = self.sem
        queue.put(lambda e: e.dma_start(out, in_, **how).then_inc(sem, 16), *waits, inc=False)
        return (sem, self.count)

    def last(self):
        return [(self.sem, self.count)] if self.count else []


class Place:

    def __init__(self, ap, index=0):
        self.ap, self.index, self.free = ap, index, []


class Ring:
    def __init__(self, places):
        self.places, self.n = places, 0

    def take(self):
        self.n += 1
        return self.places[(self.n - 1) % len(self.places)]


def flat(tokens):
    for t in tokens:
        if t is None:
            continue
        if isinstance(t, tuple) and not isinstance(t[0], (tuple, list)):
            yield t
        else:
            yield from flat(t)


def bucket_of(dist):
    d = np.maximum(dist, 1).astype(np.float32)
    large = 16 + (np.log(d / np.float32(16)) / np.float32(math.log(8.0)) * np.float32(16)).astype(np.int32)
    return np.where(dist < 16, dist, np.minimum(large, 31))


def constants():
    ident = np.eye(128, dtype=np.float32)
    oh1 = np.zeros((33, 383), np.float32)
    for j in range(383):
        dist = 255 - j
        if 0 <= dist < 128:
            oh1[int(bucket_of(np.array([dist]))[0]), j] = 1.0
        else:
            oh1[32, j] = NEG
    oh2 = np.zeros((192, 767), np.float32)
    for j in range(767):
        oh2[min(max(639 - j, -63), 128) + 63, j] = 1.0
    q = np.arange(128)
    causal = np.where(q[None, :] <= q[:, None], 0.0, NEG).astype(np.float32)
    pos = np.arange(S, dtype=np.float32)
    inv = np.power(np.float32(10000.0), -np.arange(0, 32, 2, dtype=np.float32) / np.float32(32)).astype(np.float32)
    ang = (pos[:, None] * inv[None, :]).astype(np.float32)
    cos, sin = np.cos(ang).astype(np.float32), np.sin(ang).astype(np.float32)
    ropeq = np.concatenate([cos.T, cos.T, -sin.T, sin.T], 0)
    ropek = np.concatenate([cos, cos, -sin, sin], 1).reshape(NT, 128, 64).transpose(1, 0, 2)
    return {"c_ident": ident, "c_oh1": oh1, "c_oh2": oh2, "c_causal": causal,
            "c_ropeq": np.ascontiguousarray(ropeq), "c_ropek": np.ascontiguousarray(ropek)}


def block_kernel(nc, I, out):
    ctx = ExitStack()
    with ctx:
        build(nc, ctx, I, out)


def build(nc, ctx, I, out_dram):
    BASE = 16512
    RING = 5
    off = {"stage": BASE, "wh": BASE + 8 * KB, "wl": BASE + (8 + 4 * RING) * KB}
    off["ah"] = off["wl"] + 4 * RING * KB
    off["al"] = off["ah"] + 32 * KB
    off["sg"] = off["al"] + 32 * KB
    off["big"] = off["sg"] + 4 * KB
    off["small"] = off["big"] + 88 * KB
    BIG = off["big"]

    def sb(name, shape, at, dt=F32):
        return nc.alloc_sbuf_tensor_at(name, shape, dt, offset=at)

    def big(name, shape, kb, dt=F32):
        return sb(name, shape, BIG + int(kb * KB), dt)

    def sem(name):
        return ctx.enter_context(nc.semaphore(name))

    PE, AC, DV, PL, SP = (Queue(sem("s_" + n)) for n in ("pe", "act", "dve", "pool", "sp"))

    def mark():
        return PE.last() + AC.last() + DV.last() + PL.last()

    P = ctx.enter_context(nc.psum_tensor("P", [128, 8, 512], F32))
    PF = P[:, :, :].rearrange("p b n -> p (b n)")
    banks = [Place(P[:, i, :], i) for i in range(8)]
    bank_turn = [0]

    def take_bank():
        b = banks[bank_turn[0] % 8]
        bank_turn[0] += 1
        return b

    stage = [sb(f"stage{i}", [128, 1024], off["stage"] + 4 * KB * i) for i in range(2)]
    WH = [sb(f"wh{i}", [128, 1024], off["wh"] + 4 * KB * i, F32R) for i in range(RING)]
    WL = [sb(f"wl{i}", [128, 1024], off["wl"] + 4 * KB * i, F32R) for i in range(RING)]
    AH = sb("ah", [128, 8, 1024], off["ah"], F32R)
    AL = sb("al", [128, 8, 1024], off["al"], F32R)
    sm = [off["small"]]

    def small(name, n):
        t = sb(name, [128, n], sm[0])
        sm[0] += 4 * n
        return t

    ident = small("ident", 128)
    nhalf = small("nhalf", 8)
    sinks = small("sinks", 8)
    nsink = small("nsink", 8)
    stats = small("stats", 480)
    stat_at = [0]

    def col(n=1):
        if stat_at[0] + n > 480:
            stat_at[0] = 0
        stat_at[0] += n
        return stats[:, stat_at[0] - n:stat_at[0]]

    l_const = Landing(sem("l_const"))
    l_stage = [Landing(sem(f"l_stage{i}")) for i in range(2)]
    l_xr = [Landing(sem(f"l_xr{i}")) for i in range(2)]
    l_gb = [Landing(sem(f"l_gb{i}")) for i in range(2)]
    l_h = [Landing(sem(f"l_h{i}")) for i in range(2)]
    l_bias = Landing(sem("l_bias"))
    l_sk = [Landing(sem(f"l_sk{i}")) for i in range(2)]
    l_aug = Landing(sem("l_aug"))
    l_out = [Landing(sem(f"l_out{i}")) for i in range(2)]
    l_misc = Landing(sem("l_misc"))
    l_mem = Landing(sem("l_mem"))

    h1 = nc.dram_tensor("h1", (S, D), F32, kind="Internal").ap()
    h2 = nc.dram_tensor("h2", (S, D), F32, kind="Internal").ap()
    h3 = nc.dram_tensor("h3", (S, D), F32, kind="Internal").ap()
    h4 = nc.dram_tensor("h4", (S, D), F32, kind="Internal").ap()
    sk1 = nc.dram_tensor("sk1", (8, 128 * 384), F32, kind="Internal")
    sk2 = nc.dram_tensor("sk2", (4, 128 * 768), F32, kind="Internal")

    t_ident = l_const.start(SP, ident[:, :], I["c_ident"])
    t_nhalf = DV.put(lambda e: e.memset(nhalf[:, :], -0.5))

    def mm(out, l, r, start, stop, *waits, inc=False):
        return PE.put(lambda e: e.matmul(out, l, r, start=start, stop=stop), *waits, inc=inc)

    def mm3(out, lh, ll, rh, rl, start, stop, *waits, inc=False):
        mm(out, lh, rh, start, False, *waits)
        mm(out, lh, rl, False, False)
        return mm(out, ll, rh, False, stop, inc=inc)

    def tr(out, in_, *waits, inc=False):
        p = in_.shape[0]
        return PE.put(lambda e: e.transpose(out, in_, ident[0:p, 0:p]), t_ident, *waits, inc=inc)

    def act(out, in_, func, *waits, **kw):
        return AC.put(lambda e: e.activation(out, in_, func, **kw), *waits)

    def tt(out, a, b, op, *waits):
        return DV.put(lambda e: e.tensor_tensor(out, a, b, op), *waits)

    def ts(out, a, s1, s2, op0, op1, *waits):
        if op1 is None:
            return DV.put(lambda e: e.tensor_scalar(out, a, s1, None, op0), *waits)
        return DV.put(lambda e: e.tensor_scalar(out, a, s1, s2, op0, op1), *waits)

    def stt(out, a, s, b, op0, op1, *waits):
        return DV.put(lambda e: e.scalar_tensor_tensor(out, a, s, b, op0, op1), *waits)

    def cp(out, in_, *waits):
        return DV.put(lambda e: e.tensor_copy(out, in_), *waits)

    def inv_sqrt(v, *waits):
        r = col(v.shape[1])
        n = v.shape[1]
        return r, PL.put(lambda e: e.tensor_tensor(r, v, nhalf[:, 0:n], ALU.pow), t_nhalf, *waits)

    plan = []
    sent = [0]
    used = [0]
    w_slots = [Place(None, i) for i in range(RING)]
    s_slots = [Place(stage[i], i) for i in range(2)]
    ready = {}

    def send_chunk():
        c = sent[0]
        sent[0] += 1
        n, parts = plan[c]
        st, sl = s_slots[c % 2], w_slots[c % RING]
        for dst, src in parts:
            t_in = l_stage[c % 2].start(SP, dst(st.ap), src, st.free)
        i = sl.index
        t_hi = act(WH[i][:, 0:n], st.ap[:, 0:n], ACT.Copy, t_in, sl.free)
        t_lo = PL.put(lambda e: e.tensor_tensor(WL[i][:, 0:n], st.ap[:, 0:n], WH[i][:, 0:n].bitcast(F32), ALU.subtract),
                      t_in, t_hi, sl.free)
        st.free = [t_hi, t_lo]
        ready[c] = [t_hi, t_lo]

    class Chunk:
        pass

    def next_chunk():
        c = used[0]
        used[0] += 1
        while sent[0] <= c:
            send_chunk()
        k = Chunk()
        k.slot = w_slots[c % RING]
        k.hi, k.lo, k.ready = WH[c % RING], WL[c % RING], ready.pop(c)
        return k

    def run_ahead():
        while sent[0] < min(used[0] + RING - 1, len(plan)):
            send_chunk()

    def chunk_done(k, token):
        k.slot.free = [token]
        if sent[0] < len(plan) and sent[0] < used[0] + RING - 1:
            send_chunk()

    def cols_chunk(w, c0, nk=8, n=128):
        src = w[:, c0:c0 + n].rearrange("(k p) c -> p k c", p=128)
        return (nk * n, [(lambda s: s[:, 0:nk * n].rearrange("p (k c) -> p k c", k=nk), src)])

    def rows_chunk(w, ks, ranges):
        width = sum(b - a for a, b in ranges)
        parts = []
        for i, k in enumerate(ks):
            at = i * width
            for a, b in ranges:
                parts.append((lambda s, at=at, n=b - a: s[:, at:at + n], w[k * 128:(k + 1) * 128, a:b]))
                at += b - a
        return (len(ks) * width, parts)

    w_in, w_out, w_pw = I["w_in"], I["w_out"], I["w_conv_pw"]
    w_in2, w_uq, w_ukv, w_o = I["w_in_2"][0], I["w_uq_2"][0], I["w_ukv_2"][0], I["w_o_2"][0]
    w_cq, w_ckv, w_co, w_gu = I["w_cq_2"][0], I["w_ckv_2"][0], I["w_co_2"][0], I["w_gu_2"][0]

    for c in range(4):
        plan.append(cols_chunk(w_in, 1280 + 128 * c))
        plan.append(cols_chunk(w_in, 768 + 128 * c))
    for c0 in (512, 640, 0, 128, 256, 384):
        plan.append(cols_chunk(w_in, c0))
    for m in range(4):
        plan.append(cols_chunk(w_pw, 128 * m, nk=4))

    def plan_tok(w, orders):
        for j, order in enumerate(orders):
            for i in range(0, len(order), 2):
                plan.append(rows_chunk(w, order[i:i + 2], [(512 * j, 512 * j + 512)]))

    down_order = [list(range(NF)), list(range(14, NF)) + list(range(14))]

    def plan_ffn(wg, g0, wu, u0, wd):
        for m in range(NF):
            plan.append(cols_chunk(wg, g0 + 128 * m))
            plan.append(cols_chunk(wu, u0 + 128 * m))
        plan_tok(wd, down_order)

    plan_tok(w_out, [list(range(8))] * 2)
    plan_ffn(I["w_gate"], 0, I["w_up"], 0, I["w_down"])
    for c0 in (1188, 1316, 1444, 1572):
        plan.append(cols_chunk(w_in2, c0))
    for i in range(0, 8, 2):
        plan.append(rows_chunk(w_in2, [i, i + 1], [(928, 1184), (1700, 1956)]))
    for c0 in (416, 544, 672, 800):
        plan.append(cols_chunk(w_in2, c0))
    for i in range(0, 8, 2):
        plan.append(rows_chunk(w_in2, [i, i + 1], [(0, 416), (1184, 1188)]))
    uq_parts = []
    for k in range(2):
        src = w_uq[k * 128:(k + 1) * 128, :].rearrange("p (h c) -> p h c", h=4)
        for a, b, at in ((0, 96, 0), (80, 96, 96), (64, 80, 112)):
            uq_parts.append((lambda s, k=k, at=at, n=b - a: s[:, 512 * k:512 * k + 512].rearrange(
                "p (h c) -> p h c", h=4)[:, :, at:at + n], src[:, :, a:b]))
    plan.append((1024, uq_parts))
    plan.append((768, [(lambda s: s[:, 0:768], w_ukv)]))
    plan_tok(w_o, [list(range(8))] * 2)
    for m in range(4):
        plan.append(cols_chunk(w_cq, 128 * m))
    for m in range(4):
        plan.append(cols_chunk(w_ckv, 128 * m))
    for i in range(0, 8, 2):
        plan.append(rows_chunk(w_ckv, [i, i + 1], [(512, 1024)]))
    plan_tok(w_co, [list(range(4))] * 2)
    plan_ffn(w_gu, 0, w_gu, FF, I["w_down_2"][0])

    col_ready = [[] for _ in range(NT)]
    col_free = [[] for _ in range(NT)]

    def turn_in(src, n, t, k0, *waits):
        made, last = [], None
        for g in range(0, n, 4):
            w = min(4, n - g)
            b = take_bank()
            for j in range(w):
                last = tr(b.ap[:, 128 * j:128 * j + 128], src[:, 128 * (g + j):128 * (g + j) + 128],
                          b.free, *waits, inc=(j == w - 1))
            made += split_in(b, w, AH[:, k0 + g:k0 + g + w, 128 * t:128 * t + 128],
                             AL[:, k0 + g:k0 + g + w, 128 * t:128 * t + 128], last, col_free[t])
        col_ready[t] = col_ready[t] + made
        return last

    def split_in(b, w, hi, lo, *waits):
        v = b.ap[:, 0:128 * w].rearrange("p (k c) -> p k c", k=w)
        t_hi = act(hi, v, ACT.Copy, *waits)
        t_lo = tt(lo, v, hi.bitcast(F32), ALU.subtract, t_hi, *waits)
        b.free = [t_lo]
        return [t_hi, t_lo]

    pending = []

    def flush():
        while pending:
            pending.pop(0)()

    def feature_unit(k, lhs, nk, rhs, th, b, *waits):
        for i in range(nk):
            lh, ll = lhs(i)
            rh, rl = rhs(i)
            tok = mm3(b.ap, lh, ll, rh, rl, i == 0, i == nk - 1, k.ready, b.free, *waits, inc=(i == nk - 1))
        return tok

    def act_cols(th, nk=8):
        return lambda i: (AH[:, i, 512 * th:512 * th + 512], AL[:, i, 512 * th:512 * th + 512])

    def feature_tile(evac, between=None):
        k = next_chunk()
        v = lambda i: (k.hi[:, 128 * i:128 * i + 128], k.lo[:, 128 * i:128 * i + 128])
        for th in range(2):
            if th == 1:
                flush()
            b = take_bank()
            tok = feature_unit(k, v, 8, act_cols(th), th, b, [col_ready[t] for t in range(4 * th, 4 * th + 4)])
            if th == 1:
                chunk_done(k, tok)
            b.free = flatten(evac(th, b, tok))
            if between:
                between()
        return tok

    def flatten(tokens):
        return list(flat([tokens]))

    def all_cols_read(tok):
        for t in range(NT):
            col_free[t] = [tok]

    M0 = [big(f"m0_{t}", [128, 512], 56 + 2 * t) for t in range(NT)]
    GB = [big(f"gb{i}", [128, 1024], 72 + 4 * i) for i in range(2)]
    XR = [Place(big(f"xr{i}", [128, 1024], 80 + 4 * i)) for i in range(2)]
    HT = [Place(big(f"ht{i}", [128, 1024], 4 * i)) for i in range(2)]
    XN = [Place(big(f"xn{i}", [128, 1024], 8 + 4 * i)) for i in range(2)]

    class Passage:

        def __init__(self, x, g_post, g_pre, h, final=False, after=(), xfree=()):
            self.x, self.h, self.final, self.g_post = x, h, final, g_post
            self.after = list(after)
            self.t_gb = [None, None]
            if g_post is not None:
                self.t_gb[0] = l_gb[0].start(SP, GB[0][:, :], g_post.partition_broadcast(128), self.after)
            self.t_gb[1] = l_gb[1].start(SP, GB[1][:, :], g_pre.partition_broadcast(128), self.after)
            for r in (XR, HT, XN):
                for p in r:
                    p.free = list(self.after)
            self.t_x, self.m0, self.ss0, self.r1, self.r2 = {}, {}, {}, {}, {}
            self.t_h, self.t_xn = {}, {}
            for t in range(2):
                self.load(t)

        def load(self, t):
            if t < NT:
                self.t_x[t] = l_xr[t % 2].start(SP, XR[t % 2].ap[:, :], self.x[128 * t:128 * t + 128, :], XR[t % 2].free)

        def keep(self, t, b, tok, *waits):
            t_m = cp(M0[t][:, :], b.ap, tok, self.after, *waits)
            b.free = [t_m]
            self.m0[t] = t_m
            if self.g_post is not None:
                s, v = col(), col()
                junk = HT[t % 2]
                t_s = act(junk.ap[:, 0:512], M0[t][:, :], ACT.Square, t_m, junk.free, accum_out=s)
                junk.free = [t_s]
                self.ss0[t] = (v, ts(v, s, 1.0 / D, EPS, ALU.mult, ALU.add, t_s))

        def a(self, t, b, tok):
            self.tok = tok
            if self.g_post is None:
                return
            s, v = col(), col()
            v0, t_v0 = self.ss0[t]
            j = HT[t % 2]
            t_s = act(j.ap[:, 0:512], b.ap, ACT.Square, tok, j.free, accum_out=s)
            j.free = [t_s]
            t_v = ts(v, s, 1.0 / D, v0, ALU.mult, ALU.add, t_s, t_v0)
            self.r1[t] = inv_sqrt(v, t_v)

        def b(self, t, b, tok):
            H, X = HT[t % 2], XR[t % 2]
            h = H.ap
            if self.g_post is not None:
                r, t_r = self.r1[t]
                stt(h[:, 0:512], M0[t][:, :], r, GB[0][:, 0:512], ALU.mult, ALU.mult, t_r, self.t_gb[0], self.m0[t], H.free)
                t_u = stt(h[:, 512:], b.ap, r, GB[0][:, 512:], ALU.mult, ALU.mult, tok)
                b.free = [t_u]
                t_h = tt(h[:, :], h[:, :], X.ap[:, :], ALU.add, t_u, self.t_x[t])
            else:
                tt(h[:, 0:512], M0[t][:, :], X.ap[:, 0:512], ALU.add, self.m0[t], self.t_x[t], H.free)
                t_h = tt(h[:, 512:], b.ap, X.ap[:, 512:], ALU.add, tok)
                b.free = [t_h]
            X.free = [t_h]
            self.load(t + 2)
            s, v = col(), col()
            t_s = act(XN[t % 2].ap[:, :], h[:, :], ACT.Square, t_h, XN[t % 2].free, accum_out=s)
            H.free = [t_s]
            if self.h is not None:
                H.free.append(l_h[t % 2].start(AC, self.h[128 * t:128 * t + 128, :], h[:, :], t_h))
            t_v = ts(v, s, 1.0 / D, EPS, ALU.mult, ALU.add, t_s)
            self.r2[t] = inv_sqrt(v, t_v)
            self.t_h[t] = t_h

        def c(self, t):
            r, t_r = self.r2[t]
            X, H = XN[t % 2], HT[t % 2]
            self.t_xn[t] = stt(X.ap[:, :], H.ap[:, :], r, GB[1][:, :], ALU.mult, ALU.mult, t_r, self.t_gb[1])
            H.free.append(self.t_xn[t])
            if self.final:
                X.free = [l_out[t % 2].start(SP, out_dram[128 * t:128 * t + 128, :], X.ap[:, :], self.t_xn[t])]

        def d(self, t):
            if not self.final:
                col_ready[t] = []
                XN[t % 2].free = [turn_in(XN[t % 2].ap, 8, t, 0, self.t_xn[t])]

    def token_stage(order, slot, col_tok, passage, extra=None, keep_waits=()):
        last_use = {}
        for j in range(2):
            ks = order[j]
            tail = 2 if j == 0 else min(8, len(ks))
            held = []
            for t in range(NT):
                banks[t].open = False
            body = len(ks) - tail
            for i in range(0, body, 2):
                k = next_chunk()
                for ii in range(2):
                    p = i + ii
                    if extra:
                        extra(j, p)
                    for t in range(NT):
                        s = slot(j, p)
                        tok = mm3(banks[t].ap, AH[:, s, 128 * t:128 * t + 128], AL[:, s, 128 * t:128 * t + 128],
                                  k.hi[:, 512 * ii:512 * ii + 512], k.lo[:, 512 * ii:512 * ii + 512], p == 0, False,
                                  k.ready, banks[t].free if p == 0 else None, col_tok(j, p, t), inc=(t == NT - 1))
                    last_use[s] = tok
                    if extra:
                        extra.used(j, p, tok)
                chunk_done(k, tok)
            chunks = [next_chunk() for _ in range(tail // 2)]
            if extra:
                for p in range(body, len(ks)):
                    extra(j, p)
            for t in range(NT):
                for p in range(body, len(ks)):
                    k, ii, s = chunks[(p - body) // 2], (p - body) % 2, slot(j, p)
                    tok = mm3(banks[t].ap, AH[:, s, 128 * t:128 * t + 128], AL[:, s, 128 * t:128 * t + 128],
                              k.hi[:, 512 * ii:512 * ii + 512], k.lo[:, 512 * ii:512 * ii + 512], p == 0,
                              p == len(ks) - 1, k.ready, banks[t].free if p == 0 else None, col_tok(j, p, t),
                              inc=(p == len(ks) - 1))
                if j == 0:
                    passage.keep(t, banks[t], tok, *keep_waits)
                    if t == NT - 1:
                        for k in chunks:
                            chunk_done(k, tok)
                        if extra:
                            for p in range(body, len(ks)):
                                extra.used(j, p, tok)
                else:
                    if t == NT - 1:
                        for k in chunks:
                            chunk_done(k, tok)
                    col_free[t] = [tok]
                    passage.a(t, banks[t], tok)
                    if t >= 2:
                        bank_turn[0] = t - 2
                        passage.d(t - 2)
                    if t >= 1:
                        passage.c(t - 1)
                    passage.b(t, banks[t], tok)
        passage.c(NT - 1)
        bank_turn[0] = 0

        def tail_turn(t):
            bank_turn[0] = 2 * (t - 5)
            passage.d(t)
            bank_turn[0] = 6

        if not passage.final:
            pending.append(lambda: tail_turn(6))
            pending.append(lambda: tail_turn(7))
        run_ahead()

    def softmax_rows(src, dst, n, nm, t_nm, waits=(), scale=1.0):
        rs = col()
        return rs, act(dst, src, ACT.Exp, t_nm, *waits, bias=nm, accum_out=rs)

    SGT = [sb(f"sg{i}", [128, 512], off["sg"] + 2 * KB * i) for i in range(2)]
    SGR = Ring([Place(t) for t in SGT])

    oh1 = big("oh1", [33, 383], 20)
    rb1 = big("rb1", [33, 8], 22)
    oh2a = big("oh2a", [128, 767], 24)
    oh2b = big("oh2b", [64, 767], 28)
    rb2a = big("rb2a", [128, 4], 32)
    rb2b = big("rb2b", [64, 4], 32.5)
    ones_row = DV.put(lambda e: e.memset(rb1[32:33, :], 1.0))
    l_misc.start(SP, oh1[:, :], I["c_oh1"])
    l_misc.start(SP, rb1[0:32, :], I["rel_bias"])
    l_misc.start(SP, oh2a[:, :], I["c_oh2"][0:128, :])
    l_misc.start(SP, oh2b[:, :], I["c_oh2"][128:192, :])
    rel2 = I["rel_bias_2"][0]
    l_misc.start(SP, rb2a[:, :], rel2[:, 0:128].rearrange("h r -> r h"), allow_slow_non_contiguous=True)
    l_misc.start(SP, rb2b[:, :], rel2[:, 128:192].rearrange("h r -> r h"), allow_slow_non_contiguous=True)
    cw = big("cw", [34, 512], 33)
    l_misc.start(SP, cw[0:31, :], I["conv_dw"])
    for i, name in enumerate(("conv_dw_b", "conv_ln_g", "conv_ln_b")):
        l_misc.start(SP, cw[31 + i:32 + i, :], I[name].rearrange("(a n) -> a n", a=1))
    t_misc = l_misc.start(SP, sinks[:, :], I["attn_sinks"].partition_broadcast(128))
    t_nsink = ts(nsink[:, :], sinks[:, :], -1.0, None, ALU.mult, None, t_misc)

    pas0 = Passage(I["x"], None, I["mix_pre_g"], None)
    t_xn0 = {}
    for t in range(NT):
        X = XR[t % 2]
        s, v = col(), col()
        N = XN[t % 2]
        t_s = act(N.ap[:, :], X.ap[:, :], ACT.Square, pas0.t_x[t], N.free, accum_out=s)
        t_v = ts(v, s, 1.0 / D, EPS, ALU.mult, ALU.add, t_s)
        r, t_r = inv_sqrt(v, t_v)
        t_n = stt(N.ap[:, :], X.ap[:, :], r, GB[1][:, :], ALU.mult, ALU.mult, t_r, pas0.t_gb[1])
        X.free = [t_n]
        pas0.load(t + 2)
        N.free = [turn_in(N.ap, 8, t, 0, t_n)]

    l_sk_tok = []
    for h in range(8):
        b, g = take_bank(), SGR.take()
        t_m = mm(b.ap[:, 0:383], rb1[0:33, h:h + 1].to_broadcast([33, 128]), oh1[:, :], True, True,
                 t_misc, ones_row, b.free, inc=True)
        t_c = cp(g.ap[:, 0:383], b.ap[:, 0:383], t_m, g.free)
        b.free = [t_c]
        g.free = [l_sk[h % 2].start(SP, bass.AP(sk1, h * 128 * 384, [[384, 128], [1, 383]]), g.ap[:, 0:383], t_c)]
        l_sk_tok.append(g.free[0])
    for h in range(4):
        for a, n in ((0, 512), (512, 255)):
            b, g = take_bank(), SGR.take()
            mm(b.ap[:, 0:n], rb2a[:, h:h + 1].to_broadcast([128, 128]), oh2a[:, a:a + n], True, False, t_misc, b.free)
            t_m = mm(b.ap[:, 0:n], rb2b[:, h:h + 1].to_broadcast([64, 128]), oh2b[:, a:a + n], False, True, inc=True)
            t_c = cp(g.ap[:, 0:n], b.ap[:, 0:n], t_m, g.free)
            b.free = [t_c]
            g.free = [l_sk[(a > 0)].start(SP, bass.AP(sk2, h * 128 * 768 + a, [[768, 128], [1, n]]), g.ap[:, 0:n], t_c)]
            l_sk_tok.append(g.free[0])
    t_skew = l_sk[0].last() + l_sk[1].last()

    q1 = big("q1", [128, 4, 1024], 0)
    kp1 = big("kp1", [128, 4, 1024], 16)
    v1 = big("v1", [128, 8, 128], 32)
    hp = big("hp", [128, 4, 1054], 36)
    acc = big("acc", [128, 4, 1024], 52.5)
    b1 = big("b1", [128, 8, 256], 68.5)
    s1 = [Place(big(f"s1_{i}", [128, 2, 256], 76.5 + 2 * i)) for i in range(2)]
    v1t = big("v1t", [128, 1024], 76.5)
    pt1 = [Place(big(f"pt1_{i}", [128, 4, 128], 80.5 + 2 * i)) for i in range(2)]
    o1 = Place(big("o1", [128, 512], 84.5))
    cwt = big("cwt", [128, 4, 34], 86.5)

    b = take_bank()
    for c in range(4):
        t_m = tr(b.ap[:, 34 * c:34 * c + 34], cw[0:34, 128 * c:128 * c + 128], t_misc, b.free, inc=(c == 3))
    t_cw = cp(cwt[:, :, :], b.ap[:, 0:136].rearrange("p (c w) -> p c w", c=4), t_m)
    b.free = [t_cw]
    first = mark() + t_skew + l_xr[0].last() + l_xr[1].last()
    t_b1 = l_bias.start(SP, b1[:, :, :], bass.AP(sk1, 127, [[383, 128], [128 * 384, 8], [1, 256]]), first)
    t_hp0 = DV.put(lambda e: e.memset(hp[:, :, 0:30], 0.0), first)

    taps = []

    def tap_steps(c, t_h):
        state = [None]

        def step(w):
            def go():
                src = hp[:, c, w:w + 1024]
                if w == 0:
                    state[0] = ts(acc[:, c, :], src, cwt[:, c, 0:1], cwt[:, c, 31:32], ALU.mult, ALU.add,
                                  t_h, t_cw, t_hp0, first)
                else:
                    state[0] = stt(acc[:, c, :], src, cwt[:, c, w:w + 1], acc[:, c, :], ALU.mult, ALU.add, state[0])
            return go

        taps.extend(step(w) for w in range(TAPS))

    def some_taps(n):
        for _ in range(min(n, len(taps))):
            taps.pop(0)()

    for c in range(4):
        sg = {}

        def gate(th, b, tok):
            g = SGR.take()
            sg[th] = (g, act(g.ap[:, :], b.ap, ACT.Sigmoid, tok, g.free))
            return [sg[th][1]]

        t_hc = []

        def glu(th, b, tok):
            g, t_g = sg[th]
            t = tt(hp[:, c, 30 + 512 * th:542 + 512 * th], b.ap, g.ap[:, :], ALU.mult, tok, t_g, first)
            g.free = [t]
            t_hc.append(t)
            return [t]

        feature_tile(gate, lambda: some_taps(4))
        feature_tile(glu, lambda: some_taps(4))
        tap_steps(c, t_hc)

    t_kz = []
    for g in range(2):
        for s_ in range(2):
            z = 64 * (1 - s_)
            t_kz.append(DV.put(lambda e, i=2 * g + s_, z=z: e.memset(kp1[z:z + 64, i, :], 0.0), first))
    t_k1 = []

    def k_out(th, b, tok):
        cs = slice(512 * th, 512 * th + 512)
        t = []
        for g in range(2):
            for s_ in range(2):
                o, i = kp1[64 * s_:64 * s_ + 64, 2 * g + s_, cs], b.ap[64 * g:64 * g + 64, :]
                t.append(act(o, i, ACT.Copy, tok, first))
        t_k1.extend(t)
        return t

    feature_tile(k_out, lambda: some_taps(4))
    t_vt = []

    def v_out(th, b, tok):
        t = act(v1t[:, 512 * th:512 * th + 512], b.ap, ACT.Copy, tok, first)
        t_vt.append(t)
        return [t]

    feature_tile(v_out, lambda: some_taps(4))
    t_v1 = []

    def v_turn():
        for g in range(2):
            b = take_bank()
            for j in range(4):
                t = 4 * g + j
                t_m = tr(b.ap[:, 128 * j:128 * j + 128], v1t[:, 128 * t:128 * t + 128], t_vt, b.free, inc=(j == 3))
            t_c = act(v1[:, 4 * g:4 * g + 4, :], b.ap.rearrange("p (t d) -> p t d", t=4), ACT.Copy, t_m, first)
            b.free = [t_c]
            t_v1.append(t_c)
        s1[0].free, s1[1].free = [t_m], [t_m]

    t_q1 = {}

    def q_out(m):
        def go(th, b, tok):
            t = act(q1[:, m, 512 * th:512 * th + 512], b.ap, ACT.Copy, tok, first, scale=0.125)
            t_q1[m] = t
            return [t]
        return go

    for m in range(4):
        tok = feature_tile(q_out(m), lambda: some_taps(4))
        if m == 0:
            v_turn()
    all_cols_read(tok)

    def attention(steps, scores, soft, turn, values):
        n = len(steps)
        for i in range(n + 2):
            if i < n:
                scores(i)
                soft(i)
            if i >= 2:
                values(i - 2)
            if 1 <= i <= n:
                turn(i - 1)
            some_taps(1)
            for due, fn in list(later):
                if due <= i:
                    later.remove((due, fn))
                    fn()
        for due, fn in list(later):
            later.remove((due, fn))
            fn()

    later = []
    sc_banks = [banks[0], banks[1]]
    tr_banks = Ring([banks[2], banks[3]])
    o_banks = [banks[4], banks[5]]
    y_banks = [6, 7]
    st = {}
    steps1 = [(n, g) for n in range(NT) for g in range(4)]

    def sc1(i):
        n, g = steps1[i]
        W = 128 if n == 0 else 256
        b = sc_banks[i % 2]
        for j in range(2):
            kv = g // 2
            t_m = mm(b.ap[:, 256 * j:256 * j + W], q1[:, g, 128 * n:128 * n + 128],
                     kp1[:, 2 * kv + j, 128 * (n + 1) - W:128 * (n + 1)], True, True,
                     t_q1[g], t_k1, t_kz, b.free, inc=(j == 1))
        st[i] = {"W": W, "sc": t_m}

    rows = {}

    def so1(i):
        n, g = steps1[i]
        d = st[i]
        W, b, s = d["W"], sc_banks[i % 2], s1[i % 2]
        if g == 0:
            rows[n] = {"rs": col(8), "es": col(8), "t": []}
        mx, nm, es = col(2), col(2), col(2)
        for j in range(2):
            h = 2 * g + j
            t_x = DV.put(lambda e, j=j, h=h: e.tensor_tensor_reduce(
                out=s.ap[:, j, 0:W], in0=b.ap[:, 256 * j:256 * j + W], in1=b1[:, h, 256 - W:256], scale=1.0,
                scalar=NEG, op0=ALU.add, op1=ALU.max, accum_out=mx[:, j:j + 1]), d["sc"], t_b1, s.free)
        b.free = [t_x]
        t_n = stt(nm, mx, -1.0, nsink[:, 2 * g:2 * g + 2], ALU.mult, ALU.min, t_x, t_nsink)
        t_d = tt(es, nm, sinks[:, 2 * g:2 * g + 2], ALU.add, t_n)
        for j in range(2):
            t_e = act(s.ap[:, j, 0:W], s.ap[:, j, 0:W], ACT.Exp, t_n, bias=nm[:, j:j + 1],
                      accum_out=rows[n]["rs"][:, 2 * g + j:2 * g + j + 1])
        rows[n]["t"].append(act(rows[n]["es"][:, 2 * g:2 * g + 2], es, ACT.Exp, t_d))
        d["p"] = t_e

    def tu1(i):
        d = st[i]
        W, s, pt = d["W"], s1[i % 2], pt1[i % 2]
        nb = W // 128
        b = tr_banks.take()
        for j in range(2):
            for kb in range(nb):
                t_m = tr(b.ap[:, 128 * (nb * j + kb):128 * (nb * j + kb) + 128], s.ap[:, j, 128 * kb:128 * kb + 128],
                         d["p"], b.free, inc=(j == 1 and kb == nb - 1))
        s.free = [t_m]
        o, v = pt.ap[:, 0:2 * nb, :], b.ap[:, 0:256 * nb].rearrange("p (k c) -> p k c", c=128)
        t_c = act(o, v, ACT.Copy, t_m, pt.free)
        b.free = [t_c]
        d["pt"] = t_c

    def va1(i):
        n, g = steps1[i]
        d = st[i]
        W, pt, ob = d["W"], pt1[i % 2], o_banks[n % 2]
        nb, kv = W // 128, g // 2
        for j in range(2):
            for kb in range(nb):
                h = 2 * g + j
                t_m = mm(ob.ap[:, 64 * h:64 * h + 64], pt.ap[:, nb * j + kb, :],
                         v1[:, n + 1 - nb + kb, 64 * kv:64 * kv + 64], kb == 0, kb == nb - 1,
                         d["pt"], t_v1, ob.free if g == 0 else None, inc=(j == 1 and kb == nb - 1))
        pt.free = [t_m]
        if g == 3:
            r = rows[n]
            den, rden = col(8), col(8)
            t_d = tt(den, r["rs"], r["es"], ALU.add, r["t"], AC.last())
            t_r = DV.put(lambda e: e.reciprocal(rden, den), t_d)
            t_o = tt(o1.ap[:, :].rearrange("p (h d) -> p h d", h=8), ob.ap.rearrange("p (h d) -> p h d", h=8),
                     rden.unsqueeze(2).to_broadcast([128, 8, 64]), ALU.mult, t_r, t_m, o1.free)
            ob.free = [t_o]

            def turn_y():
                bank_turn[0] = y_banks[n % 2]
                col_ready[n] = []
                o1.free = [turn_in(o1.ap, 4, n, 0, t_o)]
            later.append((i + 3, turn_y))

    attention(steps1, sc1, so1, tu1, va1)
    bank_turn[0] = 0

    some_taps(len(taps))
    t_conv = DV.last()
    done1 = mark()
    ZH = big("zh", [128, 4, 1024], 0, F32R)
    ZL = big("zl", [128, 4, 1024], 16, F32R)
    yc1 = [Place(big(f"yc1_{i}", [128, 512], 76.5 + 2 * i)) for i in range(4)]
    t_z = {}

    def ln_tile(tb):
        b, y = take_bank(), yc1[tb % 4]
        for c in range(4):
            t_m = tr(b.ap[:, 128 * c:128 * c + 128], acc[:, c, 128 * tb:128 * tb + 128], t_conv, b.free, inc=(c == 3))
        bs, mv, v = col(6), col(2), col()
        t_b = DV.put(lambda e: e.bn_stats(bs, b.ap), t_m)
        t_a = DV.put(lambda e: e.bn_aggr(mv, bs), t_b)
        t_v = ts(v, mv[:, 1:2], EPS, None, ALU.add, None, t_a)
        r, t_r = inv_sqrt(v, t_v)
        t_y = ts(y.ap[:, :], b.ap, mv[:, 0:1], r, ALU.subtract, ALU.mult, t_r, y.free, done1)
        b.free = [t_y]
        return t_y

    for th in range(2):
        t_y = [ln_tile(4 * th + j) for j in range(4)]
        t_last = []
        for c in range(4):
            b, g = take_bank(), SGR.take()
            for j in range(4):
                t_m = tr(b.ap[:, 128 * j:128 * j + 128], yc1[j].ap[:, 128 * c:128 * c + 128], t_y, b.free, inc=(j == 3))
            t_s = act(g.ap[:, :], b.ap, ACT.Silu, t_m, g.free, bias=cwt[:, c, 33:34], scale=cwt[:, c, 32:33])
            b.free = [t_s]
            cs = slice(512 * th, 512 * th + 512)
            t_hi = act(ZH[:, c, cs], g.ap[:, :], ACT.Copy, t_s, done1)
            t_lo = tt(ZL[:, c, cs], g.ap[:, :], ZH[:, c, cs].bitcast(F32), ALU.subtract, t_hi)
            g.free = [t_lo]
            t_z[th, c] = [t_hi, t_lo]
        for j in range(4):
            yc1[j].free = [t_m]

    for m in range(4):
        k = next_chunk()
        v = lambda i: (k.hi[:, 128 * i:128 * i + 128], k.lo[:, 128 * i:128 * i + 128])
        for th in range(2):
            b = take_bank()
            cs = slice(512 * th, 512 * th + 512)
            tok = feature_unit(k, v, 4, lambda i: (ZH[:, i, cs], ZL[:, i, cs]), th, b, [t_z[th, c] for c in range(4)])
            hi, lo = AH[:, 4 + m, cs], AL[:, 4 + m, cs]
            t_hi = act(hi, b.ap, ACT.Copy, tok, col_free[0])
            t_lo = tt(lo, b.ap, hi.bitcast(F32), ALU.subtract, t_hi, col_free[0])
            b.free = [t_lo]
            for t in range(4 * th, 4 * th + 4):
                col_ready[t] = col_ready[t] + [t_hi, t_lo]
        chunk_done(k, tok)

    pas = Passage(I["x"], I["mix_post_g"], I["ffn_pre_g"], h1, after=mark() + [t_b1])
    eight = [list(range(8))] * 2
    token_stage(eight, lambda j, p: p, lambda j, p, t: col_ready[t], pas)

    ff_big = big("ff", [128, NF, 1024], 0)

    def ffn(x, g_post, g_pre, h, final=False):
        nonlocal pas
        t_ff = {}
        held = {}
        entered = mark()
        store = l_h[0].last() + l_h[1].last()

        class Split:
            free = {}
            made = {}
            done = 0

            def __call__(self, j, p):
                at = p if j == 0 else 14 + p
                goal = min(at + 5, NF if j == 0 else NF + 14)
                while self.done < goal:
                    self.one(self.done)
                    self.done += 1

            def one(self, at):
                f = at % NF
                s = at % 8
                w = self.free.get(s, col_free[0])
                t_hi = act(AH[:, s, :], ff_big[:, f, :], ACT.Copy, t_ff[f], w)
                t_lo = tt(AL[:, s, :], ff_big[:, f, :], AH[:, s, :].bitcast(F32), ALU.subtract, t_hi, w)
                self.made[at] = [t_hi, t_lo]

            def used(self, j, p, tok):
                at = p if j == 0 else 14 + p
                self.free[at % 8] = [tok]

        for m in range(NF):
            sg = {}

            def gate(th, b, tok):
                g = SGR.take()
                sg[th] = (g, act(g.ap[:, :], b.ap, ACT.Silu, tok, g.free))
                return [sg[th][1]]

            def up(th, b, tok):
                g, t_g = sg[th]
                w = held.get("mark")
                t = tt(ff_big[:, m, 512 * th:512 * th + 512], b.ap, g.ap[:, :], ALU.mult, tok, t_g, w)
                g.free = [t]
                t_ff.setdefault(m, []).append(t)
                return [t]

            feature_tile(gate)
            if m == 0:
                held["mark"] = mark() + store + l_h[0].last() + l_h[1].last()
            tok = feature_tile(up)
        all_cols_read(tok)
        split = Split()
        split(0, 0)

        def slot(j, p):
            return (p if j == 0 else 14 + p) % 8

        def col_tok(j, p, t):
            return split.made[p if j == 0 else 14 + p]

        class Later:
            pas = None

            def begin(self):
                spent = flatten([split.made[a] for a in range(14, 22)])
                p = self.pas = Passage.__new__(Passage)
                p.x, p.h, p.final, p.g_post, p.after = x, h, final, g_post, spent
                p.t_gb = [None, None]
                if g_post is not None:
                    p.t_gb[0] = l_gb[0].start(SP, GB[0][:, :], g_post.partition_broadcast(128), spent)
                p.t_gb[1] = l_gb[1].start(SP, GB[1][:, :], g_pre.partition_broadcast(128), spent)
                for q in XR:
                    q.free = spent
                p.t_x, p.m0, p.ss0, p.r1, p.r2, p.t_h, p.t_xn = {}, {}, {}, {}, {}, {}, {}
                for t in range(2):
                    p.load(t)
                p.g_post = None
                self.p = p

            def keep(self, t, b, tok, *waits):
                if self.pas is None:
                    self.begin()
                self.p.keep(t, b, tok, *waits)

            def squares(self):
                spent = flatten([split.made[a] for a in range(22, 26)])
                p = self.p
                p.g_post = g_post
                for q in HT + XN:
                    q.free = spent
                if g_post is not None:
                    for t in range(NT):
                        s, v = col(), col()
                        j = HT[t % 2]
                        t_s = act(j.ap[:, 0:512], M0[t][:, :], ACT.Square, p.m0[t], j.free, accum_out=s)
                        j.free = [t_s]
                        p.ss0[t] = (v, ts(v, s, 1.0 / D, EPS, ALU.mult, ALU.add, t_s))

            def a(self, t, b, tok):
                if t == 0:
                    self.squares()
                self.p.a(t, b, tok)

            def b(self, t, b, tok):
                self.p.b(t, b, tok)

            def c(self, t):
                self.p.c(t)

            def d(self, t):
                self.p.d(t)

            @property
            def final(self):
                return final

        later_pas = Later()
        token_stage(down_order, slot, col_tok, later_pas, extra=split)

    ffn(h1, I["ffn_post_g"], I["norm_mix_2"][0], h2)

    cv = big("cv", [128, 8, 256], 0)
    fv = big("fv", [128, 8, 256], 8)
    cq = big("cq", [128, 2, 1024], 16)
    ckp = big("ckp", [128, 4, 1024], 24)
    b2 = big("b2", [128, 4, 640], 40)
    s2 = [Place(big(f"s2_{i}", [128, 640], 50 + 2.5 * i)) for i in range(2)]
    pt2 = [Place(big(f"pt2_{i}", [128, 5, 128], 55 + 2.5 * i)) for i in range(2)]
    o2 = [Place(big(f"o2_{i}", [128, 256], 60 + i)) for i in range(2)]
    yc = big("yc", [128, 8, 256], 62)
    gout = sb("gout", [128, 1024], off["sg"])
    fqp = big("fqp", [128, 4, 1024], 70)
    fkp = big("fkp", [128, 4, 1024], 16)
    CH = big("ch", [128, 3, 1024], 32, F32R)
    CL = big("cl", [128, 3, 1024], 44, F32R)
    kpe = big("kpe", [128, 1024], 4)

    in0 = mark()
    t_ckz = [DV.put(lambda e, h=h: e.memset(ckp[64 * (1 - h % 2):64 * (1 - h % 2) + 64, h, :], 0.0), in0) for h in range(4)]
    t_cq, t_ck = [], []

    def cq_out(m):
        def go(th, b, tok):
            t_cq.append(act(cq[:, m, 512 * th:512 * th + 512], b.ap, ACT.Copy, tok, in0, scale=0.125))
            return [t_cq[-1]]
        return go

    def pair_out(dst, m, toks, scale, waits):
        def go(th, b, tok):
            t = []
            for s_ in range(2):
                t.append(act(dst[64 * s_:64 * s_ + 64, 2 * m + s_, 512 * th:512 * th + 512],
                             b.ap[64 * s_:64 * s_ + 64, :], ACT.Copy, tok, waits, scale=scale))
            toks.extend(t)
            return t
        return go

    for m in range(2):
        feature_tile(cq_out(m))
    in1 = mark() + l_h[0].last() + l_h[1].last()
    t_gout = l_gb[0].start(SP, gout[:, :], I["out_norm_2"][0].partition_broadcast(128), in1)
    t_b2 = l_bias.start(SP, b2[:, :, :], bass.AP(sk2, 127, [[767, 128], [128 * 768, 4], [1, 640]]), in1, t_skew)
    t_b2m = [DV.put(lambda e: e.memset(b2[0:64, :, 576:640], NEG), t_b2),
             DV.put(lambda e: e.memset(b2[64:128, :, 0:64], NEG), t_b2)]
    for m in range(2):
        feature_tile(pair_out(ckp, m, t_ck, 1.0, in0))

    def token_group(width, evac, take=None):
        chunks = []
        for i in range(0, 8, 2):
            k = next_chunk()
            for ii in range(2):
                for t in range(NT):
                    p = i + ii
                    if p == 7:
                        continue
                    tok = mm3(banks[t].ap[:, 0:width], AH[:, p, 128 * t:128 * t + 128], AL[:, p, 128 * t:128 * t + 128],
                              k.hi[:, width * ii:width * ii + width], k.lo[:, width * ii:width * ii + width], p == 0,
                              False, k.ready, banks[t].free if p == 0 else None, col_ready[t], inc=(t == NT - 1))
            if i < 6:
                chunk_done(k, tok)
        for t in range(NT):
            tok = mm3(banks[t].ap[:, 0:width], AH[:, 7, 128 * t:128 * t + 128], AL[:, 7, 128 * t:128 * t + 128],
                      k.hi[:, width:2 * width], k.lo[:, width:2 * width], False, True, inc=True)
            if t == NT - 1:
                chunk_done(k, tok)
            banks[t].free = flatten(evac(t, banks[t], tok))
        return tok

    t_cv, t_fv = {}, {}

    def fvcv_out(t, b, tok):
        t_fv[t] = act(fv[:, t, :], b.ap[:, 0:256], ACT.Copy, tok, in1)
        t_cv[t] = act(cv[:, t, :], b.ap[:, 256:512], ACT.Copy, tok, in1)
        return [t_cv[t]]

    token_group(512, fvcv_out)
    bank_turn[0] = 0

    def heads_attention(kind, q, k, v, nh, dv, width, p_ring, pt_ring, o_ring, finish, t_q, t_k, t_v, began):
        steps = [(i, h) for i in range(NT) for h in range(nh)]
        st, rows = {}, {}
        pairs = [(0, 1), (2, 3)]
        tb = Ring([banks[4], banks[5]])

        def sc(x):
            i, h = steps[x]
            a, b = width(i)
            W = b - a
            p = pairs[x % 2]
            for w in range(0, W, 512):
                n = min(512, W - w)
                bk = banks[p[w // 512]]
                t_m = mm(bk.ap[:, 0:n], q(h, i), k(h, a + w, a + w + n), True, True, t_q, t_k, banks[p[0]].free,
                         banks[p[1]].free, inc=True)
            st[x] = {"W": W, "t": t_m, "ap": PF[:, 512 * p[0]:512 * p[0] + W]}

        def so(x):
            i, h = steps[x]
            d, pr = st[x], p_ring[x % 2]
            W, ap, p = d["W"], d["ap"], pairs[x % 2]
            if h == 0:
                rows[i] = col(nh)
            nm = col()
            dst = pr.ap[:, 0:W]
            src = ap
            if kind == "chunk":
                mx = col()
                t_x = DV.put(lambda e: e.tensor_tensor_reduce(out=dst, in0=ap, in1=b2[:, h, 640 - W:640], scale=1.0,
                                                              scalar=NEG, op0=ALU.add, op1=ALU.max, accum_out=mx),
                             d["t"], t_b2m, pr.free)
                banks[p[0]].free = banks[p[1]].free = [t_x]
                t_n = ts(nm, mx, -1.0, None, ALU.mult, None, t_x)
                src = dst
            else:
                t_m = d["t"]
                if kind == "mla":
                    t_m = DV.put(lambda e: e.memset(ap[0:64, W - 64:W], NEG), d["t"])
                elif kind == "fox":
                    t_m = tt(ap[:, W - 128:W], ap[:, W - 128:W], causal[:, :], ALU.add, d["t"], t_causal)
                t_n = DV.put(lambda e: e.tensor_reduce(nm, ap, AX.X, ALU.max, negate=True), t_m)
            rs = rows[i][:, h:h + 1]
            d["p"] = act(dst, src, ACT.Exp, t_n, pr.free, bias=nm, accum_out=rs)
            if kind != "chunk":
                banks[p[0]].free = banks[p[1]].free = [d["p"]]

        def tu(x):
            d, pr, pt = st[x], p_ring[x % 2], pt_ring[x % 2]
            nb = d["W"] // 128
            made = []
            for g in range(0, nb, 4):
                w = min(4, nb - g)
                b = tb.take()
                for j in range(w):
                    t_m = tr(b.ap[:, 128 * j:128 * j + 128], pr.ap[:, 128 * (g + j):128 * (g + j) + 128], d["p"], b.free,
                             inc=(j == w - 1))
                o, v_ = pt.ap[:, g:g + w, :], b.ap[:, 0:128 * w].rearrange("p (k c) -> p k c", c=128)
                t_c = cp(o, v_, t_m, pt.free) if (x + g // 4) % 2 else act(o, v_, ACT.Copy, t_m, pt.free)
                b.free = [t_c]
                made.append(t_c)
            pr.free = [t_m]
            d["pt"] = made

        def va(x):
            i, h = steps[x]
            d, pt, ob = st[x], pt_ring[x % 2], banks[6]
            a, b = width(i)
            nb = d["W"] // 128
            for kb in range(nb):
                t_m = mm(ob.ap[:, dv * h:dv * h + dv], pt.ap[:, kb, :], v(h, a // 128 + kb), kb == 0, kb == nb - 1,
                         d["pt"], t_v, ob.free if h == 0 else None, inc=(kb == nb - 1))
            pt.free = [t_m]
            if h == nh - 1:
                rden = col(nh)
                o = o_ring[i % 2]
                t_r = DV.put(lambda e: e.reciprocal(rden, rows[i]), [st[y]["p"] for y in range(x - nh + 1, x + 1)])
                t_o = tt(o.ap[:, :].rearrange("p (h d) -> p h d", h=nh),
                         ob.ap[:, 0:nh * dv].rearrange("p (h d) -> p h d", h=nh),
                         rden.unsqueeze(2).to_broadcast([128, nh, dv]), ALU.mult, t_r, t_m, o.free)
                ob.free = [t_o]
                finish(i, o, t_o, x)

        for r in (p_ring, pt_ring, o_ring):
            for pl in r:
                pl.free = list(began)
        attention(steps, sc, so, tu, va)

    def group_norm(o, n, g0, junk, t_o, *waits):
        s, v = col(), col()
        t_s = act(junk, o, ACT.Square, t_o, *waits, accum_out=s)
        t_v = ts(v, s, 1.0 / n, EPS, ALU.mult, ALU.add, t_s)
        r, t_r = inv_sqrt(v, t_v)
        return r, t_r

    in2 = mark()
    t_yc = {}

    def chunk_finish(i, o, t_o, x):
        r, t_r = group_norm(o.ap[:, :], 256, 768, yc[:, i, :], t_o, in2)
        t_yc[i] = stt(yc[:, i, :], o.ap[:, :], r, gout[:, 768:1024], ALU.mult, ALU.mult, t_r, t_gout)
        o.free = [t_yc[i]]

    heads_attention("chunk", lambda h, i: cq[:, h // 2, 128 * i:128 * i + 128], lambda h, a, b: ckp[:, h, a:b],
                    lambda h, kb: cv[:, kb, 64 * h:64 * h + 64], 4, 64,
                    lambda i: (max(0, 128 * i - 512), 128 * i + 128), s2, pt2, o2, chunk_finish,
                    t_cq, [t_ck, t_ckz], [t_cv[t] for t in range(NT)], in2)
    bank_turn[0] = 0

    in3 = mark()
    t_fz = []
    for h in range(4):
        z = 64 * (1 - h % 2)
        for dst in (fqp, fkp):
            t0 = DV.put(lambda e, dst=dst, z=z, h=h: e.memset(dst[z:z + 64, h, :], 0.0), in3)
            t_fz.append(DV.put(lambda e, dst=dst, z=z, h=h: e.memset(dst[z:z + 2, h, :], 1.0), t0))
    t_fq, t_fk = [], []
    for m in range(2):
        feature_tile(pair_out(fqp, m, t_fq, 0.125, in3))
    for m in range(2):
        feature_tile(pair_out(fkp, m, t_fk, 1.0, in3))

    tt_ring = [Place(big(f"tt_{i}", [128, 512], 56 + 2 * i)) for i in range(2)]
    ropek = big("ropek", [128, 8, 64], 60)
    gq = big("gq", [128, 384], 86)
    fl = big("fl", [4, 1024], 0)
    t_rk = l_mem.start(SP, ropek[:, :, :], I["c_ropek"], in3)
    t_rk = l_mem.start(SP, gq[:, 0:256], I["q_norm_2"][0].partition_broadcast(128), in3)
    t_rk = l_mem.start(SP, gq[:, 256:384], I["kv_norm_2"][0].partition_broadcast(128), in3)
    t_ttz = [DV.put(lambda e, i=i: e.memset(tt_ring[i].ap[:, 384:512], 0.0), in3) for i in range(2)]
    ra = big("ra", [128, 2, 32], 87.5)
    t_narrow = {}
    lat = []

    def narrow_out(t, b, tok):
        T = tt_ring[t % 2]
        w = [T.free, in3, t_ttz]
        res = []
        sq = col(2)
        v = col(2)
        t_s = act(T.ap[:, 0:256], b.ap[:, 0:256], ACT.Square, tok, w, accum_out=sq[:, 0:1])
        t_s2 = act(T.ap[:, 256:384], b.ap[:, 256:384], ACT.Square, tok, w, accum_out=sq[:, 1:2])
        t_a = ts(v[:, 0:1], sq[:, 0:1], 1.0 / 256, EPS, ALU.mult, ALU.add, t_s)
        t_b = ts(v[:, 1:2], sq[:, 1:2], 1.0 / 128, EPS, ALU.mult, ALU.add, t_s2)
        r, t_r = inv_sqrt(v, t_a, t_b)
        x12 = b.ap[:, 384:416]
        ta = tt(ra[:, 0, :], x12, ropek[:, t, 0:32], ALU.mult, tok, t_s2, t_rk, in3, DV.last())
        tb1 = tt(ra[:, 1, 0:16], b.ap[:, 400:416], ropek[:, t, 32:48], ALU.mult, DV.last())
        tb2 = tt(ra[:, 1, 16:32], b.ap[:, 384:400], ropek[:, t, 48:64], ALU.mult, DV.last())
        tf = cp(T.ap[:, 384:388], b.ap[:, 416:420], w)
        t1 = tt(T.ap[:, 448:480], ra[:, 0, :], ra[:, 1, :], ALU.add, ta, tb1, tb2, w)
        t2 = stt(T.ap[:, 0:256], b.ap[:, 0:256], r[:, 0:1], gq[:, 0:256], ALU.mult, ALU.mult, t_r, t_rk)
        t3 = stt(T.ap[:, 256:384], b.ap[:, 256:384], r[:, 1:2], gq[:, 256:384], ALU.mult, ALU.mult)
        t_narrow[t] = [tf, t1, t2, t3]

        def turn():
            b2_ = banks[t]
            for j in range(4):
                t_m = tr(b2_.ap[:, 128 * j:128 * j + 128], T.ap[:, 128 * j:128 * j + 128], t_narrow[t], b2_.free,
                         inc=(j == 3))
            T.free = [t_m]
            cs = slice(128 * t, 128 * t + 128)
            vv = b2_.ap[:, 0:384].rearrange("p (k c) -> p k c", k=3)
            t_hi = act(CH[:, :, cs], vv, ACT.Copy, t_m, in3)
            t_k = act(kpe[64:96, cs], b2_.ap[64:96, 384:512], ACT.Copy, t_m, in3)
            t_f = act(fl[0:4, cs], b2_.ap[0:4, 384:512], ACT.Copy, t_m, in3)
            t_lo = tt(CL[:, :, cs], vv, CH[:, :, cs].bitcast(F32), ALU.subtract, t_hi, t_f, in3)
            b2_.free = [t_lo]
            lat.append((t_hi, t_lo, t_k, t_f))

        turns.append(turn)
        if len(turns) >= 2:
            turns.pop(0)()
        return [t3]

    turns = []
    tok = token_group(420, narrow_out)
    while turns:
        turns.pop(0)()
    all_cols_read(tok)
    bank_turn[0] = 0
    for t in range(NT):
        col_ready[t] = []
    for t in range(NT):
        t_m = turn_in(yc[:, t, :], 2, t, 6, t_yc[t])

    in4 = mark()
    fbias = small("fbias", 1)
    t_fb = l_mem.start(SP, fbias[0:4, :], I["f_bias_2"][0].rearrange("(n a) -> n a", a=1), in3)
    z0 = big("z0", [4, 1024], 60)
    z1 = big("z1", [4, 1024], 56)
    z2 = big("z2", [4, 1024], 64)
    t1 = ts(z0[:, :], fl[:, :], fbias[0:4, 0:1], None, ALU.add, None, in4, t_fb)
    t2 = stt(z1[:, :], z0[:, :], -1.0, z0[:, :], ALU.mult, ALU.max, t1, in4)
    t3 = act(z1[:, :], z1[:, :], ACT.Exp, t2, scale=-1.0)
    t4 = act(z1[:, :], z1[:, :], ACT.Ln, t3, bias=1.0)
    t5 = stt(z0[:, :], z0[:, :], 0.0, z1[:, :], ALU.min, ALU.subtract, t4)
    t6 = DV.put(lambda e: e.memset(z1[:, :], 1.0), t5)
    t7 = DV.put(lambda e: e.tensor_tensor_scan(z2[:, :], z1[:, :], z0[:, :], 0.0, ALU.mult, ALU.add), t6, in4)
    t8 = ts(z0[:, :], z2[:, :], -1.0, None, ALU.mult, None, t7)
    for h in range(4):
        z = 64 * (1 - h % 2)
        l_aug.start(SP, fqp[z + 1:z + 2, h, :], z2[h:h + 1, :], t8, t_fz)
        t_aug = l_aug.start(SP, fkp[z:z + 1, h, :], z0[h:h + 1, :], t8, t_fz)
    causal = big("causal", [128, 128], 87)
    t_causal = l_mem.start(SP, causal[:, :], I["c_causal"], in4)

    p3 = [Place(big("p3_0", [128, 1024], 56)), Place(big("p3_1", [128, 1024], 60))]
    pt3 = [Place(big("pt3_0", [128, 8, 128], 64)), Place(big("pt3_1", [128, 8, 128], 0))]
    o3 = [Place(big(f"o3_{i}", [128, 256], 68 + i)) for i in range(2)]
    in5 = mark() + [t_aug]

    def fox_finish(i, o, t_o, x):
        sq = SQ[i % 2]
        r, t_r = group_norm(o.ap[:, :], 256, 512, sq.ap[:, 0:256], t_o, sq.free)
        t_y = stt(o.ap[:, :], o.ap[:, :], r, gout[:, 512:768], ALU.mult, ALU.mult, t_r, t_gout)
        sq.free = [t_r]

        def turn_y():
            bank_turn[0] = 7
            o.free = [turn_in(o.ap, 2, i, 4, t_y)]
        later.append((x + 4, turn_y))

    SQ = [Place(stage_sq) for stage_sq in (big("sq0", [128, 128], 86), big("sq1", [128, 128], 86.5))]
    SQ = [Place(big("sqj0", [128, 256], 86)), Place(big("sqj1", [128, 256], 86))]
    heads_attention("fox", lambda h, i: fqp[:, h, 128 * i:128 * i + 128], lambda h, a, b: fkp[:, h, a:b],
                    lambda h, kb: fv[:, kb, 64 * h:64 * h + 64], 4, 64, lambda i: (0, 128 * i + 128),
                    p3, pt3, o3, fox_finish, [t_fq, t_fz, t_aug], [t_fk], [t_fv[t] for t in range(NT)], in5)
    bank_turn[0] = 0

    in6 = mark()
    mq = big("mq", [128, 4, 1024], 56)
    mk = big("mk", [128, 4, 1024], 72)
    mv_ = big("mv", [128, 8, 512], 8)
    ropeq = big("ropeq", [128, 1024], 0)
    rtmp = big("rtmp", [128, 512], 24)
    t_rq = l_mem.start(SP, ropeq[64:128, :], I["c_ropeq"], in6)
    lat_t = flatten([list(x) for x in lat])
    MS = 96 ** -0.5
    t_mz = [DV.put(lambda e: e.memset(mk[96:128, :, :], 0.0), in6), DV.put(lambda e: e.memset(mq[96:128, :, :], 0.0), in6)]
    for h in range(4):
        t_mz.append(cp(mk[64:96, h, :], kpe[64:96, :], lat_t, in6))
    t_mq, t_mk, t_mv = [], [], []
    k = next_chunk()
    for h in range(4):
        for th in range(2):
            b = take_bank()
            cs = slice(512 * th, 512 * th + 512)
            tok = feature_unit(k, lambda i: (k.hi[:, 512 * i + 128 * h:512 * i + 128 * h + 128],
                                             k.lo[:, 512 * i + 128 * h:512 * i + 128 * h + 128]), 2,
                               lambda i: (CH[:, i, cs], CL[:, i, cs]), th, b, lat_t)
            t0 = act(mq[0:64, h, cs], b.ap[0:64, :], ACT.Copy, tok, in6, scale=MS)
            t1 = stt(mq[64:96, h, cs], b.ap[64:96, :], MS, ropeq[64:96, cs], ALU.mult, ALU.mult, tok, t0, t_rq, in6)
            t2 = stt(rtmp[64:96, :], b.ap[96:128, :], MS, ropeq[96:128, cs], ALU.mult, ALU.mult, t1)
            t3 = tt(mq[64:96, h, cs], mq[64:96, h, cs], rtmp[64:96, :], ALU.add, t1, t2)
            b.free = [t2]
            t_mq += [t0, t3]
    chunk_done(k, tok)
    k = next_chunk()
    for h in range(4):
        for th in range(2):
            b = take_bank()
            cs = slice(512 * th, 512 * th + 512)
            tok = feature_unit(k, lambda i: (k.hi[:, 192 * h:192 * h + 128], k.lo[:, 192 * h:192 * h + 128]), 1,
                               lambda i: (CH[:, 2, cs], CL[:, 2, cs]), th, b, lat_t)
            t0 = act(mk[0:64, h, cs], b.ap[0:64, :], ACT.Copy, tok, in6)
            b.free = [t0]
            t_mk.append(t0)
    vh = k.hi[:, 0:768].rearrange("p (h c) -> p h c", h=4)[:, :, 64:192]
    vl = k.lo[:, 0:768].rearrange("p (h c) -> p h c", h=4)[:, :, 64:192]
    for t in range(NT):
        b = take_bank()
        cs = slice(128 * t, 128 * t + 128)
        tok = mm3(b.ap.rearrange("p (h c) -> p h c", h=4), CH[:, 2, cs], CL[:, 2, cs], vh, vl, True, True, b.free,
                  k.ready, lat_t, inc=True)
        t0 = cp(mv_[:, t, :], b.ap, tok, in6)
        b.free = [t0]
        t_mv.append(t0)
    chunk_done(k, tok)
    in7 = mark()
    p4 = [Place(big(f"p4_{i}", [128, 1024], 24 + 4 * i)) for i in range(2)]
    pt4 = [Place(big(f"pt4_{i}", [128, 8, 128], 32 + 4 * i)) for i in range(2)]
    o4 = [Place(big(f"o4_{i}", [128, 512], 40 + 2 * i)) for i in range(2)]
    SQ4 = [Place(big("sq4_0", [128, 512], 44)), Place(big("sq4_1", [128, 512], 46))]
    for q_ in SQ4:
        q_.free = list(in7)

    def mla_finish(i, o, t_o, x):
        sq = SQ4[i % 2]
        r, t_r = group_norm(o.ap[:, :], 512, 0, sq.ap[:, :], t_o, sq.free)
        t_y = stt(o.ap[:, :], o.ap[:, :], r, gout[:, 0:512], ALU.mult, ALU.mult, t_r, t_gout)
        sq.free = [t_r]

        def turn_y():
            bank_turn[0] = 7
            o.free = [turn_in(o.ap, 4, i, 0, t_y)]
        later.append((x + 4, turn_y))

    heads_attention("mla", lambda h, i: mq[:, h, 128 * i:128 * i + 128], lambda h, a, b: mk[:, h, a:b],
                    lambda h, kb: mv_[:, kb, 128 * h:128 * h + 128], 4, 128, lambda i: (0, 128 * i + 128),
                    p4, pt4, o4, mla_finish, [t_mq, t_mz], [t_mk, t_mz], t_mv, in7)
    bank_turn[0] = 0

    stored = lambda: l_h[0].last() + l_h[1].last()
    pas = Passage(h2, None, I["norm_cross_2"][0], h3, after=mark() + stored())
    token_stage(eight, lambda j, p: p, lambda j, p, t: col_ready[t], pas)

    xq = big("xq", [128, 4, 1024], 16)
    MH = big("mh", [128, 8, 256], 32, F32R)
    ML = big("ml", [128, 8, 256], 40, F32R)
    xk = big("xk", [128, 4, 256], 48)
    xv = big("xv", [128, 2, 512], 52)
    in8 = mark()
    t_xq = []

    def xq_out(m):
        def go(th, b, tok):
            t_xq.append(act(xq[:, m, 512 * th:512 * th + 512], b.ap, ACT.Copy, tok, in8, scale=128 ** -0.5))
            return [t_xq[-1]]
        return go

    for m in range(4):
        tok = feature_tile(xq_out(m))
        if m == 0:
            in9 = mark() + stored()
            memx = [big(f"memx{i}", [128, 1024], 60 + 4 * i) for i in range(2)]
            gmem = big("gmem", [128, 1024], 68)
            memn = [big(f"memn{i}", [128, 1024], 72 + 4 * i) for i in range(2)]
            t_g = l_mem.start(SP, gmem[:, :], I["norm_mem_2"][0].partition_broadcast(128), in9)
            for i in range(2):
                t_g = l_mem.start(SP, memx[i][:, :], I["mem_2"][0][128 * i:128 * i + 128, :], in9)
            t_mh = []
            mem_turn = []
            for i in range(2):
                s, v = col(), col()
                t_s = act(memn[i][:, :], memx[i][:, :], ACT.Square, t_g, in9, accum_out=s)
                t_v = ts(v, s, 1.0 / D, EPS, ALU.mult, ALU.add, t_s)
                r, t_r = inv_sqrt(v, t_v)
                t_n = stt(memn[i][:, :], memx[i][:, :], r, gmem[:, :], ALU.mult, ALU.mult, t_r)
                mem_turn.append((i, t_n))
        if m == 1:
            for i, t_n in mem_turn:
                for g in range(2):
                    b = take_bank()
                    for j in range(4):
                        kk = 4 * g + j
                        t_m = tr(b.ap[:, 128 * j:128 * j + 128], memn[i][:, 128 * kk:128 * kk + 128], t_n, b.free,
                                 inc=(j == 3))
                    t_mh += split_in(b, 4, MH[:, 4 * g:4 * g + 4, 128 * i:128 * i + 128],
                                     ML[:, 4 * g:4 * g + 4, 128 * i:128 * i + 128], t_m, in8)
    all_cols_read(tok)
    t_xk, t_xv = [], []
    for m in range(4):
        k = next_chunk()
        b = take_bank()
        for i in range(8):
            tok = mm3(b.ap[:, 0:256], k.hi[:, 128 * i:128 * i + 128], k.lo[:, 128 * i:128 * i + 128], MH[:, i, :],
                      ML[:, i, :], i == 0, i == 7, k.ready, b.free, t_mh, inc=(i == 7))
        t0 = act(xk[:, m, :], b.ap[:, 0:256], ACT.Copy, tok, in8)
        b.free = [t0]
        t_xk.append(t0)
        chunk_done(k, tok)
    vb = [take_bank(), take_bank()]
    for i in range(0, 8, 2):
        k = next_chunk()
        for ii in range(2):
            for t in range(2):
                tok = mm3(vb[t].ap, MH[:, i + ii, 128 * t:128 * t + 128], ML[:, i + ii, 128 * t:128 * t + 128],
                          k.hi[:, 512 * ii:512 * ii + 512], k.lo[:, 512 * ii:512 * ii + 512], i + ii == 0, i + ii == 7,
                          k.ready, vb[t].free, inc=(t == 1))
        chunk_done(k, tok)
    for t in range(2):
        t0 = cp(xv[:, t, :], vb[t].ap, tok, in8)
        vb[t].free = [t0]
        t_xv.append(t0)

    in10 = mark()
    p5 = [Place(big(f"p5_{i}", [128, 256], i)) for i in range(2)]
    pt5 = [Place(big(f"pt5_{i}", [128, 2, 128], 2 + i)) for i in range(2)]
    o5 = [Place(big(f"o5_{i}", [128, 512], 4 + 2 * i)) for i in range(2)]

    def cross_finish(i, o, t_o, x):
        def turn_y():
            bank_turn[0] = 7
            col_ready[i] = []
            o.free = [turn_in(o.ap, 4, i, 0, t_o)]
        later.append((x + 3, turn_y))

    heads_attention("cross", lambda h, i: xq[:, h, 128 * i:128 * i + 128], lambda h, a, b: xk[:, h, a:b],
                    lambda h, kb: xv[:, kb, 128 * h:128 * h + 128], 4, 128, lambda i: (0, 256),
                    p5, pt5, o5, cross_finish, t_xq, t_xk, t_xv, in10)
    bank_turn[0] = 0

    pas = Passage(h3, None, I["norm_ffn_2"][0], h4, after=mark() + stored())
    token_stage([list(range(4))] * 2, lambda j, p: p, lambda j, p, t: col_ready[t], pas)
    ffn(h4, None, I["final_norm_2"], None, final=True)

    for l in l_out + l_h + l_sk:
        for token in l.last():
            SP.items.append(([token], None, False))

    block = ctx.enter_context(nc.Block())

    @block.tensor
    def _(e):
        PE.run(e)

    @block.scalar
    def _(e):
        AC.run(e)

    @block.vector
    def _(e):
        DV.run(e)

    @block.gpsimd
    def _(e):
        PL.run(e)

    @block.sync
    def _(e):
        for need, fn, inc in SP.items:
            for s_, value in need:
                e.wait_ge(s_, value)
            if fn is not None:
                fn(e)


_INS = ["x", "mix_pre_g", "mix_post_g", "ffn_pre_g", "ffn_post_g", "w_in", "conv_dw", "conv_dw_b", "conv_ln_g",
        "conv_ln_b", "w_conv_pw", "attn_sinks", "rel_bias", "w_out", "w_gate", "w_up", "w_down", "mem_2",
        "norm_mix_2", "w_in_2", "q_norm_2", "w_uq_2", "kv_norm_2", "w_ukv_2", "f_bias_2", "rel_bias_2", "out_norm_2",
        "w_o_2", "norm_cross_2", "norm_mem_2", "w_cq_2", "w_ckv_2", "w_co_2", "norm_ffn_2", "w_gu_2", "w_down_2",
        "final_norm_2"]


def kernel(**inputs):
    import numpy as _np
    import concourse.bacc as _bacc
    from concourse import mybir as _mybir
    from concourse.bass_utils import run_bass_kernel_spmd as _run

    nc = _bacc.Bacc("TRN2", target_bir_lowering=False, num_devices=1)
    arrays, args = {}, {}
    given = {name: _np.ascontiguousarray(inputs[name]) for name in _INS}
    given["x"] = given["x"].reshape(1024, 1024)
    given.update(constants())
    for name, a in given.items():
        arrays[f"in_{name}_dram"] = a
        args[name] = nc.dram_tensor(f"in_{name}_dram", a.shape, _mybir.dt.from_np(a.dtype), kind="ExternalInput").ap()
    out = nc.dram_tensor("out_0_dram", (1024, 1024), _mybir.dt.float32, kind="ExternalOutput").ap()
    block_kernel(nc, args, out)
    r = _run(nc, [arrays], core_ids=[0])
    return r.results[0]["out_0_dram"].reshape(1, 1024, 1024)
```

```python
import math
from contextlib import ExitStack

import numpy as np

import concourse.bass as bass
from concourse import mybir

F32 = mybir.dt.float32
F32R = mybir.dt.float32r
ACT = mybir.ActivationFunctionType
ALU = mybir.AluOpType
AX = mybir.AxisListType

S = 1024
D = 1024
NT = 8
FF = 2816
NF = FF // 128
EPS = 1e-6
NEG = -1e30
TAPS = 31
KB = 1024


class Queue:

    def __init__(self, sem):
        self.sem, self.items, self.count, self.met, self.own = sem, [], 0, {}, 0

    def put(self, fn, *waits, inc=True, stream=False):
        need = {}
        for sem, value in flat(waits):
            if self.met.get(sem.name, 0) < value:
                self.met[sem.name] = value
                need[sem.name] = (sem, value)
        if inc:
            self.count += 1
        if not stream:
            self.own = self.count
        self.items.append((list(need.values()), fn, inc))
        return (self.sem, self.count) if inc else None

    def last(self):
        return [(self.sem, self.own)] if self.own else []

    def run(self, eng):
        for need, fn, inc in self.items:
            for sem, value in need:
                eng.wait_ge(sem, value)
            ins = fn(eng)
            if inc:
                ins.then_inc(self.sem, 1)


class Landing:

    def __init__(self, sem):
        self.sem, self.count = sem, 0

    def start(self, queue, out, in_, *waits, **how):
        self.count += 16
        sem = self.sem
        queue.put(lambda e: e.dma_start(out, in_, **how).then_inc(sem, 16), *waits, inc=False)
        return (sem, self.count)

    def last(self):
        return [(self.sem, self.count)] if self.count else []


class Place:

    def __init__(self, ap, index=0):
        self.ap, self.index, self.free = ap, index, []


class Ring:
    def __init__(self, places):
        self.places, self.n = places, 0

    def take(self):
        self.n += 1
        return self.places[(self.n - 1) % len(self.places)]


def flat(tokens):
    for t in tokens:
        if t is None:
            continue
        if isinstance(t, tuple) and not isinstance(t[0], (tuple, list)):
            yield t
        else:
            yield from flat(t)


def bucket_of(dist):
    d = np.maximum(dist, 1).astype(np.float32)
    large = 16 + (np.log(d / np.float32(16)) / np.float32(math.log(8.0)) * np.float32(16)).astype(np.int32)
    return np.where(dist < 16, dist, np.minimum(large, 31))


def constants():
    ident = np.eye(128, dtype=np.float32)
    oh1 = np.zeros((33, 383), np.float32)
    for j in range(383):
        dist = 255 - j
        if 0 <= dist < 128:
            oh1[int(bucket_of(np.array([dist]))[0]), j] = 1.0
        else:
            oh1[32, j] = NEG
    oh2 = np.zeros((192, 767), np.float32)
    for j in range(767):
        oh2[min(max(639 - j, -63), 128) + 63, j] = 1.0
    q = np.arange(128)
    causal = np.where(q[None, :] <= q[:, None], 0.0, NEG).astype(np.float32)
    pos = np.arange(S, dtype=np.float32)
    inv = np.power(np.float32(10000.0), -np.arange(0, 32, 2, dtype=np.float32) / np.float32(32)).astype(np.float32)
    ang = (pos[:, None] * inv[None, :]).astype(np.float32)
    cos, sin = np.cos(ang).astype(np.float32), np.sin(ang).astype(np.float32)
    ropeq = np.concatenate([cos.T, cos.T, -sin.T, sin.T], 0)
    ropek = np.concatenate([cos, cos, -sin, sin], 1).reshape(NT, 128, 64).transpose(1, 0, 2)
    return {"c_ident": ident, "c_oh1": oh1, "c_oh2": oh2, "c_causal": causal,
            "c_ropeq": np.ascontiguousarray(ropeq), "c_ropek": np.ascontiguousarray(ropek)}


def block_kernel(nc, I, out):
    ctx = ExitStack()
    with ctx:
        build(nc, ctx, I, out)


def build(nc, ctx, I, out_dram):
    BASE = 16512
    RING = 5
    off = {"stage": BASE, "wh": BASE + 8 * KB, "wl": BASE + (8 + 4 * RING) * KB}
    off["ah"] = off["wl"] + 4 * RING * KB
    off["al"] = off["ah"] + 32 * KB
    off["sg"] = off["al"] + 32 * KB
    off["big"] = off["sg"] + 4 * KB
    off["small"] = off["big"] + 88 * KB
    BIG = off["big"]

    def sb(name, shape, at, dt=F32):
        return nc.alloc_sbuf_tensor_at(name, shape, dt, offset=at)

    def big(name, shape, kb, dt=F32):
        return sb(name, shape, BIG + int(kb * KB), dt)

    def sem(name):
        return ctx.enter_context(nc.semaphore(name))

    PE, AC, DV, PL, SP = (Queue(sem("s_" + n)) for n in ("pe", "act", "dve", "pool", "sp"))

    def mark():
        return PE.last() + AC.last() + DV.last() + PL.last()

    P = ctx.enter_context(nc.psum_tensor("P", [128, 8, 512], F32))
    PF = P[:, :, :].rearrange("p b n -> p (b n)")
    banks = [Place(P[:, i, :], i) for i in range(8)]
    bank_turn = [0]

    def take_bank():
        b = banks[bank_turn[0] % 8]
        bank_turn[0] += 1
        return b

    stage = [sb(f"stage{i}", [128, 1024], off["stage"] + 4 * KB * i) for i in range(2)]
    WH = [sb(f"wh{i}", [128, 1024], off["wh"] + 4 * KB * i, F32R) for i in range(RING)]
    WL = [sb(f"wl{i}", [128, 1024], off["wl"] + 4 * KB * i, F32R) for i in range(RING)]
    AH = sb("ah", [128, 8, 1024], off["ah"], F32R)
    AL = sb("al", [128, 8, 1024], off["al"], F32R)
    sm = [off["small"]]

    def small(name, n):
        t = sb(name, [128, n], sm[0])
        sm[0] += 4 * n
        return t

    ident = small("ident", 128)
    nhalf = small("nhalf", 8)
    epsc = small("epsc", 8)
    sinks = small("sinks", 8)
    nsink = small("nsink", 8)
    stats = small("stats", 480)
    ra = small("ra", 64)[:, :].rearrange("p (a b) -> p a b", a=2)
    causal = small("causal", 128)
    stat_at = [0]

    def col(n=1):
        if stat_at[0] + n > 480:
            stat_at[0] = 0
        stat_at[0] += n
        return stats[:, stat_at[0] - n:stat_at[0]]

    l_const = Landing(sem("l_const"))
    l_stage = [Landing(sem(f"l_stage{i}")) for i in range(2)]
    l_xr = [Landing(sem(f"l_xr{i}")) for i in range(2)]
    l_gb = [Landing(sem(f"l_gb{i}")) for i in range(2)]
    l_h = [Landing(sem(f"l_h{i}")) for i in range(2)]
    l_bias = Landing(sem("l_bias"))
    l_sk = [Landing(sem(f"l_sk{i}")) for i in range(3)]
    l_aug = Landing(sem("l_aug"))
    l_out = [Landing(sem(f"l_out{i}")) for i in range(4)]
    l_misc = Landing(sem("l_misc"))
    l_mem = Landing(sem("l_mem"))

    h1 = nc.dram_tensor("h1", (S, D), F32, kind="Internal").ap()
    h2 = nc.dram_tensor("h2", (S, D), F32, kind="Internal").ap()
    h3 = nc.dram_tensor("h3", (S, D), F32, kind="Internal").ap()
    h4 = nc.dram_tensor("h4", (S, D), F32, kind="Internal").ap()
    sk1 = nc.dram_tensor("sk1", (8, 128 * 384), F32, kind="Internal")
    sk2 = nc.dram_tensor("sk2", (4, 128 * 768), F32, kind="Internal")

    t_ident = l_const.start(SP, ident[:, :], I["c_ident"])
    t_eps = DV.put(lambda e: e.memset(epsc[:, :], EPS))
    t_nhalf = DV.put(lambda e: e.memset(nhalf[:, :], -0.5))

    def mm(out, l, r, start, stop, *waits, inc=False):
        return PE.put(lambda e: e.matmul(out, l, r, start=start, stop=stop), *waits, inc=inc)

    def mm3(out, lh, ll, rh, rl, start, stop, *waits, inc=False):
        mm(out, lh, rh, start, False, *waits)
        mm(out, lh, rl, False, False)
        return mm(out, ll, rh, False, stop, inc=inc)

    def tr(out, in_, *waits, inc=False):
        p = in_.shape[0]
        return PE.put(lambda e: e.transpose(out, in_, ident[0:p, 0:p]), t_ident, *waits, inc=inc)

    def act(out, in_, func, *waits, **kw):
        return AC.put(lambda e: e.activation(out, in_, func, **kw), *waits)

    def tt(out, a, b, op, *waits):
        return DV.put(lambda e: e.tensor_tensor(out, a, b, op), *waits)

    def ts(out, a, s1, s2, op0, op1, *waits):
        if op1 is None:
            return DV.put(lambda e: e.tensor_scalar(out, a, s1, None, op0), *waits)
        return DV.put(lambda e: e.tensor_scalar(out, a, s1, s2, op0, op1), *waits)

    def stt(out, a, s, b, op0, op1, *waits):
        return DV.put(lambda e: e.scalar_tensor_tensor(out, a, s, b, op0, op1), *waits)

    def cp(out, in_, *waits):
        return DV.put(lambda e: e.tensor_copy(out, in_), *waits)

    def inv_sqrt(v, *waits):
        r = col(v.shape[1])
        n = v.shape[1]
        return r, PL.put(lambda e: e.tensor_tensor(r, v, nhalf[:, 0:n], ALU.pow), t_nhalf, *waits)

    def inv_rms(s, more, *waits):
        r, v = col(), col()
        t_v = PL.put(lambda e: e.tensor_tensor(v, s, more, ALU.add), t_eps, *waits)
        return r, PL.put(lambda e: e.tensor_tensor(r, v, nhalf[:, 0:1], ALU.pow), t_nhalf, t_v)

    RT = D ** -0.5

    plan = []
    sent = [0]
    used = [0]
    w_slots = [Place(None, i) for i in range(RING)]
    s_slots = [Place(stage[i], i) for i in range(2)]
    ready = {}

    landed = {}
    narrow_pool = []

    def load_chunk():
        c = len(landed)
        if c < len(plan):
            st = s_slots[c % 2]
            for dst, src in plan[c][1]:
                landed[c] = l_stage[c % 2].start(SP, dst(st.ap), src, st.free)

    def send_chunk():
        c = sent[0]
        sent[0] += 1
        n = plan[c][0]
        st, sl = s_slots[c % 2], w_slots[c % RING]
        i = sl.index
        t_hi = AC.put(lambda e: e.activation(WH[i][:, 0:n], st.ap[:, 0:n], ACT.Copy), landed[c], sl.free, stream=True)
        t_lo = PL.put(lambda e: e.tensor_tensor(WL[i][:, 0:n], st.ap[:, 0:n], WH[i][:, 0:n].bitcast(F32), ALU.subtract),
                      landed[c], t_hi, sl.free, narrow_pool, stream=True)
        st.free = [t_hi, t_lo]
        ready[c] = [t_hi, t_lo]
        load_chunk()

    class Chunk:
        pass

    def next_chunk():
        c = used[0]
        used[0] += 1
        while sent[0] <= c:
            send_chunk()
        k = Chunk()
        k.slot = w_slots[c % RING]
        k.hi, k.lo, k.ready = WH[c % RING], WL[c % RING], ready.pop(c)
        return k

    done = [0]

    def run_ahead(most=1, margin=0):
        while most and sent[0] < min(done[0] + RING - margin, len(plan)):
            send_chunk()
            most -= 1

    def chunk_done(k, token):
        k.slot.free = [token]
        done[0] += 1
        run_ahead(1, 1)

    def chunks_done(ks, token):
        for k in ks:
            k.slot.free = [token]
            done[0] += 1
        run_ahead(2)

    def cols_chunk(w, c0, nk=8, n=128):
        src = w[:, c0:c0 + n].rearrange("(k p) c -> p k c", p=128)
        return (nk * n, [(lambda s: s[:, 0:nk * n].rearrange("p (k c) -> p k c", k=nk), src)])

    def rows_chunk(w, ks, ranges):
        width = sum(b - a for a, b in ranges)
        parts = []
        for i, k in enumerate(ks):
            at = i * width
            for a, b in ranges:
                parts.append((lambda s, at=at, n=b - a: s[:, at:at + n], w[k * 128:(k + 1) * 128, a:b]))
                at += b - a
        return (len(ks) * width, parts)

    w_in, w_out, w_pw = I["w_in"], I["w_out"], I["w_conv_pw"]
    w_in2, w_uq, w_ukv, w_o = I["w_in_2"][0], I["w_uq_2"][0], I["w_ukv_2"][0], I["w_o_2"][0]
    w_cq, w_ckv, w_co, w_gu = I["w_cq_2"][0], I["w_ckv_2"][0], I["w_co_2"][0], I["w_gu_2"][0]

    for c in range(4):
        plan.append(cols_chunk(w_in, 1280 + 128 * c))
        plan.append(cols_chunk(w_in, 768 + 128 * c))
    for c0 in (512, 640, 0, 128, 256, 384):
        plan.append(cols_chunk(w_in, c0))
    for m in range(4):
        plan.append(cols_chunk(w_pw, 128 * m, nk=4))

    def plan_tok(w, orders):
        for j, order in enumerate(orders):
            for i in range(0, len(order), 2):
                plan.append(rows_chunk(w, order[i:i + 2], [(512 * j, 512 * j + 512)]))

    down_order = [list(range(NF)), list(range(14, NF)) + list(range(14))]

    def plan_ffn(wg, g0, wu, u0, wd):
        for m in range(NF):
            plan.append(cols_chunk(wg, g0 + 128 * m))
            plan.append(cols_chunk(wu, u0 + 128 * m))
        plan_tok(wd, down_order)

    plan_tok(w_out, [list(range(8))] * 2)
    plan_ffn(I["w_gate"], 0, I["w_up"], 0, I["w_down"])
    for c0 in (1188, 1316, 1444, 1572):
        plan.append(cols_chunk(w_in2, c0))
    for i in range(0, 8, 2):
        plan.append(rows_chunk(w_in2, [i, i + 1], [(928, 1184), (1700, 1956)]))
    for i in range(0, 8, 2):
        plan.append(rows_chunk(w_in2, [i, i + 1], [(0, 416), (1184, 1188)]))
    for c0 in (416, 544, 672, 800):
        plan.append(cols_chunk(w_in2, c0))
    uq_parts = []
    for k in range(2):
        src = w_uq[k * 128:(k + 1) * 128, :].rearrange("p (h c) -> p h c", h=4)
        for a, b, at in ((0, 96, 0), (80, 96, 96), (64, 80, 112)):
            uq_parts.append((lambda s, k=k, at=at, n=b - a: s[:, 512 * k:512 * k + 512].rearrange(
                "p (h c) -> p h c", h=4)[:, :, at:at + n], src[:, :, a:b]))
    plan.append((1024, uq_parts))
    plan.append((768, [(lambda s: s[:, 0:768], w_ukv)]))
    plan_tok(w_o, [list(range(8))] * 2)
    for m in range(4):
        plan.append(cols_chunk(w_cq, 128 * m))
    for m in range(4):
        plan.append(cols_chunk(w_ckv, 128 * m))
    for i in range(0, 8, 2):
        plan.append(rows_chunk(w_ckv, [i, i + 1], [(512, 1024)]))
    plan_tok(w_co, [list(range(4))] * 2)
    plan_ffn(w_gu, 0, w_gu, FF, I["w_down_2"][0])

    col_ready = [[] for _ in range(NT)]
    col_free = [[] for _ in range(NT)]

    def turn_in(src, n, t, k0, *waits):
        made, last = [], None
        for g in range(0, n, 4):
            w = min(4, n - g)
            b = take_bank()
            for j in range(w):
                last = tr(b.ap[:, 128 * j:128 * j + 128], src[:, 128 * (g + j):128 * (g + j) + 128],
                          b.free, *waits, inc=(j == w - 1))
            made += split_in(b, w, AH[:, k0 + g:k0 + g + w, 128 * t:128 * t + 128],
                             AL[:, k0 + g:k0 + g + w, 128 * t:128 * t + 128], last, col_free[t])
        col_ready[t] = col_ready[t] + made
        return last

    def split_in(b, w, hi, lo, *waits):
        v = b.ap[:, 0:128 * w].rearrange("p (k c) -> p k c", k=w)
        t_hi = act(hi, v, ACT.Copy, *waits)
        t_lo = tt(lo, v, hi.bitcast(F32), ALU.subtract, t_hi, *waits)
        b.free = [t_lo]
        return [t_hi, t_lo]

    pending = []

    def flush():
        while pending:
            pending.pop(0)()

    def feature_unit(k, lhs, nk, rhs, th, b, *waits):
        for i in range(nk):
            lh, ll = lhs(i)
            rh, rl = rhs(i)
            tok = mm3(b.ap, lh, ll, rh, rl, i == 0, i == nk - 1, k.ready, b.free, *waits, inc=(i == nk - 1))
        return tok

    def act_cols(th, nk=8):
        return lambda i: (AH[:, i, 512 * th:512 * th + 512], AL[:, i, 512 * th:512 * th + 512])

    def flatten(tokens):
        return list(flat([tokens]))

    def feature_group(evacs, between=None):
        ks = [next_chunk() for _ in evacs]
        for th in range(2):
            if th == 1:
                flush()
                run_ahead()
            for k, evac in zip(ks, evacs):
                v = lambda i, k=k: (k.hi[:, 128 * i:128 * i + 128], k.lo[:, 128 * i:128 * i + 128])
                b = take_bank()
                half = range(4 * th, 4 * th + 4)
                tok = feature_unit(k, v, 8, act_cols(th), th, b, [col_ready[t] for t in half])
                for t in half:
                    col_free[t] = [tok]
                b.free = flatten(evac(th, b, tok))
                if th == 1:
                    chunk_done(k, tok)
                if between:
                    between()
        return tok

    M0 = [big(f"m0_{t}", [128, 512], 56 + 2 * t) for t in range(NT)]
    GB = [big(f"gb{i}", [128, 1024], 72 + 4 * i) for i in range(2)]
    XR = [Place(big(f"xr{i}", [128, 1024], 80 + 4 * i)) for i in range(2)]
    HT = [Place(big(f"ht{i}", [128, 1024], 4 * i)) for i in range(2)]
    XN = [Place(big(f"xn{i}", [128, 1024], at)) for i, at in enumerate((8, 12, 56, 60))]

    class Passage:

        def __init__(self, x, g_post, g_pre, h, final=False, after=(), xfree=()):
            self.x, self.h, self.final, self.g_post = x, h, final, g_post
            self.after = list(after)
            self.t_gb = [None, None]
            if g_post is not None:
                self.t_gb[0] = l_gb[0].start(SP, GB[0][:, :], g_post.partition_broadcast(128), self.after)
            self.t_gb[1] = l_gb[1].start(SP, GB[1][:, :], g_pre.partition_broadcast(128), self.after)
            for r in (XR, HT, XN):
                for p in r:
                    p.free = list(self.after)
            self.t_x, self.m0, self.ss0, self.r1, self.r2 = {}, {}, {}, {}, {}
            self.t_h, self.t_xn = {}, {}
            for t in range(2):
                self.load(t)

        def load(self, t):
            if t < NT:
                self.t_x[t] = l_xr[t % 2].start(SP, XR[t % 2].ap[:, :], self.x[128 * t:128 * t + 128, :], XR[t % 2].free)

        def keep(self, t, b, tok, *waits):
            t_m = cp(M0[t][:, :], b.ap, tok, self.after, *waits)
            b.free = [t_m]
            self.m0[t] = t_m
            if self.g_post is not None:
                s, v = col(), col()
                junk = HT[t % 2]
                t_s = act(junk.ap[:, 0:512], M0[t][:, :], ACT.Square, t_m, junk.free, scale=RT, accum_out=s)
                junk.free = [t_s]
                self.ss0[t] = (v, ts(v, s, EPS, None, ALU.add, None, t_s))

        def a(self, t, b, tok):
            self.tok = tok
            if self.g_post is None:
                return
            s = col()
            v0, t_v0 = self.ss0[t]
            j = XN[t % 4]
            t_s = act(j.ap[:, 0:512], b.ap, ACT.Square, tok, j.free, scale=RT, accum_out=s)
            self.r1[t] = inv_rms(s, v0, t_s, t_v0)

        def b(self, t, b, tok):
            H, X = HT[t % 2], XR[t % 2]
            h = H.ap
            if self.g_post is not None:
                r, t_r = self.r1[t]
                stt(h[:, 0:512], M0[t][:, :], r, GB[0][:, 0:512], ALU.mult, ALU.mult, t_r, self.t_gb[0], self.m0[t], H.free)
                t_u = stt(h[:, 512:], b.ap, r, GB[0][:, 512:], ALU.mult, ALU.mult, tok)
                b.free = [t_u]
                t_h = tt(h[:, :], h[:, :], X.ap[:, :], ALU.add, t_u, self.t_x[t])
            else:
                tt(h[:, 0:512], M0[t][:, :], X.ap[:, 0:512], ALU.add, self.m0[t], self.t_x[t], H.free)
                t_h = tt(h[:, 512:], b.ap, X.ap[:, 512:], ALU.add, tok)
                b.free = [t_h]
            X.free = [t_h]
            self.load(t + 2)
            s = col()
            t_s = act(XN[t % 4].ap[:, :], h[:, :], ACT.Square, t_h, XN[t % 4].free, scale=RT, accum_out=s)
            H.free = [t_s]
            if self.h is not None:
                H.free.append(l_h[t % 2].start(AC, self.h[128 * t:128 * t + 128, :], h[:, :], t_h))
            self.r2[t] = inv_rms(s, epsc[:, 0:1], t_s)
            self.t_h[t] = t_h

        def c(self, t):
            r, t_r = self.r2[t]
            X, H = XN[t % 4], HT[t % 2]
            self.t_xn[t] = stt(X.ap[:, :], H.ap[:, :], r, GB[1][:, :], ALU.mult, ALU.mult, t_r, self.t_gb[1])
            H.free.append(self.t_xn[t])
            if self.final:
                X.free = [l_out[t % 4].start(SP, out_dram[128 * t:128 * t + 128, :], X.ap[:, :], self.t_xn[t])]

        def d(self, t):
            if not self.final:
                col_ready[t] = []
                XN[t % 4].free = [turn_in(XN[t % 4].ap, 8, t, 0, self.t_xn[t])]

    def token_stage(order, slot, col_tok, passage, extra=None, keep_waits=()):
        last_use = {}
        for j in range(2):
            ks = order[j]
            tail = 2 if j == 0 else min(6, len(ks))
            held = []
            for t in range(NT):
                banks[t].open = False
            body = len(ks) - tail
            for i in range(0, body, 2):
                k = next_chunk()
                for ii in range(2):
                    p = i + ii
                    if extra:
                        extra(j, p)
                    for t in range(NT):
                        s = slot(j, p)
                        tok = mm3(banks[t].ap, AH[:, s, 128 * t:128 * t + 128], AL[:, s, 128 * t:128 * t + 128],
                                  k.hi[:, 512 * ii:512 * ii + 512], k.lo[:, 512 * ii:512 * ii + 512], p == 0, False,
                                  k.ready, banks[t].free if p == 0 else None, col_tok(j, p, t), inc=(t == NT - 1))
                    last_use[s] = tok
                    if extra:
                        extra.used(j, p, tok)
                chunk_done(k, tok)
            chunks = [next_chunk() for _ in range(tail // 2)]
            if extra:
                for p in range(body, len(ks)):
                    extra(j, p)
            for t in range(NT):
                for p in range(body, len(ks)):
                    k, ii, s = chunks[(p - body) // 2], (p - body) % 2, slot(j, p)
                    tok = mm3(banks[t].ap, AH[:, s, 128 * t:128 * t + 128], AL[:, s, 128 * t:128 * t + 128],
                              k.hi[:, 512 * ii:512 * ii + 512], k.lo[:, 512 * ii:512 * ii + 512], p == 0,
                              p == len(ks) - 1, k.ready, banks[t].free if p == 0 else None, col_tok(j, p, t),
                              inc=(p == len(ks) - 1))
                if j == 0:
                    passage.keep(t, banks[t], tok, *keep_waits)
                    if t == NT - 1:
                        for k in chunks:
                            chunk_done(k, tok)
                        if extra:
                            for p in range(body, len(ks)):
                                extra.used(j, p, tok)
                else:
                    col_free[t] = [tok]
                    passage.a(t, banks[t], tok)
                    if t == 2:
                        run_ahead()
                    if t >= 2:
                        passage.c(t - 2)
                    if t >= 3:
                        bank_turn[0] = t - 3
                        passage.d(t - 3)
                    passage.b(t, banks[t], tok)
        passage.c(NT - 2)
        passage.c(NT - 1)
        chunks_done(chunks, tok)
        bank_turn[0] = 0

        def tail_turn(t):
            bank_turn[0] = 2 * (t - 4)
            passage.d(t)

        if not passage.final:
            for t in range(5, NT):
                pending.append(lambda t=t: tail_turn(t))

    def softmax_rows(src, dst, n, nm, t_nm, waits=(), scale=1.0):
        rs = col()
        return rs, act(dst, src, ACT.Exp, t_nm, *waits, bias=nm, accum_out=rs)

    SGT = [sb(f"sg{i}", [128, 512], off["sg"] + 2 * KB * i) for i in range(2)]
    SGR = Ring([Place(t) for t in SGT])

    oh1 = big("oh1", [33, 383], 20)
    rb1 = big("rb1", [33, 8], 22)
    oh2a = big("oh2a", [128, 767], 24)
    oh2b = big("oh2b", [64, 767], 28)
    rb2a = big("rb2a", [128, 4], 32)
    rb2b = big("rb2b", [64, 4], 32.5)
    ones_row = DV.put(lambda e: e.memset(rb1[32:33, :], 1.0))
    cw = big("cw", [34, 512], 33)

    x0 = [Place(big(f"x0_{i}", [128, 1024], at)) for i, at in enumerate((56, 60, 64, 68, 80, 84))]
    l_x0 = l_xr + l_h + l_out
    n0 = [Place(big(f"n0_{i}", [128, 1024], 4 * i)) for i in range(4)]
    t_x0 = {}

    def load0(t):
        if t < NT:
            p = x0[t % 6]
            t_x0[t] = l_x0[t % 6].start(SP, p.ap[:, :], I["x"][128 * t:128 * t + 128, :], p.free)

    stat0 = {}

    def square0(t):
        X, N = x0[t % 6], n0[t % 4]
        s = col()
        t_s = act(N.ap[:, :], X.ap[:, :], ACT.Square, t_x0[t], N.free, scale=RT, accum_out=s)
        stat0[t] = inv_rms(s, epsc[:, 0:1], t_s)

    def norm0(t):
        X, N = x0[t % 6], n0[t % 4]
        r, t_r = stat0[t]
        t_n = stt(N.ap[:, :], X.ap[:, :], r, GB[1][:, :], ALU.mult, ALU.mult, t_r, t_g0)
        X.free = [t_n]
        load0(t + 6)
        return t_n

    load0(0)
    t_g0 = l_gb[1].start(SP, GB[1][:, :], I["mix_pre_g"].partition_broadcast(128))
    for t in range(1, 4):
        load0(t)
    load_chunk()
    load_chunk()
    for t in range(4, 6):
        load0(t)
    l_misc.start(SP, cw[0:31, :], I["conv_dw"])
    for i, name in enumerate(("conv_dw_b", "conv_ln_g", "conv_ln_b")):
        l_misc.start(SP, cw[31 + i:32 + i, :], I[name].rearrange("(a n) -> a n", a=1))
    l_misc.start(SP, oh1[:, :], I["c_oh1"])
    l_misc.start(SP, rb1[0:32, :], I["rel_bias"])
    l_misc.start(SP, oh2a[:, :], I["c_oh2"][0:128, :])
    l_misc.start(SP, oh2b[:, :], I["c_oh2"][128:192, :])
    rel2 = I["rel_bias_2"][0]
    l_misc.start(SP, rb2a[:, :], rel2[:, 0:128].rearrange("h r -> r h"), allow_slow_non_contiguous=True)
    l_misc.start(SP, rb2b[:, :], rel2[:, 128:192].rearrange("h r -> r h"), allow_slow_non_contiguous=True)
    t_misc = l_misc.start(SP, sinks[:, :], I["attn_sinks"].partition_broadcast(128))

    t_n0 = {}
    for t in range(3):
        square0(t)
    t_n0[0] = norm0(0)
    for t in range(4):
        if t + 1 < 4:
            t_n0[t + 1] = norm0(t + 1)
        n0[t].free = [turn_in(n0[t].ap, 8, t, 0, t_n0[t])]
        if t == 0:
            square0(3)
        if t in (0, 2):
            send_chunk()
    square0(4)
    square0(5)
    for t in range(4, NT):
        t_n0[t] = norm0(t)
        if t < 6:
            square0(t + 2)

    def turn0(t):
        n0[t % 4].free = [turn_in(n0[t % 4].ap, 8, t, 0, t_n0[t])]

    for t in range(4, NT):
        pending.append(lambda t=t: turn0(t))

    def bias_tables():
        b, g = take_bank(), SGR.take()
        t_m = mm(b.ap[0:8, 0:383], rb1[0:33, :], oh1[:, :], True, True, t_misc, ones_row, b.free, inc=True)
        t_c = cp(g.ap[0:8, 0:383], b.ap[0:8, 0:383], t_m, g.free)
        b.free = [t_c]
        g.free = [l_sk[0].start(SP, bass.AP(sk1, 0, [[128 * 384, 8], [384, 128], [1, 383]]),
                               g.ap[0:8, 0:383].unsqueeze(1).to_broadcast([8, 128, 383]), t_c)]
        for i, (a, n) in enumerate(((0, 512), (512, 255))):
            b, g = take_bank(), SGR.take()
            mm(b.ap[0:4, 0:n], rb2a[:, :], oh2a[:, a:a + n], True, False, t_misc, b.free)
            t_m = mm(b.ap[0:4, 0:n], rb2b[:, :], oh2b[:, a:a + n], False, True, inc=True)
            t_c = cp(g.ap[0:4, 0:n], b.ap[0:4, 0:n], t_m, g.free)
            b.free = [t_c]
            g.free = [l_sk[1 + i].start(SP, bass.AP(sk2, a, [[128 * 768, 4], [768, 128], [1, n]]),
                                   g.ap[0:4, 0:n].unsqueeze(1).to_broadcast([4, 128, n]), t_c)]

    q1 = big("q1", [128, 4, 1024], 0)
    kp1 = big("kp1", [128, 4, 1024], 16)
    v1 = big("v1", [128, 8, 128], 32)
    hp = big("hp", [128, 4, 1054], 36)
    acc = big("acc", [128, 4, 1024], 52.5)
    b1 = big("b1", [128, 8, 256], 68.5)
    s1 = [Place(big(f"s1_{i}", [128, 2, 256], 76.5 + 2 * i)) for i in range(3)]
    v1t = big("v1t", [128, 1024], 76.5)
    pt1 = [Place(big(f"pt1_{i}", [128, 4, 128], 82.5 + 2 * i)) for i in range(2)]
    o1s = [Place(t) for t in SGT]
    cwt = big("cwt", [128, 4, 34], 86.5)

    b = take_bank()
    for c in range(4):
        t_m = tr(b.ap[:, 34 * c:34 * c + 34], cw[0:34, 128 * c:128 * c + 128], t_misc, b.free, inc=(c == 3))
    t_cw = cp(cwt[:, :, :], b.ap[:, 0:136].rearrange("p (c w) -> p c w", c=4), t_m, x0[5].free)
    b.free = [t_cw]
    first = []
    t_hp0 = DV.put(lambda e: e.memset(hp[:, :, 0:30], 0.0))
    t_nsink = ts(nsink[:, :], sinks[:, :], -1.0, None, ALU.mult, None, t_misc)

    taps = []

    def tap_steps(c, t_h):
        state = [None]

        def step(w):
            def go():
                src = hp[:, c, w:w + 1024]
                if w == 0:
                    state[0] = ts(acc[:, c, :], src, cwt[:, c, 0:1], cwt[:, c, 31:32], ALU.mult, ALU.add,
                                  t_h, t_cw, t_hp0, first)
                else:
                    state[0] = stt(acc[:, c, :], src, cwt[:, c, w:w + 1], acc[:, c, :], ALU.mult, ALU.add, state[0])
            return go

        more = [step(w) for w in range(TAPS)]
        mixed = []
        while taps or more:
            mixed += taps[0:1] + more[0:1]
            del taps[0:1], more[0:1]
        taps.extend(mixed)

    def some_taps(n):
        for _ in range(min(n, len(taps))):
            taps.pop(0)()

    prod = Ring([Place(big(f"prod{i}", [128, 512], 80.5 + 2 * i)) for i in range(3)])
    ptaps = []
    p_acc = [None, None]

    def pool_taps(t_h):
        def step(w, hf):
            def go():
                src, dst = hp[:, 0, w + 512 * hf:w + 512 * hf + 512], acc[:, 0, 512 * hf:512 * hf + 512]
                if w == 0:
                    p_acc[hf] = act(dst, src, ACT.Identity, t_h, t_cw, t_hp0, first, scale=cwt[:, 0, 0:1],
                                    bias=cwt[:, 0, 31:32])
                    return
                g = prod.take()
                t_p = act(g.ap[:, :], src, ACT.Copy, g.free, first, scale=cwt[:, 0, w:w + 1])
                p_acc[hf] = PL.put(lambda e: e.tensor_tensor(dst, dst, g.ap[:, :], ALU.add), t_p, p_acc[hf])
                g.free = [p_acc[hf]]
            return go
        ptaps.extend(step(w, hf) for w in range(TAPS) for hf in range(2))

    def spare():
        some_taps(4)
        for _ in range(min(3, len(ptaps))):
            ptaps.pop(0)()

    for c in range(4):
        sg = {}

        def gate(th, b, tok):
            g = SGR.take()
            sg[th] = (g, act(g.ap[:, :], b.ap, ACT.Sigmoid, tok, g.free))
            return [sg[th][1]]

        t_hc = []

        def glu(th, b, tok):
            g, t_g = sg[th]
            t = tt(hp[:, c, 30 + 512 * th:542 + 512 * th], b.ap, g.ap[:, :], ALU.mult, tok, t_g)
            g.free = [t]
            t_hc.append(t)
            return [t]

        feature_group([gate, glu], spare)
        if c == 0:
            bias_tables()
            t_skew = flatten([l.last() for l in l_sk])
            first += mark() + l_xr[0].last() + l_xr[1].last() + t_skew
            t_b1 = l_bias.start(SP, b1[:, :, :], bass.AP(sk1, 127, [[383, 128], [128 * 384, 8], [1, 256]]), first)
            pool_taps(t_hc)
        else:
            tap_steps(c, t_hc)

    t_kz = []
    for g in range(2):
        for s_ in range(2):
            z = 64 * (1 - s_)
            t_kz.append(DV.put(lambda e, i=2 * g + s_, z=z: e.memset(kp1[z:z + 64, i, :], 0.0), first))
    t_k1 = []

    def k_out(th, b, tok):
        cs = slice(512 * th, 512 * th + 512)
        t = []
        for g in range(2):
            for s_ in range(2):
                o, i = kp1[64 * s_:64 * s_ + 64, 2 * g + s_, cs], b.ap[64 * g:64 * g + 64, :]
                t.append(act(o, i, ACT.Copy, tok, first))
        t_k1.extend(t)
        return t

    feature_group([k_out], spare)
    t_vt = []

    def v_out(th, b, tok):
        t = act(v1t[:, 512 * th:512 * th + 512], b.ap, ACT.Copy, tok, first)
        t_vt.append(t)
        return [t]

    feature_group([v_out], spare)
    t_v1 = []

    def v_turn():
        for g in range(2):
            b = take_bank()
            for j in range(4):
                t = 4 * g + j
                t_m = tr(b.ap[:, 128 * j:128 * j + 128], v1t[:, 128 * t:128 * t + 128], t_vt, b.free, inc=(j == 3))
            t_c = act(v1[:, 4 * g:4 * g + 4, :], b.ap.rearrange("p (t d) -> p t d", t=4), ACT.Copy, t_m, first)
            b.free = [t_c]
            t_v1.append(t_c)
        s1[0].free, s1[1].free = [t_m], [t_m]

    t_q1 = {}

    def q_out(m):
        def go(th, b, tok):
            t = act(q1[:, m, 512 * th:512 * th + 512], b.ap, ACT.Copy, tok, first, scale=0.125)
            t_q1[m] = t
            return [t]
        return go

    for m in range(4):
        feature_group([q_out(m)], spare)
        if m == 0:
            v_turn()
    while ptaps:
        ptaps.pop(0)()
    pooled = p_acc + [g.free for g in prod.places]

    def attention(steps, scores, soft, turn, values):
        n = len(steps)
        for i in range(n + 3):
            if i < n:
                scores(i)
            if i >= 3:
                values(i - 3)
            if 2 <= i <= n + 1:
                turn(i - 2)
            if i < n:
                soft(i)
            if i in (3, 6, 9):
                run_ahead()
            some_taps(1)
            for due, fn in list(later):
                if due <= i:
                    later.remove((due, fn))
                    fn()
        for due, fn in list(later):
            later.remove((due, fn))
            fn()

    later = []
    sc_banks = banks[0:3]
    tr_banks = Ring(banks[3:5])
    o_banks = banks[5:7]
    for i in range(2):
        o1s[i].free = SGR.places[i].free
        pt1[i].free = pooled
    s1[2].free = pooled
    st = {}
    steps1 = [(n, g) for n in range(NT) for g in range(4)]

    def sc1(i):
        n, g = steps1[i]
        W = 128 if n == 0 else 256
        b = sc_banks[i % 3]
        for j in range(2):
            kv = g // 2
            t_m = mm(b.ap[:, 256 * j:256 * j + W], q1[:, g, 128 * n:128 * n + 128],
                     kp1[:, 2 * kv + j, 128 * (n + 1) - W:128 * (n + 1)], True, True,
                     t_q1[g], t_k1, t_kz, b.free, inc=(j == 1))
        st[i] = {"W": W, "sc": t_m}

    rows = {}

    def so1(i):
        n, g = steps1[i]
        d = st[i]
        W, b, s = d["W"], sc_banks[i % 3], s1[i % 3]
        if g == 0:
            rows[n] = {"rs": col(8), "es": col(8), "t": []}
        mx, nm, es = col(2), col(2), col(2)
        for j in range(2):
            h = 2 * g + j
            t_x = DV.put(lambda e, j=j, h=h: e.tensor_tensor_reduce(
                out=s.ap[:, j, 0:W], in0=b.ap[:, 256 * j:256 * j + W], in1=b1[:, h, 256 - W:256], scale=1.0,
                scalar=NEG, op0=ALU.add, op1=ALU.max, accum_out=mx[:, j:j + 1]), d["sc"], t_b1, s.free)
        b.free = [t_x]
        t_n = stt(nm, mx, -1.0, nsink[:, 2 * g:2 * g + 2], ALU.mult, ALU.min, t_x, t_nsink)
        t_d = tt(es, nm, sinks[:, 2 * g:2 * g + 2], ALU.add, t_n)
        for j in range(2):
            t_e = act(s.ap[:, j, 0:W], s.ap[:, j, 0:W], ACT.Exp, t_n, bias=nm[:, j:j + 1],
                      accum_out=rows[n]["rs"][:, 2 * g + j:2 * g + j + 1])
        rows[n]["t"].append(act(rows[n]["es"][:, 2 * g:2 * g + 2], es, ACT.Exp, t_d))
        d["p"] = t_e

    def tu1(i):
        d = st[i]
        W, s, pt = d["W"], s1[i % 3], pt1[i % 2]
        nb = W // 128
        b = tr_banks.take()
        for j in range(2):
            for kb in range(nb):
                t_m = tr(b.ap[:, 128 * (nb * j + kb):128 * (nb * j + kb) + 128], s.ap[:, j, 128 * kb:128 * kb + 128],
                         d["p"], b.free, inc=(j == 1 and kb == nb - 1))
        s.free = [t_m]
        o, v = pt.ap[:, 0:2 * nb, :], b.ap[:, 0:256 * nb].rearrange("p (k c) -> p k c", c=128)
        t_c = cp(o, v, t_m, pt.free) if i % 3 == 0 else act(o, v, ACT.Copy, t_m, pt.free)
        b.free = [t_c]
        d["pt"] = t_c

    def va1(i):
        n, g = steps1[i]
        d = st[i]
        W, pt, ob = d["W"], pt1[i % 2], o_banks[n % 2]
        nb, kv = W // 128, g // 2
        for j in range(2):
            for kb in range(nb):
                h = 2 * g + j
                t_m = mm(ob.ap[:, 64 * h:64 * h + 64], pt.ap[:, nb * j + kb, :],
                         v1[:, n + 1 - nb + kb, 64 * kv:64 * kv + 64], kb == 0, kb == nb - 1,
                         d["pt"], t_v1, ob.free if g == 0 else None, inc=(j == 1 and kb == nb - 1))
        pt.free = [t_m]
        if g == 3:
            r = rows[n]
            den, rden, o1 = col(8), col(8), o1s[n % 2]
            t_d = tt(den, r["rs"], r["es"], ALU.add, r["t"], AC.last())
            t_r = DV.put(lambda e: e.reciprocal(rden, den), t_d)
            t_o = tt(o1.ap[:, :].rearrange("p (h d) -> p h d", h=8), ob.ap.rearrange("p (h d) -> p h d", h=8),
                     rden.unsqueeze(2).to_broadcast([128, 8, 64]), ALU.mult, t_r, t_m, o1.free)
            ob.free = [t_o]

            def turn_y():
                bank_turn[0] = 7
                col_ready[n] = []
                o1.free = [turn_in(o1.ap, 4, n, 0, t_o)]
            later.append((i + 3, turn_y))

    yc1 = [Place(big(f"yc1_{i}", [128, 512], 36 + 2 * i)) for i in range(NT)]
    t_y = {}

    def conv_norm(tb):
        some_taps(len(taps))
        b, y = banks[7], yc1[tb].ap
        for c in range(4):
            t_m = tr(b.ap[:, 128 * c:128 * c + 128], acc[:, c, 128 * tb:128 * tb + 128], conv_done(), b.free, inc=(c == 3))
        bs, mv, v = col(6), col(2), col()
        t_c = act(y[:, :], b.ap, ACT.Copy, t_m, conv_done())
        b.free = [t_c]
        t_b = DV.put(lambda e: e.bn_stats(bs, y[:, :]), t_c)
        t_a = DV.put(lambda e: e.bn_aggr(mv, bs), t_b)
        t_v = ts(v, mv[:, 1:2], EPS, None, ALU.add, None, t_a)
        r, t_r = inv_sqrt(v, t_v)
        t_y[tb] = ts(y[:, :], y[:, :], mv[:, 0:1], r, ALU.subtract, ALU.mult, t_r)

    def conv_done():
        if "t" not in t_y:
            t_y["t"] = DV.last() + AC.last() + flatten(p_acc)
        return t_y["t"]

    for tb in range(NT):
        later.append((13 + 2 * tb, lambda tb=tb: conv_norm(tb)))

    attention(steps1, sc1, so1, tu1, va1)
    bank_turn[0] = 0

    for i in range(2):
        SGR.places[i].free = o1s[i].free
    done1 = mark()
    ZH = big("zh", [128, 4, 1024], 0, F32R)
    ZL = big("zl", [128, 4, 1024], 16, F32R)
    t_z = {}

    def ln_back(th, t_y):
        for c in range(4):
            b, g = take_bank(), SGR.take()
            for j in range(4):
                t_m = tr(b.ap[:, 128 * j:128 * j + 128], yc1[4 * th + j].ap[:, 128 * c:128 * c + 128], t_y, b.free,
                         inc=(j == 3))
            t_s = act(g.ap[:, :], b.ap, ACT.Silu, t_m, g.free, bias=cwt[:, c, 33:34], scale=cwt[:, c, 32:33])
            b.free = [t_s]
            cs = slice(512 * th, 512 * th + 512)
            t_hi = act(ZH[:, c, cs], g.ap[:, :], ACT.Copy, t_s, done1)
            t_lo = tt(ZL[:, c, cs], g.ap[:, :], ZH[:, c, cs].bitcast(F32), ALU.subtract, t_hi)
            g.free = [t_lo]
            t_z[th, c] = [t_hi, t_lo]

    ln_back(0, [t_y[tb] for tb in range(4)])
    pws = [next_chunk() for _ in range(4)]
    for th in range(2):
        for m, k in enumerate(pws):
            v = lambda i: (k.hi[:, 128 * i:128 * i + 128], k.lo[:, 128 * i:128 * i + 128])
            b = take_bank()
            cs = slice(512 * th, 512 * th + 512)
            tok = feature_unit(k, v, 4, lambda i: (ZH[:, i, cs], ZL[:, i, cs]), th, b, [t_z[th, c] for c in range(4)])
            hi, lo = AH[:, 4 + m, cs], AL[:, 4 + m, cs]
            t_hi = act(hi, b.ap, ACT.Copy, tok, col_free[0])
            t_lo = tt(lo, b.ap, hi.bitcast(F32), ALU.subtract, t_hi, col_free[0])
            b.free = [t_lo]
            for t in range(4 * th, 4 * th + 4):
                col_ready[t] = col_ready[t] + [t_hi, t_lo]
            if th == 0 and m == 0:
                ln_back(1, [t_y[tb] for tb in range(4, 8)])
            if th == 1:
                chunk_done(k, tok)

    pas = Passage(I["x"], I["mix_post_g"], I["ffn_pre_g"], h1, after=mark())
    eight = [list(range(8))] * 2
    token_stage(eight, lambda j, p: p, lambda j, p, t: col_ready[t], pas)

    ff_big = big("ff", [128, NF, 1024], 0)

    def ffn(x, g_post, g_pre, h, final=False):
        nonlocal pas
        t_ff = {}
        held = {}
        first_in = mark() + l_h[0].last() + l_h[1].last()

        class Split:
            free = {}
            made = {}
            done = 0
            early = {}

            def __call__(self, j, p):
                at = p if j == 0 else 14 + p
                goal = min(at + 5, NF if j == 0 else NF + 14)
                while self.done < goal:
                    self.one(self.done)
                    self.done += 1

            def part(self, f, s, a, b, w):
                t_hi = act(AH[:, s, a:b], ff_big[:, f, a:b], ACT.Copy, t_ff[f], w)
                t_lo = tt(AL[:, s, a:b], ff_big[:, f, a:b], AH[:, s, a:b].bitcast(F32), ALU.subtract, t_hi, w)
                return [t_hi, t_lo]

            def begin(self):
                for f in range(2):
                    self.early[f] = self.part(f, f, 0, 512, col_free[0])

            def one(self, at):
                f, s = at % NF, at % 8
                if at in self.early:
                    self.made[at] = [self.early[at], self.part(f, s, 512, 1024, col_free[4])]
                else:
                    self.made[at] = [self.part(f, s, 0, 1024, self.free.get(s, col_free[0] + col_free[4]))] * 2

            def used(self, j, p, tok):
                at = p if j == 0 else 14 + p
                self.free[at % 8] = [tok]

        split = Split()

        def pair_of(m):
            sg = {}

            def gate(th, b, tok):
                g = SGR.take()
                sg[th] = (g, act(g.ap[:, :], b.ap, ACT.Silu, tok, g.free))
                if m == NF - 1 and th == 1:
                    split.begin()
                return [sg[th][1]]

            def up(th, b, tok):
                g, t_g = sg[th]
                if "mark" not in held and th:
                    held["mark"] = mark() + l_h[0].last() + l_h[1].last()
                w = held.get("mark", first_in)
                t = tt(ff_big[:, m, 512 * th:512 * th + 512], b.ap, g.ap[:, :], ALU.mult, tok, t_g, w)
                g.free = [t]
                t_ff.setdefault(m, []).append(t)
                return [t]
            return [gate, up]

        for m in range(NF):
            feature_group(pair_of(m))
        split(0, 0)

        def slot(j, p):
            return (p if j == 0 else 14 + p) % 8

        def col_tok(j, p, t):
            return split.made[p if j == 0 else 14 + p][t // 4]

        class Later:
            pas = None

            def begin(self):
                spent = flatten([split.made[a] for a in range(14, 22)])
                p = self.pas = Passage.__new__(Passage)
                p.x, p.h, p.final, p.g_post, p.after = x, h, final, g_post, spent
                p.t_gb = [None, None]
                if g_post is not None:
                    p.t_gb[0] = l_gb[0].start(SP, GB[0][:, :], g_post.partition_broadcast(128), spent)
                p.t_gb[1] = l_gb[1].start(SP, GB[1][:, :], g_pre.partition_broadcast(128), spent)
                for q in XR:
                    q.free = spent
                p.t_x, p.m0, p.ss0, p.r1, p.r2, p.t_h, p.t_xn = {}, {}, {}, {}, {}, {}, {}
                for t in range(2):
                    p.load(t)
                p.g_post = None
                self.p = p

            def keep(self, t, b, tok, *waits):
                if self.pas is None:
                    self.begin()
                self.p.keep(t, b, tok, *waits)

            def squares(self):
                spent = flatten([split.made[a] for a in range(22, 26)])
                p = self.p
                p.g_post = g_post
                for q in HT + XN:
                    q.free = spent
                if g_post is not None:
                    for t in range(NT):
                        s, v = col(), col()
                        j = HT[t % 2]
                        t_s = act(j.ap[:, 0:512], M0[t][:, :], ACT.Square, p.m0[t], j.free, scale=RT, accum_out=s)
                        j.free = [t_s]
                        p.ss0[t] = (v, ts(v, s, EPS, None, ALU.add, None, t_s))

            def a(self, t, b, tok):
                if t == 0:
                    self.squares()
                self.p.a(t, b, tok)

            def b(self, t, b, tok):
                self.p.b(t, b, tok)

            def c(self, t):
                self.p.c(t)

            def d(self, t):
                self.p.d(t)

            @property
            def final(self):
                return final

        later_pas = Later()
        token_stage(down_order, slot, col_tok, later_pas, extra=split)

    ffn(h1, I["ffn_post_g"], I["norm_mix_2"][0], h2)

    cv = big("cv", [128, 8, 256], 0)
    fv = big("fv", [128, 8, 256], 8)
    cq = big("cq", [128, 2, 1024], 16)
    ckp = big("ckp", [128, 4, 1024], 24)
    b2 = big("b2", [128, 4, 640], 40)
    s2 = [Place(big(f"s2_{i}", [128, 640], 50 + 2.5 * i)) for i in range(3)]
    pt2 = [Place(big(f"pt2_{i}", [128, 5, 128], 57.5 + 2.5 * i)) for i in range(2)]
    o2 = [Place(big("o2", [128, 256], 86.5))]
    yc = big("yc", [128, 8, 256], 62.5)
    gout = sb("gout", [128, 1024], off["sg"])
    fqp = big("fqp", [128, 4, 1024], 70.5)
    fkp = big("fkp", [128, 4, 1024], 16)
    CH = big("ch", [128, 3, 1024], 32, F32R)
    CL = big("cl", [128, 3, 1024], 44, F32R)
    kpe = big("kpe", [128, 1024], 4)

    in0 = mark()
    t_ckz = [DV.put(lambda e, h=h: e.memset(ckp[64 * (1 - h % 2):64 * (1 - h % 2) + 64, h, :], 0.0), in0) for h in range(4)]
    t_cq, t_ck = [], []

    def cq_out(m):
        def go(th, b, tok):
            t_cq.append(act(cq[:, m, 512 * th:512 * th + 512], b.ap, ACT.Copy, tok, in0, scale=0.125))
            return [t_cq[-1]]
        return go

    def pair_out(dst, m, toks, scale, waits):
        def go(th, b, tok):
            t = []
            for s_ in range(2):
                t.append(act(dst[64 * s_:64 * s_ + 64, 2 * m + s_, 512 * th:512 * th + 512],
                             b.ap[64 * s_:64 * s_ + 64, :], ACT.Copy, tok, waits, scale=scale))
            toks.extend(t)
            return t
        return go

    feature_group([cq_out(0), cq_out(1)])
    feature_group([pair_out(ckp, m, t_ck, 1.0, in0) for m in range(2)])
    in1 = mark() + l_h[0].last() + l_h[1].last()
    t_gout = l_gb[0].start(SP, gout[:, :], I["out_norm_2"][0].partition_broadcast(128), in1)
    t_b2 = l_bias.start(SP, b2[:, :, :], bass.AP(sk2, 127, [[767, 128], [128 * 768, 4], [1, 640]]), in1, t_skew)
    t_b2m = [DV.put(lambda e: e.memset(b2[0:64, :, 576:640], NEG), t_b2),
             DV.put(lambda e: e.memset(b2[64:128, :, 0:64], NEG), t_b2)]

    def token_group(width, evac, take=None):
        ks = [next_chunk() for _ in range(4)]
        for t in range(NT):
            b = take_bank()
            for p in range(8):
                k, ii = ks[p // 2], p % 2
                tok = mm3(b.ap[:, 0:width], AH[:, p, 128 * t:128 * t + 128], AL[:, p, 128 * t:128 * t + 128],
                          k.hi[:, width * ii:width * ii + width], k.lo[:, width * ii:width * ii + width], p == 0,
                          p == 7, k.ready, b.free, col_ready[t], inc=(p == 7))
            col_free[t] = [tok]
            b.free = flatten(evac(t, b, tok))
        chunks_done(ks, tok)
        return tok

    t_cv, t_fv = {}, {}

    def fvcv_out(t, b, tok):
        t_fv[t] = act(fv[:, t, :], b.ap[:, 0:256], ACT.Copy, tok, in1)
        t_cv[t] = act(cv[:, t, :], b.ap[:, 256:512], ACT.Copy, tok, in1)
        return [t_cv[t]]

    token_group(512, fvcv_out)

    def heads_attention(kind, q, k, v, nh, dv, width, p_ring, pt_ring, o_ring, finish, t_q, t_k, t_v, began):
        steps = [(i, h) for i in range(NT) for h in range(nh)]
        st, rows = {}, {}
        pairs = [(0, 1), (2, 3)]
        tb = Ring([banks[4], banks[5]])

        def sc(x):
            i, h = steps[x]
            a, b = width(i)
            W = b - a
            p = pairs[x % 2]
            for w in range(0, W, 512):
                n = min(512, W - w)
                bk = banks[p[w // 512]]
                t_m = mm(bk.ap[:, 0:n], q(h, i), k(h, a + w, a + w + n), True, True, t_q, t_k, banks[p[0]].free,
                         banks[p[1]].free, inc=True)
            st[x] = {"W": W, "t": t_m, "ap": PF[:, 512 * p[0]:512 * p[0] + W]}

        def so(x):
            i, h = steps[x]
            d, pr = st[x], p_ring[x % 3]
            W, ap, p = d["W"], d["ap"], pairs[x % 2]
            if h == 0:
                rows[i] = col(nh)
            nm = col()
            dst = pr.ap[:, 0:W]
            src = ap
            if kind == "chunk":
                mx = col()
                t_x = DV.put(lambda e: e.tensor_tensor_reduce(out=dst, in0=ap, in1=b2[:, h, 640 - W:640], scale=1.0,
                                                              scalar=NEG, op0=ALU.add, op1=ALU.max, accum_out=mx),
                             d["t"], t_b2m, pr.free)
                banks[p[0]].free = banks[p[1]].free = [t_x]
                t_n = ts(nm, mx, -1.0, None, ALU.mult, None, t_x)
                src = dst
            else:
                t_m = d["t"]
                if kind == "mla":
                    t_m = DV.put(lambda e: e.memset(ap[0:64, W - 64:W], NEG), d["t"])
                elif kind == "fox":
                    t_m = tt(ap[:, W - 128:W], ap[:, W - 128:W], causal[:, :], ALU.add, d["t"], t_causal)
                t_n = DV.put(lambda e: e.tensor_reduce(nm, ap, AX.X, ALU.max, negate=True), t_m)
            rs = rows[i][:, h:h + 1]
            d["p"] = act(dst, src, ACT.Exp, t_n, pr.free, bias=nm, accum_out=rs)
            if kind != "chunk":
                banks[p[0]].free = banks[p[1]].free = [d["p"]]

        def tu(x):
            d, pr, pt = st[x], p_ring[x % 3], pt_ring[x % 2]
            nb = d["W"] // 128
            made = []
            for g in range(0, nb, 4):
                w = min(4, nb - g)
                b = tb.take()
                for j in range(w):
                    t_m = tr(b.ap[:, 128 * j:128 * j + 128], pr.ap[:, 128 * (g + j):128 * (g + j) + 128], d["p"], b.free,
                             inc=(j == w - 1))
                o, v_ = pt.ap[:, g:g + w, :], b.ap[:, 0:128 * w].rearrange("p (k c) -> p k c", c=128)
                t_c = cp(o, v_, t_m, pt.free) if (x + g // 4) % 2 else act(o, v_, ACT.Copy, t_m, pt.free)
                b.free = [t_c]
                made.append(t_c)
            pr.free = [t_m]
            d["pt"] = made

        def va(x):
            i, h = steps[x]
            d, pt, ob = st[x], pt_ring[x % 2], banks[6]
            a, b = width(i)
            nb = d["W"] // 128
            for kb in range(nb):
                t_m = mm(ob.ap[:, dv * h:dv * h + dv], pt.ap[:, kb, :], v(h, a // 128 + kb), kb == 0, kb == nb - 1,
                         d["pt"], t_v, ob.free if h == 0 else None, inc=(kb == nb - 1))
            pt.free = [t_m]
            if h == nh - 1:
                rden = col(nh)
                o = o_ring[i % len(o_ring)]
                t_r = DV.put(lambda e: e.reciprocal(rden, rows[i]), [st[y]["p"] for y in range(x - nh + 1, x + 1)])
                t_o = tt(o.ap[:, :].rearrange("p (h d) -> p h d", h=nh),
                         ob.ap[:, 0:nh * dv].rearrange("p (h d) -> p h d", h=nh),
                         rden.unsqueeze(2).to_broadcast([128, nh, dv]), ALU.mult, t_r, t_m, o.free)
                ob.free = [t_o]
                finish(i, o, t_o, x)

        for r in (p_ring, pt_ring, o_ring):
            for pl in r:
                pl.free = list(began)
        attention(steps, sc, so, tu, va)

    def group_norm(o, n, g0, junk, t_o, *waits):
        s, v = col(), col()
        t_s = act(junk, o, ACT.Square, t_o, *waits, accum_out=s)
        t_v = ts(v, s, 1.0 / n, EPS, ALU.mult, ALU.add, t_s)
        r, t_r = inv_sqrt(v, t_v)
        return r, t_r

    in2 = mark()
    t_yc = {}

    def chunk_finish(i, o, t_o, x):
        r, t_r = group_norm(o.ap[:, :], 256, 768, yc[:, i, :], t_o, in2)
        t_yc[i] = stt(yc[:, i, :], o.ap[:, :], r, gout[:, 768:1024], ALU.mult, ALU.mult, t_r, t_gout)
        o.free = [t_yc[i]]

    heads_attention("chunk", lambda h, i: cq[:, h // 2, 128 * i:128 * i + 128], lambda h, a, b: ckp[:, h, a:b],
                    lambda h, kb: cv[:, kb, 64 * h:64 * h + 64], 4, 64,
                    lambda i: (max(0, 128 * i - 512), 128 * i + 128), s2, pt2, o2, chunk_finish,
                    t_cq, [t_ck, t_ckz], [t_cv[t] for t in range(NT)], in2)
    bank_turn[0] = 0

    in3 = mark()
    tt_ring = [Place(big(f"tt_{i}", [128, 512], 56 + 2 * i)) for i in range(2)]
    ropek = big("ropek", [128, 8, 64], 60)
    gq = big("gq", [128, 384], 86.5)
    fl = big("fl", [4, 1024], 0)
    l_mem.start(SP, ropek[:, :, :], I["c_ropek"], in3)
    l_mem.start(SP, gq[:, 0:256], I["q_norm_2"][0].partition_broadcast(128), in3)
    l_mem.start(SP, gq[:, 256:384], I["kv_norm_2"][0].partition_broadcast(128), in3)
    fbias = small("fbias", 1)
    l_mem.start(SP, fbias[0:4, :], I["f_bias_2"][0].rearrange("(n a) -> n a", a=1), in3)
    t_causal = t_fb = t_rk = l_mem.start(SP, causal[:, :], I["c_causal"], in3)
    t_ttz = [DV.put(lambda e, i=i: e.memset(tt_ring[i].ap[:, 384:512], 0.0), in3) for i in range(2)]
    t_narrow = {}
    lat = []

    def narrow_out(t, b, tok):
        T = tt_ring[t % 2]
        w = [T.free, in3, t_ttz]
        res = []
        sq = col(2)
        v = col(2)
        t_s = act(T.ap[:, 0:256], b.ap[:, 0:256], ACT.Square, tok, w, accum_out=sq[:, 0:1])
        t_s2 = act(T.ap[:, 256:384], b.ap[:, 256:384], ACT.Square, tok, w, accum_out=sq[:, 1:2])
        t_a = ts(v[:, 0:1], sq[:, 0:1], 1.0 / 256, EPS, ALU.mult, ALU.add, t_s)
        t_b = ts(v[:, 1:2], sq[:, 1:2], 1.0 / 128, EPS, ALU.mult, ALU.add, t_s2)
        r, t_r = inv_sqrt(v, t_a, t_b)
        x12 = b.ap[:, 384:416]
        ta = tt(ra[:, 0, :], x12, ropek[:, t, 0:32], ALU.mult, tok, t_s2, t_rk, in3, DV.last())
        tb1 = tt(ra[:, 1, 0:16], b.ap[:, 400:416], ropek[:, t, 32:48], ALU.mult, DV.last())
        tb2 = tt(ra[:, 1, 16:32], b.ap[:, 384:400], ropek[:, t, 48:64], ALU.mult, DV.last())
        tf = cp(T.ap[:, 384:388], b.ap[:, 416:420], w)
        t1 = tt(T.ap[:, 448:480], ra[:, 0, :], ra[:, 1, :], ALU.add, ta, tb1, tb2, w)
        t2 = stt(T.ap[:, 0:256], b.ap[:, 0:256], r[:, 0:1], gq[:, 0:256], ALU.mult, ALU.mult, t_r, t_rk)
        t3 = stt(T.ap[:, 256:384], b.ap[:, 256:384], r[:, 1:2], gq[:, 256:384], ALU.mult, ALU.mult)
        t_narrow[t] = [tf, t1, t2, t3]

        def turn():
            b2_ = take_bank()
            for j in range(4):
                t_m = tr(b2_.ap[:, 128 * j:128 * j + 128], T.ap[:, 128 * j:128 * j + 128], t_narrow[t], b2_.free,
                         inc=(j == 3))
            T.free = [t_m]
            cs = slice(128 * t, 128 * t + 128)
            vv = b2_.ap[:, 0:384].rearrange("p (k c) -> p k c", k=3)
            t_hi = act(CH[:, :, cs], vv, ACT.Copy, t_m, in3)
            t_k = act(kpe[64:96, cs], b2_.ap[64:96, 384:512], ACT.Copy, t_m, in3)
            t_f = act(fl[0:4, cs], b2_.ap[0:4, 384:512], ACT.Copy, t_m, in3)
            t_lo = tt(CL[:, :, cs], vv, CH[:, :, cs].bitcast(F32), ALU.subtract, t_hi, t_f, in3)
            b2_.free = [t_lo]
            lat.append((t_hi, t_lo, t_k, t_f))

        turns.append(turn)
        if len(turns) >= 2:
            turns.pop(0)()
        return [t3]

    turns = []
    tok = token_group(420, narrow_out)
    while turns:
        turns.pop(0)()
    t_fz = []
    for h in range(4):
        z = 64 * (1 - h % 2)
        for dst in (fqp, fkp):
            t0 = DV.put(lambda e, dst=dst, z=z, h=h: e.memset(dst[z:z + 64, h, :], 0.0), in3)
            t_fz.append(DV.put(lambda e, dst=dst, z=z, h=h: e.memset(dst[z:z + 2, h, :], 1.0), t0))
    in4 = mark()
    z1 = big("z1", [4, 1024], 56)
    t1 = ts(fl[:, :], fl[:, :], fbias[0:4, 0:1], None, ALU.add, None, in4, t_fb)
    t2 = stt(z1[:, :], fl[:, :], -1.0, fl[:, :], ALU.mult, ALU.max, t1, in4)
    t3 = act(z1[:, :], z1[:, :], ACT.Exp, t2, scale=-1.0)
    t4 = act(z1[:, :], z1[:, :], ACT.Ln, t3, bias=1.0)
    t5 = stt(fl[:, :], fl[:, :], 0.0, z1[:, :], ALU.min, ALU.subtract, t4)
    t6 = DV.put(lambda e: e.memset(z1[:, :], 1.0), t5)
    t7 = DV.put(lambda e: e.tensor_tensor_scan(z1[:, :], z1[:, :], fl[:, :], 0.0, ALU.mult, ALU.add), t6)
    t8 = ts(fl[:, :], z1[:, :], -1.0, None, ALU.mult, None, t7)
    for h in range(4):
        z = 64 * (1 - h % 2)
        l_aug.start(SP, fqp[z + 1:z + 2, h, :], z1[h:h + 1, :], t8, t_fz)
        t_aug = l_aug.start(SP, fkp[z:z + 1, h, :], fl[h:h + 1, :], t8, t_fz)
    t_fq, t_fk = [], []
    feature_group([pair_out(fqp, m, t_fq, 0.125, in3) for m in range(2)] +
                  [pair_out(fkp, m, t_fk, 1.0, in3) for m in range(2)])
    bank_turn[0] = 0

    def turn_yc(t):
        bank_turn[0] = 7
        col_ready[t] = []
        turn_in(yc[:, t, :], 2, t, 6, t_yc[t])

    for t in range(NT):
        later.append((3 + 3 * t, lambda t=t: turn_yc(t)))

    p3 = [Place(sb(f"p3_{i}", [128, 1024], off["ah"] + 4 * KB * i)) for i in range(3)]
    pt3 = [Place(sb(f"pt3_{i}", [128, 8, 128], off["al"] + 4 * KB * i)) for i in range(2)]
    o3 = [Place(big(f"o3_{i}", [128, 256], 58 + i)) for i in range(2)]
    SQ = [Place(big(f"sq3_{i}", [128, 256], 56 + i)) for i in range(2)]
    in5 = mark() + [t_aug]
    for q_ in SQ:
        q_.free = list(in5)

    def fox_finish(i, o, t_o, x):
        sq = SQ[i % 2]
        r, t_r = group_norm(o.ap[:, :], 256, 512, sq.ap[:, 0:256], t_o, sq.free)
        t_y = stt(o.ap[:, :], o.ap[:, :], r, gout[:, 512:768], ALU.mult, ALU.mult, t_r, t_gout)
        sq.free = [t_r]

        def turn_y():
            bank_turn[0] = 7
            o.free = [turn_in(o.ap, 2, i, 4, t_y)]
        later.append((x + 4, turn_y))

    heads_attention("fox", lambda h, i: fqp[:, h, 128 * i:128 * i + 128], lambda h, a, b: fkp[:, h, a:b],
                    lambda h, kb: fv[:, kb, 64 * h:64 * h + 64], 4, 64, lambda i: (0, 128 * i + 128),
                    p3, pt3, o3, fox_finish, [t_fq, t_fz, t_aug], [t_fk, t_fz, t_aug], [t_fv[t] for t in range(NT)], in5)
    bank_turn[0] = 0
    for t in range(NT):
        col_free[t] = mark()

    in6 = mark()
    mq = big("mq", [128, 4, 1024], 56)
    mk = big("mk", [128, 4, 1024], 72)
    mv_ = big("mv", [128, 8, 512], 8)
    ropeq = big("ropeq", [128, 1024], 0)
    rtmp = [Place(big(f"rtmp{i}", [128, 512], 24 + 2 * i)) for i in range(2)]
    t_rq = l_mem.start(SP, ropeq[64:128, :], I["c_ropeq"], in6)
    lat_t = flatten([list(x) for x in lat])
    MS = 96 ** -0.5
    t_mz = [DV.put(lambda e: e.memset(mk[96:128, :, :], 0.0), in6), DV.put(lambda e: e.memset(mq[96:128, :, :], 0.0), in6)]
    for h in range(4):
        t_mz.append(cp(mk[64:96, h, :], kpe[64:96, :], lat_t, in6))
    t_mq, t_mk, t_mv = [], [], []
    k = next_chunk()
    for h in range(4):
        for th in range(2):
            b = take_bank()
            cs = slice(512 * th, 512 * th + 512)
            tok = feature_unit(k, lambda i: (k.hi[:, 512 * i + 128 * h:512 * i + 128 * h + 128],
                                             k.lo[:, 512 * i + 128 * h:512 * i + 128 * h + 128]), 2,
                               lambda i: (CH[:, i, cs], CL[:, i, cs]), th, b, lat_t)
            t0 = act(mq[0:64, h, cs], b.ap[0:64, :], ACT.Copy, tok, in6, scale=MS)
            t1 = stt(mq[64:96, h, cs], b.ap[64:96, :], MS, ropeq[64:96, cs], ALU.mult, ALU.mult, tok, t0, t_rq, in6)
            g = rtmp[th]
            t2 = stt(g.ap[64:96, :], b.ap[96:128, :], MS, ropeq[96:128, cs], ALU.mult, ALU.mult, t1, g.free, in6)
            t3 = PL.put(lambda e, o=mq[64:96, h, cs], r=g.ap[64:96, :]: e.tensor_tensor(o, o, r, ALU.add), t1, t2, PL.last())
            g.free = narrow_pool[:] = [t3]
            b.free = [t2]
            t_mq += [t0, t3]
    chunk_done(k, tok)
    k = next_chunk()
    for h in range(4):
        for th in range(2):
            b = take_bank()
            cs = slice(512 * th, 512 * th + 512)
            tok = feature_unit(k, lambda i: (k.hi[:, 192 * h:192 * h + 128], k.lo[:, 192 * h:192 * h + 128]), 1,
                               lambda i: (CH[:, 2, cs], CL[:, 2, cs]), th, b, lat_t)
            t0 = act(mk[0:64, h, cs], b.ap[0:64, :], ACT.Copy, tok, in6)
            b.free = [t0]
            t_mk.append(t0)
    vh = k.hi[:, 0:768].rearrange("p (h c) -> p h c", h=4)[:, :, 64:192]
    vl = k.lo[:, 0:768].rearrange("p (h c) -> p h c", h=4)[:, :, 64:192]
    for t in range(NT):
        b = take_bank()
        cs = slice(128 * t, 128 * t + 128)
        tok = mm3(b.ap.rearrange("p (h c) -> p h c", h=4), CH[:, 2, cs], CL[:, 2, cs], vh, vl, True, True, b.free,
                  k.ready, lat_t, inc=True)
        t0 = act(mv_[:, t, :], b.ap, ACT.Copy, tok, in6)
        b.free = [t0]
        t_mv.append(t0)
    chunk_done(k, tok)
    in7 = mark()
    p4 = [Place(big(f"p4_{i}", [128, 1024], 24 + 4 * i)) for i in range(3)]
    pt4 = [Place(big(f"pt4_{i}", [128, 8, 128], 36 + 4 * i)) for i in range(2)]
    o4 = [Place(big(f"o4_{i}", [128, 512], 44 + 2 * i)) for i in range(2)]
    SQ4 = [Place(big(f"sq4_{i}", [128, 512], 48 + 2 * i)) for i in range(2)]
    for q_ in SQ4:
        q_.free = list(in7)

    def mla_finish(i, o, t_o, x):
        sq = SQ4[i % 2]
        r, t_r = group_norm(o.ap[:, :], 512, 0, sq.ap[:, :], t_o, sq.free)
        t_y = stt(o.ap[:, :], o.ap[:, :], r, gout[:, 0:512], ALU.mult, ALU.mult, t_r, t_gout)
        sq.free = [t_r]

        def turn_y():
            bank_turn[0] = 7
            o.free = [turn_in(o.ap, 4, i, 0, t_y)]
        later.append((x + 4, turn_y))

    heads_attention("mla", lambda h, i: mq[:, h, 128 * i:128 * i + 128], lambda h, a, b: mk[:, h, a:b],
                    lambda h, kb: mv_[:, kb, 128 * h:128 * h + 128], 4, 128, lambda i: (0, 128 * i + 128),
                    p4, pt4, o4, mla_finish, [t_mq, t_mz], [t_mk, t_mz], t_mv, in7)
    bank_turn[0] = 0

    stored = lambda: l_h[0].last() + l_h[1].last()
    pas = Passage(h2, None, I["norm_cross_2"][0], h3, after=mark() + stored())
    token_stage(eight, lambda j, p: p, lambda j, p, t: col_ready[t], pas)

    xq = big("xq", [128, 4, 1024], 16)
    MH = big("mh", [128, 8, 256], 32, F32R)
    ML = big("ml", [128, 8, 256], 40, F32R)
    xk = big("xk", [128, 4, 256], 48)
    xv = big("xv", [128, 2, 512], 52)
    in8 = mark()
    t_xq = []

    def xq_out(m):
        def go(th, b, tok):
            t_xq.append(act(xq[:, m, 512 * th:512 * th + 512], b.ap, ACT.Copy, tok, in8, scale=128 ** -0.5))
            return [t_xq[-1]]
        return go

    in9 = in8 + stored()
    memx = [big(f"memx{i}", [128, 1024], 64 + 4 * i) for i in range(2)]
    gmem = big("gmem", [128, 1024], 80)
    memn = [big(f"memn{i}", [128, 1024], 72 + 4 * i) for i in range(2)]
    for i in range(2):
        l_mem.start(SP, memx[i][:, :], I["mem_2"][0][128 * i:128 * i + 128, :], in9)
    t_g = l_mem.start(SP, gmem[:, :], I["norm_mem_2"][0].partition_broadcast(128), in9)
    t_mh = []
    feature_group([xq_out(0), xq_out(1)])
    t_n = []
    for i in range(2):
        s, v = col(), col()
        t_s = act(memn[i][:, :], memx[i][:, :], ACT.Square, t_g, in9, accum_out=s)
        t_v = ts(v, s, 1.0 / D, EPS, ALU.mult, ALU.add, t_s)
        r, t_r = inv_sqrt(v, t_v)
        t_n.append(stt(memn[i][:, :], memx[i][:, :], r, gmem[:, :], ALU.mult, ALU.mult, t_r))
    feature_group([xq_out(2), xq_out(3)])
    for i in range(2):
        for g in range(2):
            b = take_bank()
            for j in range(4):
                kk = 4 * g + j
                t_m = tr(b.ap[:, 128 * j:128 * j + 128], memn[i][:, 128 * kk:128 * kk + 128], t_n[i], b.free,
                         inc=(j == 3))
            t_mh += split_in(b, 4, MH[:, 4 * g:4 * g + 4, 128 * i:128 * i + 128],
                             ML[:, 4 * g:4 * g + 4, 128 * i:128 * i + 128], t_m, in8)
    t_xk, t_xv = [], []
    for m in range(4):
        k = next_chunk()
        b = take_bank()
        for i in range(8):
            tok = mm3(b.ap[:, 0:256], k.hi[:, 128 * i:128 * i + 128], k.lo[:, 128 * i:128 * i + 128], MH[:, i, :],
                      ML[:, i, :], i == 0, i == 7, k.ready, b.free, t_mh, inc=(i == 7))
        t0 = act(xk[:, m, :], b.ap[:, 0:256], ACT.Copy, tok, in8)
        b.free = [t0]
        t_xk.append(t0)
        chunk_done(k, tok)
    vb = [take_bank(), take_bank()]
    for i in range(0, 8, 2):
        k = next_chunk()
        for ii in range(2):
            for t in range(2):
                tok = mm3(vb[t].ap, MH[:, i + ii, 128 * t:128 * t + 128], ML[:, i + ii, 128 * t:128 * t + 128],
                          k.hi[:, 512 * ii:512 * ii + 512], k.lo[:, 512 * ii:512 * ii + 512], i + ii == 0, i + ii == 7,
                          k.ready, vb[t].free, inc=(t == 1))
        chunk_done(k, tok)
    for t in range(2):
        t0 = cp(xv[:, t, :], vb[t].ap, tok, in8)
        vb[t].free = [t0]
        t_xv.append(t0)

    in10 = mark() + stored()
    p5 = [Place(big(f"p5_{i}", [128, 256], i)) for i in range(3)]
    pt5 = [Place(big(f"pt5_{i}", [128, 2, 128], 3 + i)) for i in range(2)]
    o5 = [Place(big(f"o5_{i}", [128, 512], 6 + 2 * i)) for i in range(2)]

    def cross_finish(i, o, t_o, x):
        def turn_y():
            bank_turn[0] = 7
            col_ready[i] = []
            o.free = [turn_in(o.ap, 4, i, 0, t_o)]
        later.append((x + 3, turn_y))

    heads_attention("cross", lambda h, i: xq[:, h, 128 * i:128 * i + 128], lambda h, a, b: xk[:, h, a:b],
                    lambda h, kb: xv[:, kb, 128 * h:128 * h + 128], 4, 128, lambda i: (0, 256),
                    p5, pt5, o5, cross_finish, t_xq, t_xk, t_xv, in10)
    bank_turn[0] = 0

    pas = Passage(h3, None, I["norm_ffn_2"][0], h4, after=mark() + stored())
    token_stage([list(range(4))] * 2, lambda j, p: p, lambda j, p, t: col_ready[t], pas)
    ffn(h4, None, I["final_norm_2"], None, final=True)

    for l in l_out + l_h + l_sk:
        for token in l.last():
            SP.items.append(([token], None, False))

    block = ctx.enter_context(nc.Block())

    @block.tensor
    def _(e):
        PE.run(e)

    @block.scalar
    def _(e):
        AC.run(e)

    @block.vector
    def _(e):
        DV.run(e)

    @block.gpsimd
    def _(e):
        PL.run(e)

    @block.sync
    def _(e):
        for need, fn, inc in SP.items:
            for s_, value in need:
                e.wait_ge(s_, value)
            if fn is not None:
                fn(e)


_INS = ["x", "mix_pre_g", "mix_post_g", "ffn_pre_g", "ffn_post_g", "w_in", "conv_dw", "conv_dw_b", "conv_ln_g",
        "conv_ln_b", "w_conv_pw", "attn_sinks", "rel_bias", "w_out", "w_gate", "w_up", "w_down", "mem_2",
        "norm_mix_2", "w_in_2", "q_norm_2", "w_uq_2", "kv_norm_2", "w_ukv_2", "f_bias_2", "rel_bias_2", "out_norm_2",
        "w_o_2", "norm_cross_2", "norm_mem_2", "w_cq_2", "w_ckv_2", "w_co_2", "norm_ffn_2", "w_gu_2", "w_down_2",
        "final_norm_2"]


def kernel(**inputs):
    import numpy as _np
    import concourse.bacc as _bacc
    from concourse import mybir as _mybir
    from concourse.bass_utils import run_bass_kernel_spmd as _run

    nc = _bacc.Bacc("TRN2", target_bir_lowering=False, num_devices=1)
    arrays, args = {}, {}
    given = {name: _np.ascontiguousarray(inputs[name]) for name in _INS}
    given["x"] = given["x"].reshape(1024, 1024)
    given.update(constants())
    for name, a in given.items():
        arrays[f"in_{name}_dram"] = a
        args[name] = nc.dram_tensor(f"in_{name}_dram", a.shape, _mybir.dt.from_np(a.dtype), kind="ExternalInput").ap()
    out = nc.dram_tensor("out_0_dram", (1024, 1024), _mybir.dt.float32, kind="ExternalOutput").ap()
    block_kernel(nc, args, out)
    r = _run(nc, [arrays], core_ids=[0])
    return r.results[0]["out_0_dram"].reshape(1, 1024, 1024)
```

```python
import math
from contextlib import ExitStack

import numpy as np

import concourse.bass as bass
from concourse import mybir

F32 = mybir.dt.float32
F32R = mybir.dt.float32r
ACT = mybir.ActivationFunctionType
ALU = mybir.AluOpType
AX = mybir.AxisListType

S = 1024
D = 1024
NT = 8
FF = 2816
NF = FF // 128
EPS = 1e-6
NEG = -1e30
TAPS = 31
KB = 1024

class Queue:

    def __init__(self, sem):
        self.sem, self.items, self.count, self.met, self.own = sem, [], 0, {}, 0

    def put(self, fn, *waits, inc=True, stream=False):
        need = {}
        for sem, value in flat(waits):
            if self.met.get(sem.name, 0) < value:
                self.met[sem.name] = value
                need[sem.name] = (sem, value)
        if inc:
            self.count += 1
        if not stream:
            self.own = self.count
        self.items.append((list(need.values()), fn, inc))
        return (self.sem, self.count) if inc else None

    def last(self):
        return [(self.sem, self.own)] if self.own else []

    def run(self, eng):
        for need, fn, inc in self.items:
            for sem, value in need:
                eng.wait_ge(sem, value)
            ins = fn(eng)
            if inc:
                ins.then_inc(self.sem, 1)

class Landing:

    def __init__(self, sem):
        self.sem, self.count = sem, 0

    def start(self, queue, out, in_, *waits, **how):
        self.count += 16
        sem = self.sem
        queue.put(lambda e: e.dma_start(out, in_, **how).then_inc(sem, 16), *waits, inc=False)
        return (sem, self.count)

    def last(self):
        return [(self.sem, self.count)] if self.count else []

class Place:

    def __init__(self, ap, index=0):
        self.ap, self.index, self.free = ap, index, []

class Ring:
    def __init__(self, places):
        self.places, self.n = places, 0

    def take(self):
        self.n += 1
        return self.places[(self.n - 1) % len(self.places)]

def flat(tokens):
    for t in tokens:
        if t is None:
            continue
        if isinstance(t, tuple) and not isinstance(t[0], (tuple, list)):
            yield t
        else:
            yield from flat(t)

def bucket_of(dist):
    d = np.maximum(dist, 1).astype(np.float32)
    large = 16 + (np.log(d / np.float32(16)) / np.float32(math.log(8.0)) * np.float32(16)).astype(np.int32)
    return np.where(dist < 16, dist, np.minimum(large, 31))

def constants():
    ident = np.eye(128, dtype=np.float32)
    oh1 = np.zeros((33, 383), np.float32)
    for j in range(383):
        dist = 255 - j
        if 0 <= dist < 128:
            oh1[int(bucket_of(np.array([dist]))[0]), j] = 1.0
        else:
            oh1[32, j] = NEG
    oh2 = np.zeros((192, 767), np.float32)
    for j in range(767):
        oh2[min(max(639 - j, -63), 128) + 63, j] = 1.0
    q = np.arange(128)
    causal = np.where(q[None, :] <= q[:, None], 0.0, NEG).astype(np.float32)
    pos = np.arange(S, dtype=np.float32)
    inv = np.power(np.float32(10000.0), -np.arange(0, 32, 2, dtype=np.float32) / np.float32(32)).astype(np.float32)
    ang = (pos[:, None] * inv[None, :]).astype(np.float32)
    cos, sin = np.cos(ang).astype(np.float32), np.sin(ang).astype(np.float32)
    ropeq = np.concatenate([cos.T, cos.T, -sin.T, sin.T], 0)
    ropek = np.concatenate([cos, cos, -sin, sin], 1).reshape(NT, 128, 64).transpose(1, 0, 2)
    return {"c_ident": ident, "c_oh1": oh1, "c_oh2": oh2, "c_causal": causal,
            "c_ropeq": np.ascontiguousarray(ropeq), "c_ropek": np.ascontiguousarray(ropek)}

def block_kernel(nc, I, out):
    ctx = ExitStack()
    with ctx:
        build(nc, ctx, I, out)

def build(nc, ctx, I, out_dram):
    BASE = 16512
    RING = 5
    off = {"stage": BASE, "wh": BASE + 8 * KB, "wl": BASE + (8 + 4 * RING) * KB}
    off["ah"] = off["wl"] + 4 * RING * KB
    off["al"] = off["ah"] + 32 * KB
    off["sg"] = off["al"] + 32 * KB
    off["big"] = off["sg"] + 4 * KB
    off["small"] = off["big"] + 88 * KB
    BIG = off["big"]

    def sb(name, shape, at, dt=F32):
        return nc.alloc_sbuf_tensor_at(name, shape, dt, offset=at)

    def big(name, shape, kb, dt=F32):
        return sb(name, shape, BIG + int(kb * KB), dt)

    def sem(name):
        return ctx.enter_context(nc.semaphore(name))

    PE, AC, DV, PL, SP = (Queue(sem("s_" + n)) for n in ("pe", "act", "dve", "pool", "sp"))

    def mark():
        return PE.last() + AC.last() + DV.last() + PL.last()

    P = ctx.enter_context(nc.psum_tensor("P", [128, 8, 512], F32))
    PF = P[:, :, :].rearrange("p b n -> p (b n)")
    banks = [Place(P[:, i, :], i) for i in range(8)]
    bank_turn = [0]

    def take_bank():
        b = banks[bank_turn[0] % 8]
        bank_turn[0] += 1
        return b

    stage = [sb(f"stage{i}", [128, 1024], off["stage"] + 4 * KB * i) for i in range(2)]
    WH = [sb(f"wh{i}", [128, 1024], off["wh"] + 4 * KB * i, F32R) for i in range(RING)]
    WL = [sb(f"wl{i}", [128, 1024], off["wl"] + 4 * KB * i, F32R) for i in range(RING)]
    AH = sb("ah", [128, 8, 1024], off["ah"], F32R)
    AL = sb("al", [128, 8, 1024], off["al"], F32R)
    sm = [off["small"]]

    def small(name, n):
        t = sb(name, [128, n], sm[0])
        sm[0] += 4 * n
        return t

    ident = small("ident", 128)
    nhalf = small("nhalf", 8)
    epsc = small("epsc", 8)
    sinks = small("sinks", 8)
    nsink = small("nsink", 8)
    stats = small("stats", 480)
    ra = small("ra", 64)[:, :].rearrange("p (a b) -> p a b", a=2)
    causal = small("causal", 128)
    stat_at = [0]

    def col(n=1):
        if stat_at[0] + n > 480:
            stat_at[0] = 0
        stat_at[0] += n
        return stats[:, stat_at[0] - n:stat_at[0]]

    l_const = Landing(sem("l_const"))
    l_stage = [Landing(sem(f"l_stage{i}")) for i in range(2)]
    l_xr = [Landing(sem(f"l_xr{i}")) for i in range(2)]
    l_gb = [Landing(sem(f"l_gb{i}")) for i in range(2)]
    l_h = [Landing(sem(f"l_h{i}")) for i in range(2)]
    l_bias = Landing(sem("l_bias"))
    l_sk = [Landing(sem(f"l_sk{i}")) for i in range(3)]
    l_aug = Landing(sem("l_aug"))
    l_out = [Landing(sem(f"l_out{i}")) for i in range(4)]
    l_misc = Landing(sem("l_misc"))
    l_mem = Landing(sem("l_mem"))
    l_kv = Landing(sem("l_kv"))

    h1 = nc.dram_tensor("h1", (S, D), F32, kind="Internal").ap()
    h2 = nc.dram_tensor("h2", (S, D), F32, kind="Internal").ap()
    h3 = nc.dram_tensor("h3", (S, D), F32, kind="Internal").ap()
    h4 = nc.dram_tensor("h4", (S, D), F32, kind="Internal").ap()
    kv_dram = nc.dram_tensor("kv_dram", (2, 128, 1024), F32, kind="Internal").ap()
    sk1 = nc.dram_tensor("sk1", (8, 128 * 384), F32, kind="Internal")
    sk2 = nc.dram_tensor("sk2", (4, 128 * 768), F32, kind="Internal")

    t_ident = l_const.start(SP, ident[:, :], I["c_ident"])
    t_eps = DV.put(lambda e: e.memset(epsc[:, :], EPS))
    t_nhalf = DV.put(lambda e: e.memset(nhalf[:, :], -0.5))

    def mm(out, l, r, start, stop, *waits, inc=False):
        return PE.put(lambda e: e.matmul(out, l, r, start=start, stop=stop), *waits, inc=inc)

    def mm3(out, lh, ll, rh, rl, start, stop, *waits, inc=False):
        mm(out, lh, rh, start, False, *waits)
        mm(out, lh, rl, False, False)
        return mm(out, ll, rh, False, stop, inc=inc)

    def tr(out, in_, *waits, inc=False):
        p = in_.shape[0]
        return PE.put(lambda e: e.transpose(out, in_, ident[0:p, 0:p]), t_ident, *waits, inc=inc)

    def act(out, in_, func, *waits, **kw):
        return AC.put(lambda e: e.activation(out, in_, func, **kw), *waits)

    def tt(out, a, b, op, *waits):
        return DV.put(lambda e: e.tensor_tensor(out, a, b, op), *waits)

    def ts(out, a, s1, s2, op0, op1, *waits):
        if op1 is None:
            return DV.put(lambda e: e.tensor_scalar(out, a, s1, None, op0), *waits)
        return DV.put(lambda e: e.tensor_scalar(out, a, s1, s2, op0, op1), *waits)

    def stt(out, a, s, b, op0, op1, *waits):
        return DV.put(lambda e: e.scalar_tensor_tensor(out, a, s, b, op0, op1), *waits)

    def cp(out, in_, *waits):
        return DV.put(lambda e: e.tensor_copy(out, in_), *waits)

    def inv_sqrt(v, *waits):
        r = col(v.shape[1])
        n = v.shape[1]
        return r, PL.put(lambda e: e.tensor_tensor(r, v, nhalf[:, 0:n], ALU.pow), t_nhalf, *waits)

    def inv_rms(s, more, *waits):
        r, v = col(), col()
        t_v = PL.put(lambda e: e.tensor_tensor(v, s, more, ALU.add), t_eps, *waits)
        return r, PL.put(lambda e: e.tensor_tensor(r, v, nhalf[:, 0:1], ALU.pow), t_nhalf, t_v)

    RT = D ** -0.5

    plan = []
    sent = [0]
    used = [0]
    w_slots = [Place(None, i) for i in range(RING)]
    s_slots = [Place(stage[i], i) for i in range(2)]
    ready = {}

    landed = {}
    narrow_pool = []

    def load_chunk():
        c = len(landed)
        if c < len(plan):
            st = s_slots[c % 2]
            for dst, src in plan[c][1]:
                landed[c] = l_stage[c % 2].start(SP, dst(st.ap), src, st.free)

    def send_chunk():
        c = sent[0]
        sent[0] += 1
        n = plan[c][0]
        st, sl = s_slots[c % 2], w_slots[c % RING]
        i = sl.index
        t_hi = AC.put(lambda e: e.activation(WH[i][:, 0:n], st.ap[:, 0:n], ACT.Copy), landed[c], sl.free, stream=True)
        t_lo = PL.put(lambda e: e.tensor_tensor(WL[i][:, 0:n], st.ap[:, 0:n], WH[i][:, 0:n].bitcast(F32), ALU.subtract),
                      landed[c], t_hi, sl.free, narrow_pool, stream=True)
        st.free = [t_hi, t_lo]
        ready[c] = [t_hi, t_lo]
        load_chunk()

    class Chunk:
        pass

    def next_chunk():
        c = used[0]
        used[0] += 1
        while sent[0] <= c:
            send_chunk()
        k = Chunk()
        k.slot = w_slots[c % RING]
        k.hi, k.lo, k.ready = WH[c % RING], WL[c % RING], ready.pop(c)
        return k

    done = [0]

    def run_ahead(most=1, margin=0):
        while most and sent[0] < min(done[0] + RING - margin, len(plan)):
            send_chunk()
            most -= 1

    def chunk_done(k, token):
        k.slot.free = [token]
        done[0] += 1
        run_ahead(1, 1)

    def chunks_done(ks, token):
        for k in ks:
            k.slot.free = [token]
            done[0] += 1
        run_ahead(2)

    def cols_chunk(w, c0, nk=8, n=128):
        src = w[:, c0:c0 + n].rearrange("(k p) c -> p k c", p=128)
        return (nk * n, [(lambda s: s[:, 0:nk * n].rearrange("p (k c) -> p k c", k=nk), src)])

    def rows_chunk(w, ks, ranges):
        width = sum(b - a for a, b in ranges)
        parts = []
        for i, k in enumerate(ks):
            at = i * width
            for a, b in ranges:
                parts.append((lambda s, at=at, n=b - a: s[:, at:at + n], w[k * 128:(k + 1) * 128, a:b]))
                at += b - a
        return (len(ks) * width, parts)

    w_in, w_out, w_pw = I["w_in"], I["w_out"], I["w_conv_pw"]
    w_in2, w_uq, w_ukv, w_o = I["w_in_2"][0], I["w_uq_2"][0], I["w_ukv_2"][0], I["w_o_2"][0]
    w_cq, w_ckv, w_co, w_gu = I["w_cq_2"][0], I["w_ckv_2"][0], I["w_co_2"][0], I["w_gu_2"][0]

    for c in range(4):
        plan.append(cols_chunk(w_in, 1280 + 128 * c))
        plan.append(cols_chunk(w_in, 768 + 128 * c))
    for c0 in (512, 640, 0, 128, 256, 384):
        plan.append(cols_chunk(w_in, c0))
    for m in range(4):
        plan.append(cols_chunk(w_ckv, 128 * m))
    for i in range(0, 8, 2):
        plan.append(rows_chunk(w_ckv, [i, i + 1], [(512, 1024)]))
    for m in range(4):
        plan.append(cols_chunk(w_pw, 128 * m, nk=4))

    def plan_tok(w, orders):
        for j, order in enumerate(orders):
            for i in range(0, len(order), 2):
                plan.append(rows_chunk(w, order[i:i + 2], [(512 * j, 512 * j + 512)]))

    down_order = [list(range(NF)), list(range(14, NF)) + list(range(14))]

    def plan_ffn(wg, g0, wu, u0, wd):
        for m in range(NF):
            plan.append(cols_chunk(wg, g0 + 128 * m))
            plan.append(cols_chunk(wu, u0 + 128 * m))
        plan_tok(wd, down_order)

    plan_tok(w_out, [list(range(8))] * 2)
    plan_ffn(I["w_gate"], 0, I["w_up"], 0, I["w_down"])
    for c0 in (1188, 1316, 1444, 1572):
        plan.append(cols_chunk(w_in2, c0))
    for i in range(0, 8, 4):
        plan.append(rows_chunk(w_in2, range(i, i + 4), [(1700, 1956)]))
    for i in range(0, 8, 2):
        plan.append(rows_chunk(w_in2, [i, i + 1], [(0, 416), (1184, 1188)]))
    for i in range(0, 8, 4):
        plan.append(rows_chunk(w_in2, range(i, i + 4), [(928, 1184)]))
    for c0 in (416, 544, 672, 800):
        plan.append(cols_chunk(w_in2, c0))
    uq_parts = []
    for k in range(2):
        src = w_uq[k * 128:(k + 1) * 128, :].rearrange("p (h c) -> p h c", h=4)
        for a, b, at in ((0, 96, 0), (80, 96, 96), (64, 80, 112)):
            uq_parts.append((lambda s, k=k, at=at, n=b - a: s[:, 512 * k:512 * k + 512].rearrange(
                "p (h c) -> p h c", h=4)[:, :, at:at + n], src[:, :, a:b]))
    plan.append((1024, uq_parts))
    plan.append((768, [(lambda s: s[:, 0:768], w_ukv)]))
    plan_tok(w_o, [list(range(8))] * 2)
    for m in range(4):
        plan.append(cols_chunk(w_cq, 128 * m))
    plan_tok(w_co, [list(range(4))] * 2)
    plan_ffn(w_gu, 0, w_gu, FF, I["w_down_2"][0])

    col_ready = [[] for _ in range(NT)]
    col_free = [[] for _ in range(NT)]

    def turn_in(src, n, t, k0, *waits, ring=None):
        made, last = [], None
        for g in range(0, n, 4):
            w = min(4, n - g)
            b = ring.take() if ring else take_bank()
            for j in range(w):
                last = tr(b.ap[:, 128 * j:128 * j + 128], src[:, 128 * (g + j):128 * (g + j) + 128],
                          b.free, *waits, inc=(j == w - 1))
            made += split_in(b, w, AH[:, k0 + g:k0 + g + w, 128 * t:128 * t + 128],
                             AL[:, k0 + g:k0 + g + w, 128 * t:128 * t + 128], last, col_free[t])
        col_ready[t] = col_ready[t] + made
        return last

    def split_in(b, w, hi, lo, *waits):
        v = b.ap[:, 0:128 * w].rearrange("p (k c) -> p k c", k=w)
        t_hi = act(hi, v, ACT.Copy, *waits)
        t_lo = tt(lo, v, hi.bitcast(F32), ALU.subtract, t_hi, *waits)
        b.free = [t_lo]
        return [t_hi, t_lo]

    pending = []

    def flush():
        while pending:
            pending.pop(0)()

    def feature_unit(k, lhs, nk, rhs, th, b, *waits):
        for i in range(nk):
            lh, ll = lhs(i)
            rh, rl = rhs(i)
            tok = mm3(b.ap, lh, ll, rh, rl, i == 0, i == nk - 1, k.ready, b.free, *waits, inc=(i == nk - 1))
        return tok

    def act_cols(th, nk=8):
        return lambda i: (AH[:, i, 512 * th:512 * th + 512], AL[:, i, 512 * th:512 * th + 512])

    def flatten(tokens):
        return list(flat([tokens]))

    def feature_group(evacs, between=None):
        ks = [next_chunk() for _ in evacs]
        for th in range(2):
            if th == 1:
                flush()
                run_ahead()
            for k, evac in zip(ks, evacs):
                v = lambda i, k=k: (k.hi[:, 128 * i:128 * i + 128], k.lo[:, 128 * i:128 * i + 128])
                b = take_bank()
                half = range(4 * th, 4 * th + 4)
                tok = feature_unit(k, v, 8, act_cols(th), th, b, [col_ready[t] for t in half])
                for t in half:
                    col_free[t] = [tok]
                b.free = flatten(evac(th, b, tok))
                if th == 1:
                    chunk_done(k, tok)
                elif pending and k is not ks[-1]:
                    pending.pop(0)()
                if between:
                    between()
        return tok

    M0 = [big(f"m0_{t}", [128, 512], 56 + 2 * t) for t in range(NT)]
    GB = [big(f"gb{i}", [128, 1024], 72 + 4 * i) for i in range(2)]
    XR = [Place(big(f"xr{i}", [128, 1024], 80 + 4 * i)) for i in range(2)]
    HT = [Place(big(f"ht{i}", [128, 1024], 4 * i)) for i in range(2)]
    XN = [Place(big(f"xn{i}", [128, 1024], at)) for i, at in enumerate((8, 12, 56, 60))]

    class Passage:

        def __init__(self, x, g_post, g_pre, h, final=False, after=(), xfree=()):
            self.x, self.h, self.final, self.g_post = x, h, final, g_post
            self.after = list(after)
            self.t_gb = [None, None]
            if g_post is not None:
                self.t_gb[0] = l_gb[0].start(SP, GB[0][:, :], g_post.partition_broadcast(128), self.after)
            self.t_gb[1] = l_gb[1].start(SP, GB[1][:, :], g_pre.partition_broadcast(128), self.after)
            for r in (XR, HT, XN):
                for p in r:
                    p.free = list(self.after)
            self.t_x, self.m0, self.ss0, self.r1, self.r2 = {}, {}, {}, {}, {}
            self.t_h, self.t_xn = {}, {}
            for t in range(2):
                self.load(t)

        def load(self, t):
            if t < NT:
                self.t_x[t] = l_xr[t % 2].start(SP, XR[t % 2].ap[:, :], self.x[128 * t:128 * t + 128, :], XR[t % 2].free)

        def keep(self, t, b, tok, *waits):
            if self.g_post is None:
                t_m = cp(M0[t][:, :], b.ap, tok, self.after, *waits)
            else:
                s, v = col(), col()
                t_s = act(M0[t][:, :], b.ap, ACT.Square, tok, self.after, *waits, scale=RT, accum_out=s)
                t_m = tt(M0[t][:, :], b.ap, GB[0][:, 0:512], ALU.mult, t_s, self.t_gb[0])
                self.ss0[t] = (v, ts(v, s, EPS, None, ALU.add, None, t_s))
            b.free = [t_m]
            self.m0[t] = t_m

        def a(self, t, b, tok):
            self.tok = tok
            if self.g_post is None:
                return
            s = col()
            v0, t_v0 = self.ss0[t]
            j = XN[t % 4]
            below = self.t_h[t - 1] if t in (2, 3) else None
            t_s = act(j.ap[:, 0:512], b.ap, ACT.Square, tok, j.free, below, scale=RT, accum_out=s)
            self.t_a = t_s
            self.r1[t] = inv_rms(s, v0, t_s, t_v0)

        def b(self, t, b, tok):
            H, X = HT[t % 2], XR[t % 2]
            h = H.ap
            if self.g_post is not None:
                r, t_r = self.r1[t]
                stt(h[:, 0:512], M0[t][:, :], r, X.ap[:, 0:512], ALU.mult, ALU.add, t_r, self.m0[t], self.t_x[t], H.free)
                t_u = stt(h[:, 512:], b.ap, r, GB[0][:, 512:], ALU.mult, ALU.mult, tok, self.t_a)
                b.free = [t_u]
                t_h = tt(h[:, 512:], h[:, 512:], X.ap[:, 512:], ALU.add, t_u)
            else:
                tt(h[:, 0:512], M0[t][:, :], X.ap[:, 0:512], ALU.add, self.m0[t], self.t_x[t], H.free)
                t_h = tt(h[:, 512:], b.ap, X.ap[:, 512:], ALU.add, tok)
                b.free = [t_h]
            X.free = [t_h]
            self.load(t + 2)
            self.t_h[t] = t_h

        def squares(self, t):
            H, s = HT[t % 2], col()
            t_s = act(XN[t % 4].ap[:, :], H.ap[:, :], ACT.Square, self.t_h[t], XN[t % 4].free, scale=RT, accum_out=s)
            H.free = [t_s]
            if self.h is not None:
                H.free.append(l_h[t % 2].start(AC, self.h[128 * t:128 * t + 128, :], H.ap[:, :], self.t_h[t]))
            self.r2[t] = inv_rms(s, epsc[:, 0:1], t_s)

        def c(self, t):
            r, t_r = self.r2[t]
            X, H = XN[t % 4], HT[t % 2]
            self.t_xn[t] = stt(X.ap[:, :], H.ap[:, :], r, GB[1][:, :], ALU.mult, ALU.mult, t_r, self.t_gb[1])
            H.free.append(self.t_xn[t])
            if self.final:
                X.free = [l_out[t % 4].start(SP, out_dram[128 * t:128 * t + 128, :], X.ap[:, :], self.t_xn[t])]

        def d(self, t):
            if not self.final:
                col_ready[t] = []
                XN[t % 4].free = [turn_in(XN[t % 4].ap, 8, t, 0, self.t_xn[t])]

    def token_stage(order, slot, col_tok, passage, extra=None, keep_waits=()):
        last_use = {}
        for j in range(2):
            ks = order[j]
            tail = 2 if j == 0 else min(6, len(ks))
            held = []
            for t in range(NT):
                banks[t].open = False
            body = len(ks) - tail
            for i in range(0, body, 2):
                k = next_chunk()
                for ii in range(2):
                    p = i + ii
                    if extra:
                        extra(j, p)
                    for t in range(NT):
                        s = slot(j, p)
                        tok = mm3(banks[t].ap, AH[:, s, 128 * t:128 * t + 128], AL[:, s, 128 * t:128 * t + 128],
                                  k.hi[:, 512 * ii:512 * ii + 512], k.lo[:, 512 * ii:512 * ii + 512], p == 0, False,
                                  k.ready, banks[t].free if p == 0 else None, col_tok(j, p, t), inc=(t == NT - 1))
                    last_use[s] = tok
                    if extra:
                        extra.used(j, p, tok)
                chunk_done(k, tok)
            chunks = [next_chunk() for _ in range(tail // 2)]
            if extra:
                for p in range(body, len(ks)):
                    extra(j, p)
            for t in range(NT):
                for p in range(body, len(ks)):
                    k, ii, s = chunks[(p - body) // 2], (p - body) % 2, slot(j, p)
                    tok = mm3(banks[t].ap, AH[:, s, 128 * t:128 * t + 128], AL[:, s, 128 * t:128 * t + 128],
                              k.hi[:, 512 * ii:512 * ii + 512], k.lo[:, 512 * ii:512 * ii + 512], p == 0,
                              p == len(ks) - 1, k.ready, banks[t].free if p == 0 else None, col_tok(j, p, t),
                              inc=(p == len(ks) - 1))
                if j == 0:
                    passage.keep(t, banks[t], tok, *keep_waits)
                    if t == NT - 1:
                        for k in chunks:
                            chunk_done(k, tok)
                        if extra:
                            for p in range(body, len(ks)):
                                extra.used(j, p, tok)
                else:
                    col_free[t] = [tok]
                    passage.a(t, banks[t], tok)
                    if t == 2:
                        run_ahead()
                    if t >= 2:
                        passage.c(t - 2)
                    if t >= 3:
                        bank_turn[0] = t - 3
                        passage.d(t - 3)
                    if t >= 1:
                        passage.squares(t - 1)
                    passage.b(t, banks[t], tok)
        passage.squares(NT - 1)
        passage.c(NT - 2)
        passage.c(NT - 1)
        chunks_done(chunks, tok)
        bank_turn[0] = 0

        if not passage.final:
            for t in range(5, NT):
                pending.append(lambda t=t: passage.d(t))

    def softmax_rows(src, dst, n, nm, t_nm, waits=(), scale=1.0):
        rs = col()
        return rs, act(dst, src, ACT.Exp, t_nm, *waits, bias=nm, accum_out=rs)

    SGT = [sb(f"sg{i}", [128, 512], off["sg"] + 2 * KB * i) for i in range(2)]
    SGR = Ring([Place(t) for t in SGT])

    oh1 = big("oh1", [33, 383], 20)
    rb1 = big("rb1", [33, 8], 22)
    oh2a = big("oh2a", [128, 767], 24)
    oh2b = big("oh2b", [64, 767], 28)
    rb2a = big("rb2a", [128, 4], 32)
    rb2b = big("rb2b", [64, 4], 32.5)
    ones_row = DV.put(lambda e: e.memset(rb1[32:33, :], 1.0))
    cw = big("cw", [34, 512], 33)

    x0 = [Place(big(f"x0_{i}", [128, 1024], at)) for i, at in enumerate((56, 60, 64, 68, 80, 84))]
    l_x0 = l_xr + l_h + l_out
    n0 = [Place(big(f"n0_{i}", [128, 1024], 4 * i)) for i in range(4)]
    t_x0 = {}

    def load0(t):
        if t < NT:
            p = x0[t % 6]
            t_x0[t] = l_x0[t % 6].start(SP, p.ap[:, :], I["x"][128 * t:128 * t + 128, :], p.free)

    stat0 = {}

    def square0(t):
        X, N = x0[t % 6], n0[t % 4]
        s = col()
        t_s = act(N.ap[:, :], X.ap[:, :], ACT.Square, t_x0[t], N.free, scale=RT, accum_out=s)
        stat0[t] = inv_rms(s, epsc[:, 0:1], t_s)

    def norm0(t):
        X, N = x0[t % 6], n0[t % 4]
        r, t_r = stat0[t]
        t_n = stt(N.ap[:, :], X.ap[:, :], r, GB[1][:, :], ALU.mult, ALU.mult, t_r, t_g0)
        X.free = [t_n]
        load0(t + 6)
        return t_n

    load0(0)
    t_g0 = l_gb[1].start(SP, GB[1][:, :], I["mix_pre_g"].partition_broadcast(128))
    for t in range(1, 4):
        load0(t)
    load_chunk()
    load_chunk()
    for t in range(4, 6):
        load0(t)
    l_misc.start(SP, cw[0:31, :], I["conv_dw"])
    for i, name in enumerate(("conv_dw_b", "conv_ln_g", "conv_ln_b")):
        l_misc.start(SP, cw[31 + i:32 + i, :], I[name].rearrange("(a n) -> a n", a=1))
    l_misc.start(SP, oh1[:, :], I["c_oh1"])
    l_misc.start(SP, rb1[0:32, :], I["rel_bias"])
    l_misc.start(SP, oh2a[:, :], I["c_oh2"][0:128, :])
    l_misc.start(SP, oh2b[:, :], I["c_oh2"][128:192, :])
    rel2 = I["rel_bias_2"][0]
    l_misc.start(SP, rb2a[:, :], rel2[:, 0:128].rearrange("h r -> r h"), allow_slow_non_contiguous=True)
    l_misc.start(SP, rb2b[:, :], rel2[:, 128:192].rearrange("h r -> r h"), allow_slow_non_contiguous=True)
    t_misc = l_misc.start(SP, sinks[:, :], I["attn_sinks"].partition_broadcast(128))

    t_n0 = {}
    for t in range(3):
        square0(t)
    t_n0[0] = norm0(0)
    for t in range(4):
        if t + 1 < 4:
            t_n0[t + 1] = norm0(t + 1)
        n0[t].free = [turn_in(n0[t].ap, 8, t, 0, t_n0[t])]
        if t == 0:
            square0(3)
        if t in (0, 2):
            send_chunk()
    square0(4)
    square0(5)
    for t in range(4, NT):
        t_n0[t] = norm0(t)
        if t < 6:
            square0(t + 2)

    def turn0(t):
        n0[t % 4].free = [turn_in(n0[t % 4].ap, 8, t, 0, t_n0[t])]

    for t in range(4, NT):
        pending.append(lambda t=t: turn0(t))

    def bias_tables():
        b, g = take_bank(), SGR.take()
        t_m = mm(b.ap[0:8, 0:383], rb1[0:33, :], oh1[:, :], True, True, t_misc, ones_row, b.free, inc=True)
        t_c = cp(g.ap[0:8, 0:383], b.ap[0:8, 0:383], t_m, g.free)
        b.free = [t_c]
        g.free = [l_sk[0].start(SP, bass.AP(sk1, 0, [[128 * 384, 8], [384, 128], [1, 383]]),
                               g.ap[0:8, 0:383].unsqueeze(1).to_broadcast([8, 128, 383]), t_c)]
        for i, (a, n) in enumerate(((0, 512), (512, 255))):
            b, g = take_bank(), SGR.take()
            mm(b.ap[0:4, 0:n], rb2a[:, :], oh2a[:, a:a + n], True, False, t_misc, b.free)
            t_m = mm(b.ap[0:4, 0:n], rb2b[:, :], oh2b[:, a:a + n], False, True, inc=True)
            t_c = cp(g.ap[0:4, 0:n], b.ap[0:4, 0:n], t_m, g.free)
            b.free = [t_c]
            g.free = [l_sk[1 + i].start(SP, bass.AP(sk2, a, [[128 * 768, 4], [768, 128], [1, n]]),
                                   g.ap[0:4, 0:n].unsqueeze(1).to_broadcast([4, 128, n]), t_c)]

    q1 = big("q1", [128, 4, 1024], 0)
    kp1 = big("kp1", [128, 4, 1024], 16)
    v1 = big("v1", [128, 8, 128], 32)
    hp = big("hp", [128, 4, 1054], 36)
    acc = big("acc", [128, 4, 1024], 52.5)
    b1 = big("b1", [128, 8, 256], 68.5)
    s1 = [Place(big(f"s1_{i}", [128, 2, 256], 76.5 + 2 * i)) for i in range(3)]
    v1t = big("v1t", [128, 1024], 76.5)
    pt1 = [Place(big(f"pt1_{i}", [128, 4, 128], 82.5 + 2 * i)) for i in range(2)]
    o1s = [Place(t) for t in SGT]
    cwt = big("cwt", [128, 4, 34], 86.5)

    b = take_bank()
    for c in range(4):
        t_m = tr(b.ap[:, 34 * c:34 * c + 34], cw[0:34, 128 * c:128 * c + 128], t_misc, b.free, inc=(c == 3))
    t_cw = cp(cwt[:, :, :], b.ap[:, 0:136].rearrange("p (c w) -> p c w", c=4), t_m, x0[5].free)
    b.free = [t_cw]
    first = []
    t_hp0 = DV.put(lambda e: e.memset(hp[:, :, 0:30], 0.0))
    t_nsink = ts(nsink[:, :], sinks[:, :], -1.0, None, ALU.mult, None, t_misc)

    taps = []
    tap_last = {}

    def tap_steps(c, t_h):
        state = [None]

        def step(w):
            def go():
                src = hp[:, c, w:w + 1024]
                if w == 0:
                    state[0] = ts(acc[:, c, :], src, cwt[:, c, 0:1], cwt[:, c, 31:32], ALU.mult, ALU.add,
                                  t_h, t_cw, t_hp0, first)
                else:
                    state[0] = stt(acc[:, c, :], src, cwt[:, c, w:w + 1], acc[:, c, :], ALU.mult, ALU.add, state[0])
                tap_last[c] = state[0]
            return go

        more = [step(w) for w in range(TAPS)]
        mixed = []
        while taps or more:
            mixed += taps[0:1] + more[0:1]
            del taps[0:1], more[0:1]
        taps.extend(mixed)

    def some_taps(n):
        for _ in range(min(n, len(taps))):
            taps.pop(0)()

    prod = Ring([Place(big(f"prod{i}", [128, 512], 80.5 + 2 * i)) for i in range(3)])
    ptaps = []
    p_acc = [None, None]

    def pool_taps(t_h):
        def step(w, hf):
            def go():
                src, dst = hp[:, 0, w + 512 * hf:w + 512 * hf + 512], acc[:, 0, 512 * hf:512 * hf + 512]
                if w == 0:
                    p_acc[hf] = act(dst, src, ACT.Identity, t_h, t_cw, t_hp0, first, scale=cwt[:, 0, 0:1],
                                    bias=cwt[:, 0, 31:32])
                    return
                g = prod.take()
                t_p = act(g.ap[:, :], src, ACT.Copy, g.free, first, scale=cwt[:, 0, w:w + 1])
                p_acc[hf] = PL.put(lambda e: e.tensor_tensor(dst, dst, g.ap[:, :], ALU.add), t_p, p_acc[hf])
                g.free = [p_acc[hf]]
            return go
        ptaps.extend(step(w, hf) for w in range(TAPS) for hf in range(2))

    def spare():
        some_taps(4)
        for _ in range(min(3, len(ptaps))):
            ptaps.pop(0)()

    for c in range(4):
        sg = {}

        def gate(th, b, tok):
            g = SGR.take()
            sg[th] = (g, act(g.ap[:, :], b.ap, ACT.Sigmoid, tok, g.free))
            return [sg[th][1]]

        t_hc = []

        def glu(th, b, tok):
            g, t_g = sg[th]
            t = tt(hp[:, c, 30 + 512 * th:542 + 512 * th], b.ap, g.ap[:, :], ALU.mult, tok, t_g)
            g.free = [t]
            t_hc.append(t)
            return [t]

        feature_group([gate, glu], spare)
        if c == 0:
            bias_tables()
            t_skew = flatten([l.last() for l in l_sk])
            first += mark() + l_xr[0].last() + l_xr[1].last() + t_skew
            t_b1 = l_bias.start(SP, b1[:, :, :], bass.AP(sk1, 127, [[383, 128], [128 * 384, 8], [1, 256]]), first)
            pool_taps(t_hc)
        else:
            tap_steps(c, t_hc)

    t_kz = []
    for g in range(2):
        for s_ in range(2):
            z = 64 * (1 - s_)
            t_kz.append(DV.put(lambda e, i=2 * g + s_, z=z: e.memset(kp1[z:z + 64, i, :], 0.0), first))
    t_k1 = []

    def k_out(th, b, tok):
        cs = slice(512 * th, 512 * th + 512)
        t = []
        for g in range(2):
            for s_ in range(2):
                o, i = kp1[64 * s_:64 * s_ + 64, 2 * g + s_, cs], b.ap[64 * g:64 * g + 64, :]
                t.append(act(o, i, ACT.Copy, tok, first))
        t_k1.extend(t)
        return t

    feature_group([k_out], spare)
    t_vt = []

    def v_out(th, b, tok):
        t = act(v1t[:, 512 * th:512 * th + 512], b.ap, ACT.Copy, tok, first)
        t_vt.append(t)
        return [t]

    feature_group([v_out], spare)
    t_v1 = []

    def v_turn():
        for g in range(2):
            b = take_bank()
            for j in range(4):
                t = 4 * g + j
                t_m = tr(b.ap[:, 128 * j:128 * j + 128], v1t[:, 128 * t:128 * t + 128], t_vt, b.free, inc=(j == 3))
            t_c = act(v1[:, 4 * g:4 * g + 4, :], b.ap.rearrange("p (t d) -> p t d", t=4), ACT.Copy, t_m, first)
            b.free = [t_c]
            t_v1.append(t_c)
        s1[0].free, s1[1].free = [t_m], [t_m]

    t_q1 = {}

    def q_out(m):
        def go(th, b, tok):
            t = act(q1[:, m, 512 * th:512 * th + 512], b.ap, ACT.Copy, tok, first, scale=0.125)
            t_q1[m] = t
            return [t]
        return go

    for m in range(3):
        feature_group([q_out(m)], spare)
        if m == 0:
            v_turn()
    while ptaps:
        ptaps.pop(0)()
    pooled = p_acc + [g.free for g in prod.places]

    def attention(steps, scores, soft, turn, values):
        n = len(steps)
        for i in range(n + 3):
            if i < n:
                scores(i)
            if 2 <= i <= n + 1:
                turn(i - 2)
            if i >= 3:
                values(i - 3)
            if i < n:
                soft(i)
            if i in (3, 6, 9, 12):
                run_ahead()
            some_taps(1)
            for due, fn in list(later):
                if due <= i:
                    later.remove((due, fn))
                    fn()
        while later:
            later.pop(0)[1]()

    later = []
    sc_banks = banks[0:3]
    tr_banks = Ring(banks[3:5])
    o_banks = banks[5:7]
    for i in range(2):
        o1s[i].free = SGR.places[i].free
        pt1[i].free = pooled
    s1[2].free = pooled
    st = {}
    steps1 = [(n, g) for n in range(NT) for g in range(4)]

    def sc1(i):
        n, g = steps1[i]
        W = 128 if n == 0 else 256
        b = sc_banks[i % 3]
        for j in range(2):
            kv = g // 2
            t_m = mm(b.ap[:, 256 * j:256 * j + W], q1[:, g, 128 * n:128 * n + 128],
                     kp1[:, 2 * kv + j, 128 * (n + 1) - W:128 * (n + 1)], True, True,
                     t_q1[g], t_k1, t_kz, b.free, inc=(j == 1))
        st[i] = {"W": W, "sc": t_m}

    rows = {}

    def so1(i):
        n, g = steps1[i]
        d = st[i]
        W, b, s = d["W"], sc_banks[i % 3], s1[i % 3]
        if g == 0:
            rows[n] = {"rs": col(8), "es": col(8), "nm": col(8), "t": []}
        mx, nm = col(2), rows[n]["nm"][:, 2 * g:2 * g + 2]
        for j in range(2):
            h = 2 * g + j
            t_x = DV.put(lambda e, j=j, h=h: e.tensor_tensor_reduce(
                out=s.ap[:, j, 0:W], in0=b.ap[:, 256 * j:256 * j + W], in1=b1[:, h, 256 - W:256], scale=1.0,
                scalar=NEG, op0=ALU.add, op1=ALU.max, accum_out=mx[:, j:j + 1]), d["sc"], t_b1, s.free)
        b.free = [t_x]
        t_n = stt(nm, mx, -1.0, nsink[:, 2 * g:2 * g + 2], ALU.mult, ALU.min, t_x, t_nsink)
        for j in range(2):
            t_e = act(s.ap[:, j, 0:W], s.ap[:, j, 0:W], ACT.Exp, t_n, bias=nm[:, j:j + 1],
                      accum_out=rows[n]["rs"][:, 2 * g + j:2 * g + j + 1])
        d["p"] = t_e
        if g == 3:
            es = col(8)
            t_d = tt(es, rows[n]["nm"], sinks[:, :], ALU.add, t_n)
            rows[n]["t"].append(act(rows[n]["es"], es, ACT.Exp, t_d))

    def tu1(i):
        d = st[i]
        W, s, pt = d["W"], s1[i % 3], pt1[i % 2]
        nb = W // 128
        b = tr_banks.take()
        for j in range(2):
            for kb in range(nb):
                t_m = tr(b.ap[:, 128 * (nb * j + kb):128 * (nb * j + kb) + 128], s.ap[:, j, 128 * kb:128 * kb + 128],
                         d["p"], b.free, inc=(j == 1 and kb == nb - 1))
        s.free = [t_m]
        o, v = pt.ap[:, 0:2 * nb, :], b.ap[:, 0:256 * nb].rearrange("p (k c) -> p k c", c=128)
        t_c = cp(o, v, t_m, pt.free) if i % 2 == 0 and i > 12 else act(o, v, ACT.Copy, t_m, pt.free)
        b.free = [t_c]
        d["pt"] = t_c

    def va1(i):
        n, g = steps1[i]
        d = st[i]
        W, pt, ob = d["W"], pt1[i % 2], o_banks[n % 2]
        nb, kv = W // 128, g // 2
        for j in range(2):
            for kb in range(nb):
                h = 2 * g + j
                t_m = mm(ob.ap[:, 64 * h:64 * h + 64], pt.ap[:, nb * j + kb, :],
                         v1[:, n + 1 - nb + kb, 64 * kv:64 * kv + 64], kb == 0, kb == nb - 1,
                         d["pt"], t_v1, ob.free if g == 0 else None, inc=(j == 1 and kb == nb - 1))
        pt.free = [t_m]
        if g == 3:
            r = rows[n]
            den, rden, o1 = col(8), col(8), o1s[n % 2]
            t_d = tt(den, r["rs"], r["es"], ALU.add, r["t"], AC.last())
            t_r = DV.put(lambda e: e.reciprocal(rden, den), t_d)
            t_o = tt(o1.ap[:, :].rearrange("p (h d) -> p h d", h=8), ob.ap.rearrange("p (h d) -> p h d", h=8),
                     rden.unsqueeze(2).to_broadcast([128, 8, 64]), ALU.mult, t_r, t_m, o1.free)
            ob.free = [t_o]

            def turn_y():
                bank_turn[0] = 7
                col_ready[n] = []
                o1.free = [turn_in(o1.ap, 4, n, 0, t_o)]
            later.append((i + 6, turn_y))

    def last_q():
        bank_turn[0] = 5
        feature_group([q_out(3)], lambda: some_taps(4))

    later.append((0, last_q))

    yc1 = [Place(big(f"yc1_{i}", [128, 512], 36 + 2 * i)) for i in range(NT)]
    t_y = {}

    def conv_turn(tb):
        some_taps(len(taps))
        b, y = banks[7], yc1[tb].ap
        for c in range(4):
            t_m = tr(b.ap[:, 128 * c:128 * c + 128], acc[:, c, 128 * tb:128 * tb + 128], conv_done(), b.free, inc=(c == 3))
        t_c = act(y[:, :], b.ap, ACT.Copy, t_m, conv_done())
        b.free = [t_c]

        def stat():
            bs, mv = col(6), col(2)
            t_b = DV.put(lambda e: e.bn_stats(bs, y[:, :]), t_c)
            t_a = DV.put(lambda e: e.bn_aggr(mv, bs), t_b)
            r, t_r = inv_rms(mv[:, 1:2], epsc[:, 0:1], t_a)

            def norm():
                t_y[tb] = ts(y[:, :], y[:, :], mv[:, 0:1], r, ALU.subtract, ALU.mult, t_r)
            later.append((16 + 2 * tb, norm))
        later.append((14 + 2 * tb, stat))

    def conv_done():
        if "t" not in t_y:
            t_y["t"] = list(tap_last.values()) + flatten(p_acc)
        return t_y["t"]

    for tb in range(NT):
        later.append((13 + 2 * tb, lambda tb=tb: conv_turn(tb)))

    MH = sb("mh", [128, 8, 256], off["ah"] + 16 * KB, F32R)
    ML = sb("ml", [128, 8, 256], off["al"] + 16 * KB, F32R)
    mem_sq = sb("mem_sq", [128, 1024], off["ah"] + 16 * KB)
    memx = [sb(f"memx{i}", [128, 1024], off["ah"] + (24 + 4 * i) * KB) for i in range(2)]
    gmem = sb("gmem", [128, 1024], off["al"] + 24 * KB)
    xk_out = sb("xk_out", [128, 4, 256], off["al"] + 28 * KB)
    xv_out = sb("xv_out", [128, 2, 512], off["ah"] + 24 * KB)
    swa0, t_mem = [], []

    def mem_load():
        swa0.extend(mark())
        for i in range(2):
            l_mem.start(SP, memx[i][:, :], I["mem_2"][0][128 * i:128 * i + 128, :], swa0)
        t_mem.append(l_mem.start(SP, gmem[:, :], I["norm_mem_2"][0].partition_broadcast(128), swa0))

    later.append((1, mem_load))
    t_mn, t_mh, t_xkv, r_mem = {}, [], [], {}

    def mem_square(i):
        s = col()
        t_s = act(mem_sq[:, :], memx[i][:, :], ACT.Square, t_mem, swa0, r_mem[0][1] if i else None, scale=RT, accum_out=s)
        r_mem[i] = inv_rms(s, epsc[:, 0:1], t_s)

    def mem_norm(i):
        r, t_r = r_mem[i]
        t_mn[i] = stt(memx[i][:, :], memx[i][:, :], r, gmem[:, :], ALU.mult, ALU.mult, t_r)

    def mem_turn(i, g):
        b = banks[7]
        for j in range(4):
            kk = 4 * g + j
            t_m = tr(b.ap[:, 128 * j:128 * j + 128], memx[i][:, 128 * kk:128 * kk + 128], t_mn[i], b.free, inc=(j == 3))
        t_mh.extend(split_in(b, 4, MH[:, 4 * g:4 * g + 4, 128 * i:128 * i + 128],
                             ML[:, 4 * g:4 * g + 4, 128 * i:128 * i + 128], t_m, r_mem[1][1], swa0))

    def mem_key(m):
        k, b = next_chunk(), banks[7]
        for i in range(8):
            tok = mm3(b.ap[:, 0:256], k.hi[:, 128 * i:128 * i + 128], k.lo[:, 128 * i:128 * i + 128], MH[:, i, :],
                      ML[:, i, :], i == 0, i == 7, k.ready, b.free, t_mh, inc=(i == 7))
        t0 = act(xk_out[:, m, :], b.ap[:, 0:256], ACT.Copy, tok, swa0)
        b.free = [t0]
        t_xkv.append(t0)
        chunk_done(k, tok)

    vks = []

    def mem_value(t):
        if t == 0:
            vks.extend(next_chunk() for _ in range(4))
        b = banks[7]
        for i in range(8):
            k, ii = vks[i // 2], i % 2
            tok = mm3(b.ap, MH[:, i, 128 * t:128 * t + 128], ML[:, i, 128 * t:128 * t + 128],
                      k.hi[:, 512 * ii:512 * ii + 512], k.lo[:, 512 * ii:512 * ii + 512], i == 0, i == 7,
                      k.ready, b.free, t_mh, inc=(i == 7))
        t0 = act(xv_out[:, t, :], b.ap, ACT.Copy, tok, list(t_mn.values()))
        b.free = [t0]
        t_xkv.append(t0)
        if t == 1:
            chunks_done(vks, tok)
            l_kv.start(SP, kv_dram[0], xk_out[:, :, :].rearrange("p a b -> p (a b)"), t_xkv)
            l_kv.start(SP, kv_dram[1], xv_out[:, :, :].rearrange("p a b -> p (a b)"), t_xkv)

    for i in range(2):
        later.append((4 + i, lambda i=i: mem_square(i)))
        later.append((6 + i, lambda i=i: mem_norm(i)))
        for g in range(2):
            later.append((8 + 2 * i + g, lambda i=i, g=g: mem_turn(i, g)))
        later.append((28 + 2 * i, lambda i=i: mem_value(i)))
    for m in range(4):
        later.append((16 + 2 * m, lambda m=m: mem_key(m)))

    attention(steps1, sc1, so1, tu1, va1)
    bank_turn[0] = 0

    for i in range(2):
        SGR.places[i].free = o1s[i].free
    done1 = mark() + l_kv.last()
    ZH = big("zh", [128, 4, 1024], 0, F32R)
    ZL = big("zl", [128, 4, 1024], 16, F32R)
    t_z = {}

    def ln_back(th, t_y):
        for c in range(4):
            b, g = take_bank(), SGR.take()
            for j in range(4):
                t_m = tr(b.ap[:, 128 * j:128 * j + 128], yc1[4 * th + j].ap[:, 128 * c:128 * c + 128], t_y, b.free,
                         inc=(j == 3))
            t_s = act(g.ap[:, :], b.ap, ACT.Silu, t_m, g.free, bias=cwt[:, c, 33:34], scale=cwt[:, c, 32:33])
            b.free = [t_s]
            cs = slice(512 * th, 512 * th + 512)
            t_hi = act(ZH[:, c, cs], g.ap[:, :], ACT.Copy, t_s, done1)
            t_lo = tt(ZL[:, c, cs], g.ap[:, :], ZH[:, c, cs].bitcast(F32), ALU.subtract, t_hi)
            g.free = [t_lo]
            t_z[th, c] = [t_hi, t_lo]

    ln_back(0, [t_y[tb] for tb in range(4)])
    pws = [next_chunk() for _ in range(4)]
    for th in range(2):
        for m, k in enumerate(pws):
            v = lambda i: (k.hi[:, 128 * i:128 * i + 128], k.lo[:, 128 * i:128 * i + 128])
            b = take_bank()
            cs = slice(512 * th, 512 * th + 512)
            tok = feature_unit(k, v, 4, lambda i: (ZH[:, i, cs], ZL[:, i, cs]), th, b, [t_z[th, c] for c in range(4)])
            hi, lo = AH[:, 4 + m, cs], AL[:, 4 + m, cs]
            t_hi = act(hi, b.ap, ACT.Copy, tok, done1)
            t_lo = tt(lo, b.ap, hi.bitcast(F32), ALU.subtract, t_hi, done1)
            b.free = [t_lo]
            for t in range(4 * th, 4 * th + 4):
                col_ready[t] = col_ready[t] + [t_hi, t_lo]
            if th == 0 and m == 0:
                ln_back(1, [t_y[tb] for tb in range(4, 8)])
            if th == 1:
                chunk_done(k, tok)

    pas = Passage(I["x"], I["mix_post_g"], I["ffn_pre_g"], h1, after=mark())
    eight = [list(range(8))] * 2
    token_stage(eight, lambda j, p: p, lambda j, p, t: col_ready[t], pas)

    ff_big = big("ff", [128, NF, 1024], 0)

    def ffn(x, g_post, g_pre, h, final=False):
        nonlocal pas
        t_ff = {}
        held = {}
        first_in = mark() + l_h[0].last() + l_h[1].last()

        class Split:
            free = {}
            made = {}
            done = 0
            early = {}

            def __call__(self, j, p):
                at = p if j == 0 else 14 + p
                goal = min(at + 5, NF if j == 0 else NF + 14)
                while self.done < goal:
                    self.one(self.done)
                    self.done += 1
                    if self.done == NF:
                        later_pas.begin()

            def part(self, f, s, a, b, w):
                t_hi = act(AH[:, s, a:b], ff_big[:, f, a:b], ACT.Copy, t_ff[f], w)
                t_lo = tt(AL[:, s, a:b], ff_big[:, f, a:b], AH[:, s, a:b].bitcast(F32), ALU.subtract, t_hi, w)
                return [t_hi, t_lo]

            def begin(self):
                for f in range(2):
                    self.early[f] = self.part(f, f, 0, 512, col_free[0])

            def one(self, at):
                f, s = at % NF, at % 8
                if at in self.early:
                    self.made[at] = [self.early[at], self.part(f, s, 512, 1024, col_free[4])]
                else:
                    self.made[at] = [self.part(f, s, 0, 1024, self.free.get(s, col_free[0] + col_free[4]))] * 2

            def used(self, j, p, tok):
                at = p if j == 0 else 14 + p
                self.free[at % 8] = [tok]

        split = Split()

        def pair_of(m):
            sg = {}

            def gate(th, b, tok):
                g = SGR.take()
                sg[th] = (g, act(g.ap[:, :], b.ap, ACT.Silu, tok, g.free))
                if m == NF - 1 and th == 1:
                    split.begin()
                return [sg[th][1]]

            def up(th, b, tok):
                g, t_g = sg[th]
                if "mark" not in held and th:
                    held["mark"] = mark() + l_h[0].last() + l_h[1].last()
                w = held.get("mark", first_in)
                t = tt(ff_big[:, m, 512 * th:512 * th + 512], b.ap, g.ap[:, :], ALU.mult, tok, t_g, w)
                g.free = [t]
                t_ff.setdefault(m, []).append(t)
                return [t]
            return [gate, up]

        for m in range(NF):
            feature_group(pair_of(m))

        split(0, 0)

        def slot(j, p):
            return (p if j == 0 else 14 + p) % 8

        def col_tok(j, p, t):
            return split.made[p if j == 0 else 14 + p][t // 4]

        class Later:
            pas = None

            def begin(self):
                spent = flatten([split.made[a] for a in range(14, 22)])
                p = self.pas = Passage.__new__(Passage)
                p.x, p.h, p.final, p.g_post, p.after = x, h, final, g_post, spent
                p.t_gb = [None, None]
                if g_post is not None:
                    p.t_gb[0] = l_gb[0].start(SP, GB[0][:, :], g_post.partition_broadcast(128), spent)
                p.t_gb[1] = l_gb[1].start(SP, GB[1][:, :], g_pre.partition_broadcast(128), spent)
                for q in XR:
                    q.free = spent
                p.t_x, p.m0, p.ss0, p.r1, p.r2, p.t_h, p.t_xn = {}, {}, {}, {}, {}, {}, {}
                for t in range(2):
                    p.load(t)
                self.p = p

            def keep(self, t, b, tok, *waits):
                self.p.keep(t, b, tok, *waits)

            def a(self, t, b, tok):
                if t == 0:
                    spent = flatten([split.made[a] for a in range(14, 26)])
                    for q in HT + XN:
                        q.free = spent
                self.p.a(t, b, tok)

            def squares(self, t):
                self.p.squares(t)

            def b(self, t, b, tok):
                self.p.b(t, b, tok)

            def c(self, t):
                self.p.c(t)

            def d(self, t):
                self.p.d(t)

            @property
            def final(self):
                return final

        later_pas = Later()
        token_stage(down_order, slot, col_tok, later_pas, extra=split)

    ffn(h1, I["ffn_post_g"], I["norm_mix_2"][0], h2)

    cv = big("cv", [128, 8, 256], 0)
    fv = big("fv", [128, 8, 256], 8)
    cqs = big("cqs", [128, 4, 1024], 70.5, F32R)
    ck1 = big("ck1", [128, 4, 1024], 8, F32R)
    ck2 = big("ck2", [128, 4, 1024], 24, F32R)
    b2 = big("b2", [128, 4, 640], 40)
    s2 = [Place(big(f"s2_{i}", [128, 640], 50 + 2.5 * i)) for i in range(3)]
    pt2 = [Place(big(f"pt2_{i}", [128, 5, 128], 57.5 + 2.5 * i)) for i in range(2)]
    o2 = [Place(big("o2", [128, 256], 86.5))]
    yc = big("yc", [128, 8, 256], 62.5)
    gout = sb("gout", [128, 1024], off["sg"])
    fqp = big("fqp", [128, 4, 1024], 70.5)
    fkp = big("fkp", [128, 4, 1024], 16)
    CH = big("ch", [128, 3, 1024], 32, F32R)
    CL = big("cl", [128, 3, 1024], 44, F32R)
    kpe = big("kpe", [128, 1024], 4)

    in0 = mark()
    t_cq, t_ck, in1 = [], [], []

    def cq_out(m):
        def go(th, b, tok):
            t = []
            cs = slice(512 * th, 512 * th + 512)
            hi = [cqs[64 * s_:64 * s_ + 64, 2 * m + s_, cs] for s_ in range(2)]
            for s_ in range(2):
                t_hi = act(hi[s_], b.ap[64 * s_:64 * s_ + 64, :], ACT.Copy, tok, in0, scale=0.125)
            for s_ in range(2):
                t.append(stt(cqs[64 * (1 - s_):64 * (1 - s_) + 64, 2 * m + s_, cs], b.ap[64 * s_:64 * s_ + 64, :], 0.125,
                             hi[s_].bitcast(F32), ALU.mult, ALU.subtract, t_hi, in0))
            t_cq.extend([t_hi] + t)
            return t
        return go

    def ck_out(m):
        def go(th, b, tok):
            t = []
            cs = slice(512 * th, 512 * th + 512)
            for s_ in range(2):
                for o_ in range(2):
                    t_hi = act(ck1[64 * o_:64 * o_ + 64, 2 * m + s_, cs], b.ap[64 * s_:64 * s_ + 64, :], ACT.Copy, tok, in1)
            for s_ in range(2):
                for o_ in range(2):
                    t.append(tt(ck2[64 * o_:64 * o_ + 64, 2 * m + s_, cs], b.ap[64 * s_:64 * s_ + 64, :],
                                ck1[64 * s_:64 * s_ + 64, 2 * m + s_, cs].bitcast(F32), ALU.subtract, t_hi, in1))
            t_ck.extend([t_hi] + t)
            return t
        return go

    def pair_out(dst, m, toks, scale, waits):
        def go(th, b, tok):
            t = []
            for s_ in range(2):
                t.append(act(dst[64 * s_:64 * s_ + 64, 2 * m + s_, 512 * th:512 * th + 512],
                             b.ap[64 * s_:64 * s_ + 64, :], ACT.Copy, tok, waits, scale=scale))
            toks.extend(t)
            return t
        return go

    feature_group([cq_out(0), cq_out(1)])
    in1 += mark() + l_h[0].last() + l_h[1].last()
    feature_group([ck_out(0), ck_out(1)])
    t_gout = l_gb[0].start(SP, gout[:, :], I["out_norm_2"][0].partition_broadcast(128), in1)
    t_b2 = l_bias.start(SP, b2[:, :, :], bass.AP(sk2, 127, [[767, 128], [128 * 768, 4], [1, 640]]), in1, t_skew)
    t_b2m = [DV.put(lambda e: e.memset(b2[0:64, :, 576:640], NEG), t_b2),
             DV.put(lambda e: e.memset(b2[64:128, :, 0:64], NEG), t_b2)]

    def token_group(width, evac, per=2):
        ks = [next_chunk() for _ in range(8 // per)]
        for t in range(NT):
            b = take_bank()
            for p in range(8):
                k, ii = ks[p // per], p % per
                tok = mm3(b.ap[:, 0:width], AH[:, p, 128 * t:128 * t + 128], AL[:, p, 128 * t:128 * t + 128],
                          k.hi[:, width * ii:width * ii + width], k.lo[:, width * ii:width * ii + width], p == 0,
                          p == 7, k.ready, b.free, col_ready[t], inc=(p == 7))
            col_free[t] = [tok]
            b.free = flatten(evac(t, b, tok))
        chunks_done(ks, tok)
        return tok

    t_cv, t_fv = {}, {}

    def cv_out(t, b, tok):
        t_cv[t] = act(cv[:, t, :], b.ap[:, 0:256], ACT.Copy, tok, in1)
        return [t_cv[t]]

    def fv_out(t, b, tok):
        t_fv[t] = act(fv[:, t, :], b.ap[:, 0:256], ACT.Copy, tok, in3)
        return [t_fv[t]]

    token_group(256, cv_out, per=4)

    turn_banks = Ring([banks[4], banks[5]])

    def heads_attention(kind, q, k, v, nh, dv, width, p_ring, pt_ring, o_ring, finish, t_q, t_k, t_v, began):
        steps = [(i, h) for i in range(NT) for h in range(nh)]
        st, rows = {}, {}
        pairs = [(0, 1), (2, 3)]
        tb = turn_banks

        def sc(x):
            i, h = steps[x]
            a, b = width(i)
            W = b - a
            p = pairs[x % 2]
            size = W // 2 if kind == "chunk" and W > 512 else 512
            for w in range(0, W, size):
                n = min(size, W - w)
                bk = banks[p[w // size]]
                keys = k(h, a + w, a + w + n)
                for y, part in enumerate(keys):
                    t_m = mm(bk.ap[:, 0:n], q(h, i), part, y == 0, y == len(keys) - 1, t_q, t_k, banks[p[0]].free,
                             banks[p[1]].free, inc=(y == len(keys) - 1))
            ap = P[:, p[0]:p[0] + 2, 0:size] if size < 512 else PF[:, 512 * p[0]:512 * p[0] + W]
            st[x] = {"W": W, "t": t_m, "ap": ap}

        def so(x):
            i, h = steps[x]
            d, pr = st[x], p_ring[x % 3]
            W, ap, p = d["W"], d["ap"], pairs[x % 2]
            if h == 0:
                rows[i] = col(nh)
            nm = col()
            dst = pr.ap[:, 0:W]
            src = ap
            if kind == "chunk":
                mx = col()
                dst2, bias = dst, b2[:, h, 640 - W:640]
                if W > 512:
                    dst2, bias = (v_.rearrange("p (a n) -> p a n", a=2) for v_ in (dst, bias))
                t_x = DV.put(lambda e: e.tensor_tensor_reduce(out=dst2, in0=ap, in1=bias, scale=1.0,
                                                              scalar=NEG, op0=ALU.add, op1=ALU.max, accum_out=mx),
                             d["t"], t_b2m, pr.free)
                banks[p[0]].free = banks[p[1]].free = [t_x]
                t_n = ts(nm, mx, -1.0, None, ALU.mult, None, t_x)
                src = dst
            else:
                t_m = d["t"]
                if kind == "mla":
                    t_m = DV.put(lambda e: e.memset(ap[0:64, W - 64:W], NEG), d["t"])
                elif kind == "fox":
                    t_m = tt(ap[:, W - 128:W], ap[:, W - 128:W], causal[:, :], ALU.add, d["t"], t_causal)
                t_n = DV.put(lambda e: e.tensor_reduce(nm, ap, AX.X, ALU.max, negate=True), t_m)
            rs = rows[i][:, h:h + 1]
            d["p"] = act(dst, src, ACT.Exp, t_n, pr.free, bias=nm, accum_out=rs)
            if kind != "chunk":
                banks[p[0]].free = banks[p[1]].free = [d["p"]]

        def tu(x):
            d, pr, pt = st[x], p_ring[x % 3], pt_ring[x % 2]
            nb = d["W"] // 128
            made = []
            for g in range(0, nb, 4):
                w = min(4, nb - g)
                b = tb.take()
                for j in range(w):
                    t_m = tr(b.ap[:, 128 * j:128 * j + 128], pr.ap[:, 128 * (g + j):128 * (g + j) + 128], d["p"], b.free,
                             inc=(j == w - 1))
                o, v_ = pt.ap[:, g:g + w, :], b.ap[:, 0:128 * w].rearrange("p (k c) -> p k c", c=128)
                t_c = cp(o, v_, t_m, pt.free) if (x + g // 4) % 2 else act(o, v_, ACT.Copy, t_m, pt.free)
                b.free = [t_c]
                made.append(t_c)
            pr.free = [t_m]
            d["pt"] = made

        def va(x):
            i, h = steps[x]
            d, pt, ob = st[x], pt_ring[x % 2], banks[6 + i % 2]
            a, b = width(i)
            nb = d["W"] // 128
            for kb in range(nb):
                t_m = mm(ob.ap[:, dv * h:dv * h + dv], pt.ap[:, kb, :], v(h, a // 128 + kb), kb == 0, kb == nb - 1,
                         d["pt"], t_v, ob.free if h == 0 else None, inc=(kb == nb - 1))
            pt.free = [t_m]
            if h == nh - 1:
                rden = col(nh)
                o = o_ring[i % len(o_ring)]
                t_r = DV.put(lambda e: e.reciprocal(rden, rows[i]), [st[y]["p"] for y in range(x - nh + 1, x + 1)])
                t_o = tt(o.ap[:, :].rearrange("p (h d) -> p h d", h=nh),
                         ob.ap[:, 0:nh * dv].rearrange("p (h d) -> p h d", h=nh),
                         rden.unsqueeze(2).to_broadcast([128, nh, dv]), ALU.mult, t_r, t_m, o.free)
                ob.free = [t_o]
                finish(i, o, t_o, x)

        for r in (p_ring, pt_ring, o_ring):
            for pl in r:
                pl.free = list(began)
        attention(steps, sc, so, tu, va)

    def group_norm(o, n, junk, t_o, *waits):
        s = col()
        return inv_rms(s, epsc[:, 0:1], act(junk, o, ACT.Square, t_o, *waits, scale=n ** -0.5, accum_out=s))

    in2 = mark()
    t_yc = {}

    def chunk_finish(i, o, t_o, x):
        r, t_r = group_norm(o.ap[:, :], 256, yc[:, i, :], t_o, in2)

        def norm():
            t_yc[i] = stt(yc[:, i, :], o.ap[:, :], r, gout[:, 768:1024], ALU.mult, ALU.mult, t_r, t_gout)
            o.free = [t_yc[i]]
        later.append((x + 4, norm))

    heads_attention("chunk", lambda h, i: cqs[:, h, 128 * i:128 * i + 128],
                    lambda h, a, b: [ck1[:, h, a:b], ck2[:, h, a:b]],
                    lambda h, kb: cv[:, kb, 64 * h:64 * h + 64], 4, 64,
                    lambda i: (max(0, 128 * i - 512), 128 * i + 128), s2, pt2, o2, chunk_finish,
                    t_cq, t_ck, [t_cv[t] for t in range(NT)], in2)
    bank_turn[0] = 0

    in3 = mark()
    tt_ring = [Place(big(f"tt_{i}", [128, 512], 56 + 2 * i)) for i in range(2)]
    ropek = big("ropek", [128, 8, 64], 60)
    gq = big("gq", [128, 384], 86.5)
    fl = big("fl", [4, 1024], 0)
    l_mem.start(SP, ropek[:, :, :], I["c_ropek"], in3)
    l_mem.start(SP, gq[:, 0:256], I["q_norm_2"][0].partition_broadcast(128), in3)
    l_mem.start(SP, gq[:, 256:384], I["kv_norm_2"][0].partition_broadcast(128), in3)
    fbias = small("fbias", 1)
    l_mem.start(SP, fbias[0:4, :], I["f_bias_2"][0].rearrange("(n a) -> n a", a=1), in3)
    t_causal = t_fb = t_rk = l_mem.start(SP, causal[:, :], I["c_causal"], in3)
    t_ttz = [DV.put(lambda e, i=i: e.memset(tt_ring[i].ap[:, 384:512], 0.0), in3) for i in range(2)]
    t_narrow = {}
    lat = []

    def narrow_out(t, b, tok):
        T = tt_ring[t % 2]
        w = [T.free, in3, t_ttz]
        res = []
        sq = col(2)
        v = col(2)
        t_s = act(T.ap[:, 0:256], b.ap[:, 0:256], ACT.Square, tok, w, accum_out=sq[:, 0:1])
        t_s2 = act(T.ap[:, 256:384], b.ap[:, 256:384], ACT.Square, tok, w, accum_out=sq[:, 1:2])
        t_a = ts(v[:, 0:1], sq[:, 0:1], 1.0 / 256, EPS, ALU.mult, ALU.add, t_s)
        t_b = ts(v[:, 1:2], sq[:, 1:2], 1.0 / 128, EPS, ALU.mult, ALU.add, t_s2)
        r, t_r = inv_sqrt(v, t_a, t_b)
        x12 = b.ap[:, 384:416]
        ta = tt(ra[:, 0, :], x12, ropek[:, t, 0:32], ALU.mult, tok, t_s2, t_rk, in3, DV.last())
        tb1 = tt(ra[:, 1, 0:16], b.ap[:, 400:416], ropek[:, t, 32:48], ALU.mult, DV.last())
        tb2 = tt(ra[:, 1, 16:32], b.ap[:, 384:400], ropek[:, t, 48:64], ALU.mult, DV.last())
        tf = cp(T.ap[:, 384:388], b.ap[:, 416:420], w)
        t1 = tt(T.ap[:, 448:480], ra[:, 0, :], ra[:, 1, :], ALU.add, ta, tb1, tb2, w)
        t2 = stt(T.ap[:, 0:256], b.ap[:, 0:256], r[:, 0:1], gq[:, 0:256], ALU.mult, ALU.mult, t_r, t_rk)
        t3 = stt(T.ap[:, 256:384], b.ap[:, 256:384], r[:, 1:2], gq[:, 256:384], ALU.mult, ALU.mult)
        t_narrow[t] = [tf, t1, t2, t3]

        def turn():
            b2_ = take_bank()
            for j in range(4):
                t_m = tr(b2_.ap[:, 128 * j:128 * j + 128], T.ap[:, 128 * j:128 * j + 128], t_narrow[t], b2_.free,
                         inc=(j == 3))
            T.free = [t_m]
            cs = slice(128 * t, 128 * t + 128)
            vv = b2_.ap[:, 0:384].rearrange("p (k c) -> p k c", k=3)
            t_hi = act(CH[:, :, cs], vv, ACT.Copy, t_m, in3)
            t_k = act(kpe[64:96, cs], b2_.ap[64:96, 384:512], ACT.Copy, t_m, in3)
            t_f = act(fl[0:4, cs], b2_.ap[0:4, 384:512], ACT.Copy, t_m, in3)
            t_lo = tt(CL[:, :, cs], vv, CH[:, :, cs].bitcast(F32), ALU.subtract, t_hi, t_f, in3)
            b2_.free = [t_lo]
            lat.append((t_hi, t_lo, t_k, t_f))

        turns.append(turn)
        if len(turns) >= 2:
            turns.pop(0)()
        return [t3]

    turns = []
    tok = token_group(420, narrow_out)
    while turns:
        turns.pop(0)()

    t_fz = []
    for h in range(4):
        z = 64 * (1 - h % 2)
        for dst in (fqp, fkp):
            t0 = DV.put(lambda e, dst=dst, z=z, h=h: e.memset(dst[z:z + 64, h, :], 0.0), in3)
            t_fz.append(DV.put(lambda e, dst=dst, z=z, h=h: e.memset(dst[z:z + 2, h, :], 1.0), t0))
    in4 = mark()
    z1 = big("z1", [4, 1024], 56)
    t1 = ts(fl[:, :], fl[:, :], fbias[0:4, 0:1], None, ALU.add, None, in4, t_fb)
    t2 = stt(z1[:, :], fl[:, :], -1.0, fl[:, :], ALU.mult, ALU.max, t1, in4)
    t3 = act(z1[:, :], z1[:, :], ACT.Exp, t2, scale=-1.0)
    t4 = act(z1[:, :], z1[:, :], ACT.Ln, t3, bias=1.0)
    t5 = stt(fl[:, :], fl[:, :], 0.0, z1[:, :], ALU.min, ALU.subtract, t4)
    t6 = DV.put(lambda e: e.memset(z1[:, :], 1.0), t5)
    t7 = DV.put(lambda e: e.tensor_tensor_scan(z1[:, :], z1[:, :], fl[:, :], 0.0, ALU.mult, ALU.add), t6)
    t8 = ts(fl[:, :], z1[:, :], -1.0, None, ALU.mult, None, t7)
    for h in range(4):
        z = 64 * (1 - h % 2)
        l_aug.start(SP, fqp[z + 1:z + 2, h, :], z1[h:h + 1, :], t8, t_fz)
        t_aug = l_aug.start(SP, fkp[z:z + 1, h, :], fl[h:h + 1, :], t8, t_fz)
    t_fq, t_fk = [], []
    token_group(256, fv_out, per=4)
    feature_group([pair_out(fqp, m, t_fq, 0.125, in3) for m in range(2)])
    feature_group([pair_out(fkp, m, t_fk, 1.0, in3) for m in range(2)])
    bank_turn[0] = 0

    def turn_yc(t):
        col_ready[t] = []
        turn_in(yc[:, t, :], 2, t, 6, t_yc[t], ring=turn_banks)

    for t in range(NT):
        later.append((2 + 4 * t, lambda t=t: turn_yc(t)))

    p3 = [Place(sb(f"p3_{i}", [128, 1024], off["ah"] + 4 * KB * i)) for i in range(3)]
    pt3 = [Place(sb(f"pt3_{i}", [128, 8, 128], off["al"] + 4 * KB * i)) for i in range(2)]
    o3 = [Place(big(f"o3_{i}", [128, 256], 58 + i)) for i in range(2)]
    SQ = [Place(big(f"sq3_{i}", [128, 256], 56 + i)) for i in range(2)]
    in5 = mark() + [t_aug]
    for q_ in SQ:
        q_.free = list(in5)

    def fox_finish(i, o, t_o, x):
        sq = SQ[i % 2]
        r, t_r = group_norm(o.ap[:, :], 256, sq.ap[:, :], t_o, sq.free)
        sq.free = [t_r]

        def norm():
            t_y = stt(o.ap[:, :], o.ap[:, :], r, gout[:, 512:768], ALU.mult, ALU.mult, t_r, t_gout)

            def turn_y():
                o.free = [turn_in(o.ap, 2, i, 4, t_y, ring=Ring([banks[6 + i % 2]]))]
            later.append((x + 5, turn_y))
        later.append((x + 4, norm))

    heads_attention("fox", lambda h, i: fqp[:, h, 128 * i:128 * i + 128], lambda h, a, b: [fkp[:, h, a:b]],
                    lambda h, kb: fv[:, kb, 64 * h:64 * h + 64], 4, 64, lambda i: (0, 128 * i + 128),
                    p3, pt3, o3, fox_finish, [t_fq, t_fz, t_aug], [t_fk, t_fz, t_aug], [t_fv[t] for t in range(NT)], in5)
    bank_turn[0] = 0
    for t in range(NT):
        col_free[t] = mark()

    in6 = mark()
    mq = big("mq", [128, 4, 1024], 56)
    mk = big("mk", [128, 4, 1024], 72)
    mv_ = big("mv", [128, 8, 512], 8)
    ropeq = big("ropeq", [128, 1024], 0)
    rtmp = [Place(big(f"rtmp{i}", [128, 512], 24 + 2 * i)) for i in range(2)]
    t_rq = l_mem.start(SP, ropeq[64:128, :], I["c_ropeq"], in6)
    lat_t = flatten([list(x) for x in lat])
    MS = 96 ** -0.5
    t_mz = [DV.put(lambda e: e.memset(mk[96:128, :, :], 0.0), in6), DV.put(lambda e: e.memset(mq[96:128, :, :], 0.0), in6)]
    t_mq, t_mk, t_mv = [], [], []
    k = next_chunk()
    for h in range(4):
        for th in range(2):
            b = take_bank()
            cs = slice(512 * th, 512 * th + 512)
            tok = feature_unit(k, lambda i: (k.hi[:, 512 * i + 128 * h:512 * i + 128 * h + 128],
                                             k.lo[:, 512 * i + 128 * h:512 * i + 128 * h + 128]), 2,
                               lambda i: (CH[:, i, cs], CL[:, i, cs]), th, b, lat_t)
            t0 = act(mq[0:64, h, cs], b.ap[0:64, :], ACT.Copy, tok, in6, scale=MS)
            t1 = stt(mq[64:96, h, cs], b.ap[64:96, :], MS, ropeq[64:96, cs], ALU.mult, ALU.mult, tok, t0, t_rq, in6)
            g = rtmp[th]
            t2 = stt(g.ap[64:96, :], b.ap[96:128, :], MS, ropeq[96:128, cs], ALU.mult, ALU.mult, t1, g.free, in6)
            t3 = PL.put(lambda e, o=mq[64:96, h, cs], r=g.ap[64:96, :]: e.tensor_tensor(o, o, r, ALU.add), t1, t2, PL.last())
            g.free = narrow_pool[:] = [t3]
            b.free = [t2]
            t_mq += [t0, t3]
    chunk_done(k, tok)
    k = next_chunk()
    for h in range(4):
        for th in range(2):
            b = take_bank()
            cs = slice(512 * th, 512 * th + 512)
            tok = feature_unit(k, lambda i: (k.hi[:, 192 * h:192 * h + 128], k.lo[:, 192 * h:192 * h + 128]), 1,
                               lambda i: (CH[:, 2, cs], CL[:, 2, cs]), th, b, lat_t)
            t0 = act(mk[0:64, h, cs], b.ap[0:64, :], ACT.Copy, tok, in6)
            b.free = [t0]
            t_mk.append(t0)
    for h in range(4):
        t_mz.append(cp(mk[64:96, h, :], kpe[64:96, :], lat_t, in6))
    vh = k.hi[:, 0:768].rearrange("p (h c) -> p h c", h=4)[:, :, 64:192]
    vl = k.lo[:, 0:768].rearrange("p (h c) -> p h c", h=4)[:, :, 64:192]
    for t in range(NT):
        b = take_bank()
        cs = slice(128 * t, 128 * t + 128)
        tok = mm3(b.ap.rearrange("p (h c) -> p h c", h=4), CH[:, 2, cs], CL[:, 2, cs], vh, vl, True, True, b.free,
                  k.ready, lat_t, inc=True)
        t0 = act(mv_[:, t, :], b.ap, ACT.Copy, tok, in6)
        b.free = [t0]
        t_mv.append(t0)
    chunk_done(k, tok)

    in7 = mark()
    p4 = [Place(big(f"p4_{i}", [128, 1024], 24 + 4 * i)) for i in range(3)]
    pt4 = [Place(big(f"pt4_{i}", [128, 8, 128], 36 + 4 * i)) for i in range(2)]
    o4 = [Place(big(f"o4_{i}", [128, 512], 44 + 2 * i)) for i in range(2)]
    SQ4 = [Place(big(f"sq4_{i}", [128, 512], 48 + 2 * i)) for i in range(2)]
    for q_ in SQ4:
        q_.free = list(in7)

    def mla_finish(i, o, t_o, x):
        sq = SQ4[i % 2]
        r, t_r = group_norm(o.ap[:, :], 512, sq.ap[:, :], t_o, sq.free)
        sq.free = [t_r]

        def norm():
            t_y = stt(o.ap[:, :], o.ap[:, :], r, gout[:, 0:512], ALU.mult, ALU.mult, t_r, t_gout)

            def turn_y():
                o.free = [turn_in(o.ap, 4, i, 0, t_y, ring=Ring([banks[6 + i % 2]]))]
            later.append((x + 5, turn_y))
        later.append((x + 4, norm))

    heads_attention("mla", lambda h, i: mq[:, h, 128 * i:128 * i + 128], lambda h, a, b: [mk[:, h, a:b]],
                    lambda h, kb: mv_[:, kb, 128 * h:128 * h + 128], 4, 128, lambda i: (0, 128 * i + 128),
                    p4, pt4, o4, mla_finish, [t_mq, t_mz], [t_mk, t_mz], t_mv, in7)
    bank_turn[0] = 0

    stored = lambda: l_h[0].last() + l_h[1].last()

    pas = Passage(h2, None, I["norm_cross_2"][0], h3, after=mark() + stored())
    token_stage(eight, lambda j, p: p, lambda j, p, t: col_ready[t], pas)

    xq = big("xq", [128, 4, 1024], 16)
    xk = big("xk", [128, 4, 256], 48)
    xv = big("xv", [128, 2, 512], 52)
    in8 = mark()
    t_xq = []

    def xq_out(m):
        def go(th, b, tok):
            t_xq.append(act(xq[:, m, 512 * th:512 * th + 512], b.ap, ACT.Copy, tok, in8, scale=128 ** -0.5))
            return [t_xq[-1]]
        return go

    l_mem.start(SP, xk[:, :, :].rearrange("p a b -> p (a b)"), kv_dram[0], in8, l_kv.last())
    t_xk = t_xv = l_mem.start(SP, xv[:, :, :].rearrange("p a b -> p (a b)"), kv_dram[1], in8, l_kv.last())
    feature_group([xq_out(0), xq_out(1)])
    feature_group([xq_out(2), xq_out(3)])

    in10 = mark() + stored()
    p5 = [Place(big(f"p5_{i}", [128, 256], i)) for i in range(3)]
    pt5 = [Place(big(f"pt5_{i}", [128, 2, 128], 3 + i)) for i in range(2)]
    o5 = [Place(big(f"o5_{i}", [128, 512], 6 + 2 * i)) for i in range(2)]

    def cross_finish(i, o, t_o, x):
        def turn_y():
            col_ready[i] = []
            o.free = [turn_in(o.ap, 4, i, 0, t_o, ring=Ring([banks[6 + i % 2]]))]
        later.append((x + 4, turn_y))

    heads_attention("cross", lambda h, i: xq[:, h, 128 * i:128 * i + 128], lambda h, a, b: [xk[:, h, a:b]],
                    lambda h, kb: xv[:, kb, 128 * h:128 * h + 128], 4, 128, lambda i: (0, 256),
                    p5, pt5, o5, cross_finish, t_xq, t_xk, t_xv, in10)
    bank_turn[0] = 0

    pas = Passage(h3, None, I["norm_ffn_2"][0], h4, after=mark() + stored())
    token_stage([list(range(4))] * 2, lambda j, p: p, lambda j, p, t: col_ready[t], pas)
    ffn(h4, None, I["final_norm_2"], None, final=True)

    for l in l_out + l_h + l_sk:
        for token in l.last():
            SP.items.append(([token], None, False))

    block = ctx.enter_context(nc.Block())

    @block.tensor
    def _(e):
        PE.run(e)

    @block.scalar
    def _(e):
        AC.run(e)

    @block.vector
    def _(e):
        DV.run(e)

    @block.gpsimd
    def _(e):
        PL.run(e)

    @block.sync
    def _(e):
        for need, fn, inc in SP.items:
            for s_, value in need:
                e.wait_ge(s_, value)
            if fn is not None:
                fn(e)

_INS = ["x", "mix_pre_g", "mix_post_g", "ffn_pre_g", "ffn_post_g", "w_in", "conv_dw", "conv_dw_b", "conv_ln_g",
        "conv_ln_b", "w_conv_pw", "attn_sinks", "rel_bias", "w_out", "w_gate", "w_up", "w_down", "mem_2",
        "norm_mix_2", "w_in_2", "q_norm_2", "w_uq_2", "kv_norm_2", "w_ukv_2", "f_bias_2", "rel_bias_2", "out_norm_2",
        "w_o_2", "norm_cross_2", "norm_mem_2", "w_cq_2", "w_ckv_2", "w_co_2", "norm_ffn_2", "w_gu_2", "w_down_2",
        "final_norm_2"]

def kernel(**inputs):
    import numpy as _np
    import concourse.bacc as _bacc
    from concourse import mybir as _mybir
    from concourse.bass_utils import run_bass_kernel_spmd as _run

    nc = _bacc.Bacc("TRN2", target_bir_lowering=False, num_devices=1)
    arrays, args = {}, {}
    given = {name: _np.ascontiguousarray(inputs[name]) for name in _INS}
    given["x"] = given["x"].reshape(1024, 1024)
    given.update(constants())
    for name, a in given.items():
        arrays[f"in_{name}_dram"] = a
        args[name] = nc.dram_tensor(f"in_{name}_dram", a.shape, _mybir.dt.from_np(a.dtype), kind="ExternalInput").ap()
    out = nc.dram_tensor("out_0_dram", (1024, 1024), _mybir.dt.float32, kind="ExternalOutput").ap()
    block_kernel(nc, args, out)
    r = _run(nc, [arrays], core_ids=[0])
    return r.results[0]["out_0_dram"].reshape(1, 1024, 1024)
```
